# Optimizing a Trainium2 kernel written in Bass

```python
import math
import jax
import jax.numpy as jnp
from jax import lax
import numpy as np

D_MODEL = 1024
BATCH = 1
SEQ = 256
DEPTH = 2

CTX_LEN = 256
GRID_W = 64
N_MIXERS = 3
ROPE_THETA = 10000.0
EPS = 1e-6
Q_BLOCK = 128
F32 = jnp.float32

GDN_HEADS = 8
GDN_DK = D_MODEL // GDN_HEADS
GDN_DV = D_MODEL // GDN_HEADS
GDN_CONV = 5
GDN_CHUNK = 64

DIFF_HEADS = 8
DIFF_HEAD_DIM = D_MODEL // DIFF_HEADS // 2
DIFF_SUBLN_EPS = 1e-5

MLA_HEADS = 8
MLA_Q_LORA = (3 * D_MODEL) // 4
MLA_KV_LORA = D_MODEL // 4
MLA_NOPE = 128
MLA_ROPE = 64
MLA_V = 128
MLA_SCALE = (MLA_NOPE + MLA_ROPE) ** -0.5

MOE_GROUPS = 4
MOE_EXPERTS_PER_GROUP = 8
MOE_EXPERTS = MOE_GROUPS * MOE_EXPERTS_PER_GROUP
MOE_TOP_K = 2
MOE_D_FF = D_MODEL // 2
MOE_BLOCK = 128

kernel_name = 'hybrid_gdn_diffattn_mla_hmoe_dit'

def rmsnorm(x, gain, eps=EPS):
    xf = x.astype(F32)
    y = xf * lax.rsqrt(jnp.mean(xf * xf, axis=-1, keepdims=True) + eps)
    return (y * gain.astype(F32)).astype(x.dtype)

def l2norm(x):
    return x * lax.rsqrt(jnp.sum(x * x, axis=-1, keepdims=True) + EPS)

def axial_rope_tables(rows, rot_dim):
    quarter = rot_dim // 4
    inv_freq = ROPE_THETA ** (-jnp.arange(quarter, dtype=F32) / quarter)
    t = jnp.arange(rows * GRID_W)
    row = (t // GRID_W).astype(F32)
    col = (t % GRID_W).astype(F32)
    ang = jnp.stack([row[:, None] * inv_freq, col[:, None] * inv_freq], axis=1)
    return jnp.cos(ang), jnp.sin(ang)

def apply_axial_rope(x, cos, sin):
    shp = x.shape
    xr = x.reshape(shp[:-1] + (2, 2, shp[-1] // 4))
    x1, x2 = xr[..., 0, :], xr[..., 1, :]
    cos = cos.astype(x.dtype)
    sin = sin.astype(x.dtype)
    return jnp.stack([x1 * cos - x2 * sin, x2 * cos + x1 * sin], axis=-2).reshape(shp)

def to_query_blocks(q):
    b, h, s, d = q.shape
    return q.reshape(b, h, s // Q_BLOCK, Q_BLOCK, d).transpose(2, 0, 1, 3, 4)

def from_query_blocks(o):
    nb, b, h, qb, d = o.shape
    return o.transpose(1, 2, 0, 3, 4).reshape(b, h, nb * qb, d)

def centred_depthwise_conv(x, w):
    k, ch = w.shape
    return lax.conv_general_dilated(x, w.astype(x.dtype)[:, None, :], window_strides=(1,),
                                    padding=[(k // 2, k // 2)],
                                    dimension_numbers=('NWC', 'WIO', 'NWC'),
                                    feature_group_count=ch)

def chunk_gated_delta(q, k, v, g, beta, s0):
    b, h, length, dk = k.shape
    dv = v.shape[-1]
    c = GDN_CHUNK
    n = length // c
    chunk = lambda t: t.reshape(b, h, n, c, t.shape[-1])
    q, k, v = chunk(q), chunk(k), chunk(v)
    gc = jnp.cumsum(g.reshape(b, h, n, c), axis=-1)
    beta = beta.reshape(b, h, n, c, 1)
    incl = jnp.tril(jnp.ones((c, c), dtype=bool))
    strict = jnp.tril(jnp.ones((c, c), dtype=bool), -1)
    decay = jnp.exp(jnp.where(incl, gc[..., :, None] - gc[..., None, :], -jnp.inf))
    kb = k * beta
    lower = jnp.where(strict, jnp.einsum('bhnid,bhnjd->bhnij', kb, k) * decay, 0.0)
    tmat = lower + jnp.eye(c, dtype=F32)
    u = lax.linalg.triangular_solve(tmat, v * beta, left_side=True, lower=True)
    w = lax.linalg.triangular_solve(tmat, kb * jnp.exp(gc)[..., None], left_side=True, lower=True)
    intra = jnp.einsum('bhnid,bhnjd->bhnij', q, k) * decay

    def step(state, xs):
        q_i, k_i, u_i, w_i, a_i, g_i = xs
        v_new = u_i - w_i @ state
        o_i = (q_i * jnp.exp(g_i)[..., None]) @ state + a_i @ v_new
        g_last = g_i[..., -1:]
        state = state * jnp.exp(g_last)[..., None] + jnp.einsum(
            'bhck,bhcv->bhkv', k_i * jnp.exp(g_last - g_i)[..., None], v_new)
        return state, o_i

    xs = tuple(jnp.moveaxis(t, 2, 0) for t in (q, k, u, w, intra, gc))
    s_fin, o = lax.scan(step, s0, xs)
    return jnp.moveaxis(o, 0, 2).reshape(b, h, length, dv), s_fin

def gdn_mixer(h_ctx, h_lat, w_in, conv_w, a_log, dt_bias, o_gain, w_out):
    wk = GDN_HEADS * GDN_DK
    wv = GDN_HEADS * GDN_DV

    def project(h):
        bsz, length, _ = h.shape
        p = h @ w_in
        qkv = jax.nn.silu(centred_depthwise_conv(p[..., :2 * wk + wv], conv_w))
        z = p[..., 2 * wk + wv:2 * wk + 2 * wv]
        ab = p[..., 2 * wk + 2 * wv:].astype(F32).reshape(bsz, length, 2, 2, GDN_HEADS)
        heads = lambda t: t.reshape(bsz, length, GDN_HEADS, -1).transpose(0, 2, 1, 3).astype(F32)
        q = l2norm(heads(qkv[..., :wk])) * GDN_DK ** -0.5
        k = l2norm(heads(qkv[..., wk:2 * wk]))
        v = heads(qkv[..., 2 * wk:])
        g = -jnp.exp(a_log.astype(F32)) * jax.nn.softplus(ab[:, :, :, 0] + dt_bias.astype(F32))
        beta = jax.nn.sigmoid(ab[:, :, :, 1])
        return q, k, v, z, g.transpose(0, 2, 3, 1), beta.transpose(0, 2, 3, 1)

    qc, kc, vc, zc, gc, bc = project(h_ctx)
    ql, kl, vl, zl, gl, bl = project(h_lat)
    s0 = jnp.zeros(qc.shape[:2] + (GDN_DK, GDN_DV), F32)
    flip = lambda t: jnp.flip(t, axis=2)
    oc_f, sc_f = chunk_gated_delta(qc, kc, vc, gc[:, 0], bc[:, 0], s0)
    ol_f, _ = chunk_gated_delta(ql, kl, vl, gl[:, 0], bl[:, 0], sc_f)
    oc_b, sc_b = chunk_gated_delta(flip(qc), flip(kc), flip(vc), flip(gc[:, 1]), flip(bc[:, 1]), s0)
    ol_b, _ = chunk_gated_delta(flip(ql), flip(kl), flip(vl), flip(gl[:, 1]), flip(bl[:, 1]), sc_b)

    def finish(o, z):
        bsz, _, length, _ = o.shape
        o = rmsnorm(o, o_gain).transpose(0, 2, 1, 3).reshape(bsz, length, wv)
        return (o.astype(z.dtype) * jax.nn.silu(z)) @ w_out

    return finish(oc_f + flip(oc_b), zc), finish(ol_f + flip(ol_b), zl)

def diff_core(q, k, v, lam):
    b, h2, lq, dh = q.shape
    s = jnp.einsum('bhqd,bhkd->bhqk', q, k).astype(F32) * dh ** -0.5
    p = jax.nn.softmax(s, axis=-1).reshape(b, h2 // 2, 2, lq, -1)
    a = (p[:, :, 0] - lam * p[:, :, 1]).astype(v.dtype)
    return jnp.einsum('bhqk,bhkd->bhqd', a, v)

def diff_mixer(h_ctx, h_lat, cos, sin, w_qkv, lam_vec, sub_gain, w_out, lam_init):
    def project(h):
        bsz, length, _ = h.shape
        q, k, v = jnp.split(h @ w_qkv, 3, axis=-1)
        q = q.reshape(bsz, length, 2 * DIFF_HEADS, DIFF_HEAD_DIM).transpose(0, 2, 1, 3)
        k = k.reshape(bsz, length, 2 * DIFF_HEADS, DIFF_HEAD_DIM).transpose(0, 2, 1, 3)
        v = v.reshape(bsz, length, DIFF_HEADS, 2 * DIFF_HEAD_DIM).transpose(0, 2, 1, 3)
        return q, k, v

    qc, kc, vc = project(h_ctx)
    ql, kl, vl = project(h_lat)
    ql = apply_axial_rope(ql, cos, sin)
    kl = apply_axial_rope(kl, cos, sin)
    lv = lam_vec.astype(F32)
    lam = jnp.exp(jnp.sum(lv[0] * lv[1])) - jnp.exp(jnp.sum(lv[2] * lv[3])) + lam_init
    o_ctx = diff_core(qc, kc, vc, lam)
    k_all = jnp.concatenate([kc, kl], axis=2)
    v_all = jnp.concatenate([vc, vl], axis=2)
    o_lat = from_query_blocks(lax.map(lambda qb: diff_core(qb, k_all, v_all, lam), to_query_blocks(ql)))

    def finish(o):
        bsz, _, length, _ = o.shape
        o = rmsnorm(o, sub_gain, DIFF_SUBLN_EPS) * (1.0 - lam_init)
        return o.transpose(0, 2, 1, 3).reshape(bsz, length, -1) @ w_out

    return finish(o_ctx), finish(o_lat)

def mla_core(qn, qr, kn, kr, v):
    s = (jnp.einsum('bhqd,bhkd->bhqk', qn, kn) + jnp.einsum('bhqr,bkr->bhqk', qr, kr)).astype(F32) * MLA_SCALE
    p = jax.nn.softmax(s, axis=-1).astype(v.dtype)
    return jnp.einsum('bhqk,bhkd->bhqd', p, v)

def mla_mixer(h_ctx, h_lat, cos, sin, w_down, q_gain, kv_gain, w_uq, w_ukv, w_out):
    def project(h, rotate):
        bsz, length, _ = h.shape
        p = h @ w_down
        cq = rmsnorm(p[..., :MLA_Q_LORA], q_gain)
        ckv = rmsnorm(p[..., MLA_Q_LORA:MLA_Q_LORA + MLA_KV_LORA], kv_gain)
        k_rope = p[..., MLA_Q_LORA + MLA_KV_LORA:]
        q = (cq @ w_uq).reshape(bsz, length, MLA_HEADS, MLA_NOPE + MLA_ROPE).transpose(0, 2, 1, 3)
        kv = (ckv @ w_ukv).reshape(bsz, length, MLA_HEADS, MLA_NOPE + MLA_V).transpose(0, 2, 1, 3)
        q_nope, q_rope = q[..., :MLA_NOPE], q[..., MLA_NOPE:]
        k_nope, v = kv[..., :MLA_NOPE], kv[..., MLA_NOPE:]
        if rotate:
            q_rope = apply_axial_rope(q_rope, cos, sin)
            k_rope = apply_axial_rope(k_rope, cos, sin)
        return q_nope, q_rope, k_nope, k_rope, v

    qnc, qrc, knc, krc, vc = project(h_ctx, False)
    qnl, qrl, knl, krl, vl = project(h_lat, True)
    o_ctx = mla_core(qnc, qrc, knc, krc, vc)
    kn_all = jnp.concatenate([knc, knl], axis=2)
    kr_all = jnp.concatenate([krc, krl], axis=1)
    v_all = jnp.concatenate([vc, vl], axis=2)
    o_lat = from_query_blocks(lax.map(lambda qs: mla_core(qs[0], qs[1], kn_all, kr_all, v_all),
                                      (to_query_blocks(qnl), to_query_blocks(qrl))))

    def finish(o):
        bsz, _, length, _ = o.shape
        return o.transpose(0, 2, 1, 3).reshape(bsz, length, -1) @ w_out

    return finish(o_ctx), finish(o_lat)

def grouped_expert_mlp(h, expert_id, gate, w1, w3, w2):
    t, d = h.shape
    kk = expert_id.shape[1]
    e = w1.shape[0]
    a = t * kk
    flat_e = expert_id.reshape(a)
    order = jnp.argsort(flat_e)
    e_sorted = flat_e[order]
    tok_sorted = (order // kk).astype(jnp.int32)
    counts = jnp.bincount(flat_e, length=e)
    padded = (counts + MOE_BLOCK - 1) // MOE_BLOCK * MOE_BLOCK
    pad_end = jnp.cumsum(padded)
    pad_start = pad_end - padded
    start = jnp.cumsum(counts) - counts
    dest = pad_start[e_sorted] + jnp.arange(a) - start[e_sorted]
    n_blocks = -(-(a + e * (MOE_BLOCK - 1)) // MOE_BLOCK)
    slot_tok = jnp.full((n_blocks * MOE_BLOCK,), t, jnp.int32).at[dest].set(tok_sorted)
    h_pad = jnp.concatenate([h, jnp.zeros((1, d), h.dtype)], axis=0)
    xb = h_pad[slot_tok].reshape(n_blocks, MOE_BLOCK, d)
    blk_expert = jnp.minimum(jnp.searchsorted(pad_end, jnp.arange(n_blocks) * MOE_BLOCK, side='right'), e - 1)

    def expert_block(args):
        xi, ei = args
        return (jax.nn.silu(xi @ w1[ei]) * (xi @ w3[ei])) @ w2[ei]

    yb = lax.map(expert_block, (xb, blk_expert)).reshape(-1, d)
    y = yb[dest].astype(F32) * gate.reshape(a)[order][:, None]
    out = jnp.zeros((t, d), F32).at[tok_sorted].add(y)
    return out.astype(h.dtype)

def hier_moe(h, w_group, b_group, w_expert, b_expert, w1, w3, w2):
    t, _ = h.shape
    hf = h.astype(F32)
    g_logits = hf @ w_group.astype(F32) + b_group.astype(F32)
    g_prob = jax.nn.softmax(g_logits, axis=-1)
    g_sel = jnp.argmax(g_logits, axis=-1)
    p_group = jnp.take_along_axis(g_prob, g_sel[:, None], axis=-1)
    e_logits = (hf @ w_expert.astype(F32) + b_expert.astype(F32)).reshape(t, MOE_GROUPS, MOE_EXPERTS_PER_GROUP)
    e_in = jnp.take_along_axis(e_logits, g_sel[:, None, None], axis=1)[:, 0]
    top_v, top_i = lax.top_k(e_in, MOE_TOP_K)
    gate = p_group * jax.nn.softmax(top_v, axis=-1)
    expert_id = g_sel[:, None].astype(jnp.int32) * MOE_EXPERTS_PER_GROUP + top_i.astype(jnp.int32)
    return grouped_expert_mlp(h, expert_id, gate, w1, w3, w2)

def setup_inputs(seed: int = 0) -> dict:
    key = jax.random.key(seed)
    keys = iter(jax.random.split(key, 48))

    def normal(shape, scale):
        return jax.random.normal(next(keys), shape, F32) * scale

    def gain(shape):
        return 1.0 + normal(shape, 0.01)

    d = D_MODEL
    n_a = len(range(0, DEPTH, N_MIXERS))
    n_b = len(range(1, DEPTH, N_MIXERS))
    n_c = len(range(2, DEPTH, N_MIXERS))
    wk = GDN_HEADS * GDN_DK
    wv = GDN_HEADS * GDN_DV
    gdn_cols = 2 * wk + 2 * wv + 4 * GDN_HEADS
    a_log = jnp.log(jax.random.uniform(next(keys), (n_a, 2, GDN_HEADS), F32, minval=1.0, maxval=16.0))
    dt = jnp.exp(jax.random.uniform(next(keys), (n_a, 2, GDN_HEADS), F32,
                                    minval=math.log(1e-3), maxval=math.log(1e-1)))
    dt_bias = dt + jnp.log(-jnp.expm1(-dt))
    return {
        'x': normal((BATCH, SEQ, d), 1.0),
        'c': normal((BATCH, d), 1.0),
        'ctx': normal((BATCH, CTX_LEN, d), 1.0),
        'c_ctx': normal((d,), 1.0),
        'w_mod': normal((DEPTH, d, 6 * d), 0.5 * d ** -0.5),
        'b_mod': normal((DEPTH, 6 * d), 0.02),
        'norm_mix': gain((DEPTH, d)),
        'norm_ffn': gain((DEPTH, d)),
        'gdn_w_in': normal((n_a, d, gdn_cols), d ** -0.5),
        'gdn_conv': normal((n_a, GDN_CONV, 2 * wk + wv), GDN_CONV ** -0.5),
        'gdn_a_log': a_log,
        'gdn_dt_bias': dt_bias,
        'gdn_norm': gain((n_a, GDN_DV)),
        'gdn_w_out': normal((n_a, wv, d), wv ** -0.5),
        'diff_w_qkv': normal((n_b, d, 3 * d), d ** -0.5),
        'diff_lambda': normal((n_b, 4, DIFF_HEAD_DIM), 0.1),
        'diff_norm': gain((n_b, 2 * DIFF_HEAD_DIM)),
        'diff_w_out': normal((n_b, d, d), d ** -0.5),
        'mla_w_down': normal((n_c, d, MLA_Q_LORA + MLA_KV_LORA + MLA_ROPE), d ** -0.5),
        'mla_q_norm': gain((n_c, MLA_Q_LORA)),
        'mla_kv_norm': gain((n_c, MLA_KV_LORA)),
        'mla_w_uq': normal((n_c, MLA_Q_LORA, MLA_HEADS * (MLA_NOPE + MLA_ROPE)), MLA_Q_LORA ** -0.5),
        'mla_w_ukv': normal((n_c, MLA_KV_LORA, MLA_HEADS * (MLA_NOPE + MLA_V)), MLA_KV_LORA ** -0.5),
        'mla_w_out': normal((n_c, MLA_HEADS * MLA_V, d), (MLA_HEADS * MLA_V) ** -0.5),
        'moe_w_group': normal((DEPTH, d, MOE_GROUPS), d ** -0.5),
        'moe_b_group': normal((DEPTH, MOE_GROUPS), 0.01),
        'moe_w_expert': normal((DEPTH, d, MOE_EXPERTS), d ** -0.5),
        'moe_b_expert': normal((DEPTH, MOE_EXPERTS), 0.01),
        'moe_w1': normal((DEPTH, MOE_EXPERTS, d, MOE_D_FF), d ** -0.5),
        'moe_w3': normal((DEPTH, MOE_EXPERTS, d, MOE_D_FF), d ** -0.5),
        'moe_w2': normal((DEPTH, MOE_EXPERTS, MOE_D_FF, d), MOE_D_FF ** -0.5),
        'final_norm': gain((d,)),
    }

def reference(x, c, ctx, c_ctx, w_mod, b_mod, norm_mix, norm_ffn, gdn_w_in, gdn_conv, gdn_a_log,
              gdn_dt_bias, gdn_norm, gdn_w_out, diff_w_qkv, diff_lambda, diff_norm, diff_w_out,
              mla_w_down, mla_q_norm, mla_kv_norm, mla_w_uq, mla_w_ukv, mla_w_out, moe_w_group,
              moe_b_group, moe_w_expert, moe_b_expert, moe_w1, moe_w3, moe_w2, final_norm):
    bsz, seq, d = x.shape
    ctx_len = ctx.shape[1]
    rows = seq // GRID_W
    cos_d, sin_d = axial_rope_tables(rows, DIFF_HEAD_DIM)
    cos_m, sin_m = axial_rope_tables(rows, MLA_ROPE)
    silu_c = jax.nn.silu(c)
    silu_cc = jax.nn.silu(c_ctx)
    for i in range(DEPTH):
        kind, j = i % N_MIXERS, i // N_MIXERS
        last = i == DEPTH - 1
        mod = jnp.split((silu_c @ w_mod[i] + b_mod[i])[:, None, :], 6, axis=-1)
        mod_c = jnp.split(silu_cc @ w_mod[i] + b_mod[i], 6, axis=-1)
        h_lat = rmsnorm(x, norm_mix[i]) * (1.0 + mod[1]) + mod[0]
        h_ctx = rmsnorm(ctx, norm_mix[i]) * (1.0 + mod_c[1]) + mod_c[0]
        if kind == 0:
            o_ctx, o_lat = gdn_mixer(h_ctx, h_lat, gdn_w_in[j], gdn_conv[j], gdn_a_log[j],
                                     gdn_dt_bias[j], gdn_norm[j], gdn_w_out[j])
        elif kind == 1:
            lam_init = 0.8 - 0.6 * math.exp(-0.3 * i)
            o_ctx, o_lat = diff_mixer(h_ctx, h_lat, cos_d, sin_d, diff_w_qkv[j], diff_lambda[j],
                                      diff_norm[j], diff_w_out[j], lam_init)
        else:
            o_ctx, o_lat = mla_mixer(h_ctx, h_lat, cos_m, sin_m, mla_w_down[j], mla_q_norm[j],
                                     mla_kv_norm[j], mla_w_uq[j], mla_w_ukv[j], mla_w_out[j])
        x = x + mod[2] * o_lat
        h_lat = rmsnorm(x, norm_ffn[i]) * (1.0 + mod[4]) + mod[3]
        if last:
            y_lat = hier_moe(h_lat.reshape(-1, d), moe_w_group[i], moe_b_group[i], moe_w_expert[i],
                             moe_b_expert[i], moe_w1[i], moe_w3[i], moe_w2[i]).reshape(bsz, seq, d)
            x = x + mod[5] * y_lat
        else:
            ctx = ctx + mod_c[2] * o_ctx
            h_ctx = rmsnorm(ctx, norm_ffn[i]) * (1.0 + mod_c[4]) + mod_c[3]
            h_all = jnp.concatenate([h_ctx, h_lat], axis=1).reshape(-1, d)
            y = hier_moe(h_all, moe_w_group[i], moe_b_group[i], moe_w_expert[i], moe_b_expert[i],
                         moe_w1[i], moe_w3[i], moe_w2[i]).reshape(bsz, ctx_len + seq, d)
            ctx = ctx + mod_c[5] * y[:, :ctx_len]
            x = x + mod[5] * y[:, ctx_len:]
    return rmsnorm(x, final_norm)


_drawn_inputs = setup_inputs


def setup_inputs(seed=0):
    import zlib

    import numpy as np

    out = dict(_drawn_inputs(seed))
    spreads = {}
    factors = {'norm_mix': 6.28,
     'norm_ffn': 4.767,
     'gdn_norm': 8.0,
     'diff_norm': 8.0,
     'moe_b_group': 8.0,
     'moe_b_expert': 5.821,
     'final_norm': 5.809}
    for name, (base, spread) in spreads.items():
        noise = np.random.default_rng([zlib.crc32(name.encode()), seed]).standard_normal(out[name].shape)
        drawn = base * np.exp(spread * noise) if base else spread * noise
        out[name] = jnp.asarray(drawn.astype(out[name].dtype))
    for name, factor in factors.items():
        out[name] = (out[name] * factor).astype(out[name].dtype)
    return out
```

```python
import math
from contextlib import ExitStack

import concourse.bass as bass
from concourse import mybir
import numpy as np

P = 128
F32 = mybir.dt.float32
U32 = mybir.dt.uint32
ALU = mybir.AluOpType
ACT = mybir.ActivationFunctionType
AX = mybir.AxisListType

D = 1024
KC = D // P
N_CTX = 256
N_LAT = 256
T = N_CTX + N_LAT
NT = T // P
DEPTH = 2
GRID_W = 64
EPS = 1e-6
SUBLN_EPS = 1e-5
HEADS = 8
CHUNK = 64
NCH = T // CHUNK
TAPS = 5
HALO = TAPS // 2
SEGW = N_CTX + 2 * HALO
GDN_COLS = 4 * D + 4 * HEADS
DH = 64
GROUPS = 4
PER_GROUP = 8
EXPERTS = GROUPS * PER_GROUP
FF = D // 2
FC = FF // P
CAP = 64
MAX_ASSIGN = 2 * T
MAX_BLOCKS = EXPERTS + MAX_ASSIGN // CAP
MAX_PAIRS = MAX_BLOCKS // 2
LAM_INIT = 0.8 - 0.6 * math.exp(-0.3)
BIG = 1.0e30
LEVELS = (1, 2, 4, 8, 16, 32)


def layout(widths):
    at, out = 0, {}
    for name, width in widths:
        out[name] = (at, at + width)
        at += width
    return out, at


CONST, CONST_W = layout([
    ("ident", P), ("ones", P), ("cum_f", P), ("cum_b", P), ("block", P), ("before", P),
    ("neg", 2 * P), ("level", 2 * len(LEVELS) * P), ("rot", P), ("cos", N_LAT), ("sin", N_LAT),
    ("iota", P), ("desc4", GROUPS), ("desc32", EXPERTS), ("eid", EXPERTS), ("eid31", EXPERTS),
    ("caps", 7), ("pairs", MAX_PAIRS - 1), ("pairid", MAX_PAIRS), ("ovid", MAX_BLOCKS - EXPERTS),
    ("tok", NT),
])
PARAM, PARAM_W = layout([
    ("cond", KC * 2), ("bmod", DEPTH * 6 * KC), ("mix", DEPTH * KC), ("ffn", DEPTH * KC),
    ("final", KC), ("conv", (HEADS + 1) * 3 * TAPS), ("gdn_gain", 1), ("diff_gain", 1),
    ("alog", 2 * HEADS), ("dt", 2 * HEADS), ("lam", 4 * DH), ("rbias", DEPTH * (GROUPS + EXPERTS)),
])


def shape_constants():
    c = np.zeros((P, CONST_W), np.float32)
    row = np.arange(P)[:, None]
    col = np.arange(P)[None, :]
    same = (row // CHUNK) == (col // CHUNK)

    def put(name, v, at=0):
        a = CONST[name][0] + at
        c[:, a:a + v.shape[-1]] = v

    put("ident", (row == col).astype(np.float32))
    put("ones", np.ones((P, P), np.float32))
    put("cum_f", (same & (row <= col)).astype(np.float32))
    put("cum_b", (same & (row >= col)).astype(np.float32))
    put("block", same.astype(np.float32))
    put("before", (row < col).astype(np.float32))
    put("neg", np.where(same & (row <= col), 0.0, -BIG).astype(np.float32))
    put("neg", np.where(same & (row >= col), 0.0, -BIG).astype(np.float32), P)
    for n, s in enumerate(LEVELS):
        pair = (row // (2 * s)) == (col // (2 * s))
        low_r, low_c = (row // s) % 2 == 0, (col // s) % 2 == 0
        put("level", (pair & low_r & ~low_c).astype(np.float32), n * P)
        put("level", (pair & ~low_r & low_c).astype(np.float32), (len(LEVELS) + n) * P)
    quarter = DH // 4
    ch = np.arange(P)
    second = (ch // quarter) % 2 == 1
    rot = np.zeros((P, P), np.float32)
    for o in range(P):
        if second[o]:
            rot[o - quarter, o] = 1.0
        else:
            rot[o + quarter, o] = -1.0
    put("rot", rot)
    freq = (np.float32(10000.0) ** (-np.arange(quarter, dtype=np.float32) / quarter)).astype(np.float32)
    t = np.arange(N_LAT)
    pos = np.stack([(t // GRID_W), (t % GRID_W)]).astype(np.float32)
    axis = (ch // (2 * quarter)) % 2
    ang = pos[axis] * freq[ch % quarter][:, None]
    put("cos", np.cos(ang))
    put("sin", np.sin(ang))
    put("iota", np.broadcast_to(np.arange(P, dtype=np.float32), (P, P)))
    put("desc4", np.broadcast_to(np.arange(GROUPS, 0, -1, dtype=np.float32), (P, GROUPS)))
    put("desc32", np.broadcast_to(np.arange(EXPERTS, 0, -1, dtype=np.float32), (P, EXPERTS)))
    put("eid", np.broadcast_to(np.arange(EXPERTS, dtype=np.float32), (P, EXPERTS)))
    put("eid31", np.broadcast_to(EXPERTS - 1 - np.arange(EXPERTS, dtype=np.float32), (P, EXPERTS)))
    put("caps", np.broadcast_to(CAP * np.arange(1, 8, dtype=np.float32), (P, 7)))
    put("pairs", np.broadcast_to(P * np.arange(1, MAX_PAIRS, dtype=np.float32), (P, MAX_PAIRS - 1)))
    put("pairid", np.broadcast_to(np.arange(MAX_PAIRS, dtype=np.float32), (P, MAX_PAIRS)))
    put("ovid", np.broadcast_to(np.arange(MAX_BLOCKS - EXPERTS, dtype=np.float32), (P, MAX_BLOCKS - EXPERTS)))
    put("tok", (np.arange(P)[:, None] + P * np.arange(NT)[None, :]).astype(np.float32))
    return c


def packed_params(i):
    v = np.zeros((P, PARAM_W), np.float32)

    def put(name, a, at=0):
        s = PARAM[name][0] + at
        v[:, s:s + a.shape[-1]] = a

    def columns(a):
        return np.asarray(a).reshape(-1, P).T

    for n, a in enumerate((i["c_ctx"], i["c"][0])):
        for k in range(KC):
            put("cond", np.asarray(a)[k * P:(k + 1) * P, None], 2 * k + n)
    for d in range(DEPTH):
        put("bmod", columns(i["b_mod"][d]), d * 6 * KC)
        put("mix", columns(i["norm_mix"][d]), d * KC)
        put("ffn", columns(i["norm_ffn"][d]), d * KC)
        put("rbias", np.broadcast_to(np.asarray(i["moe_b_group"][d])[None], (P, GROUPS)), d * (GROUPS + EXPERTS))
        put("rbias", np.broadcast_to(np.asarray(i["moe_b_expert"][d])[None], (P, EXPERTS)),
            d * (GROUPS + EXPERTS) + GROUPS)
    put("final", columns(i["final_norm"]))
    conv = np.asarray(i["gdn_conv"][0])
    for h in range(HEADS):
        for piece in range(3):
            a = piece * D + h * P
            put("conv", conv[:, a:a + P].T, (h * 3 + piece) * TAPS)
    put("gdn_gain", np.asarray(i["gdn_norm"][0])[:, None])
    put("diff_gain", np.asarray(i["diff_norm"][0])[:, None])
    put("alog", np.broadcast_to(np.asarray(i["gdn_a_log"][0]).reshape(1, -1), (P, 2 * HEADS)))
    put("dt", np.broadcast_to(np.asarray(i["gdn_dt_bias"][0]).reshape(1, -1), (P, 2 * HEADS)))
    put("lam", np.broadcast_to(np.asarray(i["diff_lambda"][0]).reshape(1, -1), (P, 4 * DH)))
    return v


class Steps:

    def __init__(self, sem, names):
        self.sem, self.names, self.next = sem, list(names), 0

    def did(self, name):
        assert self.names[self.next % len(self.names)] == name, (name, self.names[self.next % len(self.names)])
        self.next += 1
        return self.sem

    def at(self, name, rnd=None):
        n = self.names.index(name) + 1
        return n if rnd is None else (rnd + 1) * len(self.names) + n

    @property
    def n(self):
        return len(self.names)


class Arena:

    def __init__(self, nc, at, tag):
        self.nc, self.at, self.tag = nc, at, tag

    def __call__(self, name, shape, dtype=F32):
        size = 4
        for s in shape[1:]:
            size *= s
        t = self.nc.alloc_sbuf_tensor_at(f"{self.tag}_{name}", shape, dtype, offset=self.at)
        self.at += (size + 31) // 32 * 32
        assert self.at <= self.nc.sbuf_usable_end, (self.tag, name, self.at, self.nc.sbuf_usable_end)
        return t


def spread(ap, axis, n):
    v = ap.unsqueeze(axis)
    shape = list(v.shape)
    shape[axis] = n
    return v.broadcast_to(shape)


class Core:

    def __init__(self, nc, ctx, ins, out):
        self.nc, self.ctx, self.ins, self.out, self.sems = nc, ctx, ins, out, 0
        self.bank = [ctx.enter_context(nc.psum_tensor(f"bank{b}", [P, 512], F32)) for b in range(8)]
        keep = Arena(nc, (nc.sbuf_usable_end - nc.sbuf_bytes_remaining + 31) // 32 * 32, "keep")
        self.cst = keep("constants", [P, CONST_W])
        self.par = keep("params", [P, PARAM_W])
        self.xT = keep("xT", [P, KC, T])
        self.cond = keep("cond", [P, KC, 2])
        self.mod = keep("mod", [P, DEPTH, 6 * KC, 2])
        self.small = keep("small", [P, 8])
        self.free = keep.at
        self.stage, self.live = 0, []

    def arena(self, at=None):
        self.stage += 1
        return Arena(self.nc, self.free if at is None else at, f"s{self.stage}")

    def sem(self, name):
        self.sems += 1
        self.live.append(self.nc.alloc_semaphore(f"{name}_{self.sems}"))
        return self.live[-1]

    def recycle(self):
        self.nc.clear_and_free_semaphores(self.live)
        self.live = []
        self.nc.all_engine_barrier()

    def c(self, name):
        a, b = CONST[name]
        return self.cst[:, a:b]

    def p(self, name):
        a, b = PARAM[name]
        return self.par[:, a:b]

    def links(self, name):
        sem, count = self.sem(name), [0]

        def link(eng, ins):
            count[0] += 1
            ins.then_inc(sem, 1)
            eng.wait_ge(sem, count[0])
        return link


def stage_load(k):
    nc, ar = k.nc, k.arena()
    x_in = ar("x_in", [P, NT, D])
    loaded, x_loaded = k.sem("loaded"), k.sem("x_loaded")
    turned, moved, done = k.sem("turned"), k.sem("moved"), k.sem("silu")
    zeros = ar("zeros", [P, D])
    zeroed, filled = k.sem("zeroed"), k.sem("filled")
    with nc.Block() as block:
        @block.gpsimd
        def _(pool):
            nc.gpsimd.memset(zeros[:], 0.0).then_inc(zeroed, 1)
            pool.wait_ge(zeroed, 1)
            for b in range(EXPERTS * CAP // P, MAX_PAIRS):
                nc.gpsimd.dma_start(k.y_dram[b * P:(b + 1) * P, :], zeros[:]).then_inc(filled, 16)
            pool.wait_ge(filled, 16 * (MAX_PAIRS - EXPERTS * CAP // P))

        @block.sync
        def _(sp):
            nc.sync.dma_start(k.cst[:], k.ins["constants"]).then_inc(loaded, 16)
            nc.sync.dma_start(k.par[:], k.ins["params"]).then_inc(loaded, 16)
            nc.sync.dma_start(x_in[:, 0:2, :], k.ins["ctx"][0].rearrange("(t p) d -> p t d", p=P)).then_inc(x_loaded, 16)
            nc.sync.dma_start(x_in[:, 2:4, :], k.ins["x"][0].rearrange("(t p) d -> p t d", p=P)).then_inc(x_loaded, 16)

        @block.tensor
        def _(pe):
            pe.wait_ge(loaded, 32)
            pe.wait_ge(x_loaded, 32)
            for kc in range(KC):
                for t in range(NT):
                    last = nc.tensor.transpose(k.bank[kc][:, t * P:(t + 1) * P], x_in[:, t, kc * P:(kc + 1) * P],
                                               k.c("ident"))
                last.then_inc(turned, 1)

        @block.vector
        def _(dve):
            for kc in range(KC):
                dve.wait_ge(turned, kc + 1)
                nc.vector.tensor_copy(k.xT[:, kc, :], k.bank[kc][:]).then_inc(moved, 1)
            dve.wait_ge(moved, KC)

        @block.scalar
        def _(act):
            act.wait_ge(loaded, 32)
            nc.scalar.activation(k.cond[:].rearrange("p a b -> p (a b)"), k.p("cond"), ACT.Silu).then_inc(done, 1)
            act.wait_ge(done, 1)


def stage_mod(k, layer):
    nc, ar = k.nc, k.arena()
    RING, STRIP = 3, 512
    rounds = 6 * D // STRIP // RING
    ring = [ar(f"w{r}", [P, KC, STRIP]) for r in range(RING)]
    landed = [k.sem(f"mod_w{r}") for r in range(RING)]
    pe_s = Steps(k.sem("mod_strip"), [f"strip{r}" for r in range(RING)])
    added = k.sem("mod_added")
    w = k.ins["w_mod"][layer].rearrange("(k p) n -> p k n", p=P)
    per = STRIP // P
    with nc.Block() as block:
        @block.sync
        def _(sp):
            with sp.Fori(0, rounds) as g:
                for r in range(RING):
                    sp.wait_ge(pe_s.sem, pe_s.at(f"strip{r}", g - 1))
                    nc.sync.dma_start(ring[r][:], w[:, :, bass.ds((g * RING + r) * STRIP, STRIP)]).then_inc(landed[r], 16)

        @block.tensor
        def _(pe):
            pe.sem_inc(pe_s.sem, pe_s.n)
            with pe.Fori(0, rounds) as g:
                for r in range(RING):
                    pe.wait_ge(landed[r], (g + 1) * 16)
                    for j in range(per):
                        for kc in range(KC):
                            last = nc.tensor.matmul(k.bank[0][:, bass.ds(((g * RING + r) * per + j) * 2, 2)],
                                                    ring[r][:, kc, j * P:(j + 1) * P], k.cond[:, kc, :],
                                                    start=(kc == 0), stop=(kc == KC - 1))
                    last.then_inc(pe_s.did(f"strip{r}"), 1)

        @block.vector
        def _(dve):
            dve.wait_ge(pe_s.sem, pe_s.at(f"strip{RING - 1}", rounds - 1))
            a = PARAM["bmod"][0] + layer * 6 * KC
            nc.vector.tensor_tensor(k.mod[:, layer], k.bank[0][:, 0:12 * KC].rearrange("p (m c) -> p m c", c=2),
                                    spread(k.par[:, a:a + 6 * KC], 2, 2), ALU.add).then_inc(added, 1)
            dve.wait_ge(added, 1)


def stage_norm(k, dst, gain, layer=None, shift=None, t0=0, eps=EPS):
    nc, ar = k.nc, k.arena(k.norm_at)
    n = T - t0
    sq = ar("sq", [P, 2, n])
    rstd = ar("rstd", [P, n])
    tmp = ar("tmp", [P, 2, n])
    scale = ar("scale", [P, KC, 2])
    squared, summed, rooted = k.sem("squared"), k.sem("summed"), k.sem("rooted")
    scaled, timed, out = k.sem("scaled"), k.sem("timed"), k.sem("normed")
    epsc = ar("epsc", [P, 1])
    halves = [(0, 0, N_CTX), (1, N_CTX, T)] if t0 == 0 else [(1, 0, n)]
    with nc.Block() as block:
        @block.tensor
        def _(pe):
            for kc in range(KC):
                pe.wait_ge(squared, kc + 1)
                nc.tensor.matmul(k.bank[0][:, 0:n], k.c("ones"), sq[:, kc % 2, :],
                                 start=(kc == 0), stop=(kc == KC - 1)).then_inc(summed, 1)

        @block.scalar
        def _(act):
            for kc in range(KC):
                if kc >= 2:
                    act.wait_ge(summed, kc - 1)
                nc.scalar.activation(sq[:, kc % 2, :], k.xT[:, kc, t0:T], ACT.Square).then_inc(squared, 1)
            act.wait_ge(summed, KC)
            act.wait_ge(scaled, 1)
            nc.scalar.activation(rstd[:], k.bank[0][:, 0:n], ACT.Ln, bias=epsc[:], scale=1.0 / D).then_inc(rooted, 1)
            act.wait_ge(rooted, 1)
            nc.scalar.activation(rstd[:], rstd[:], ACT.Exp, scale=-0.5).then_inc(rooted, 1)

        @block.vector
        def _(dve):
            nc.vector.memset(epsc[:], eps).then_inc(scaled, 1)
            if layer is None:
                nc.vector.tensor_copy(scale[:], spread(gain, 2, 2)).then_inc(scaled, 1)
                dve.wait_ge(scaled, 2)
            else:
                nc.vector.tensor_scalar(scale[:], k.mod[:, layer, (shift + 1) * KC:(shift + 2) * KC, :], 1.0, None,
                                        ALU.add).then_inc(scaled, 1)
                dve.wait_ge(scaled, 2)
                nc.vector.tensor_tensor(scale[:], scale[:], spread(gain, 2, 2), ALU.mult).then_inc(scaled, 1)
                dve.wait_ge(scaled, 3)
            dve.wait_ge(rooted, 2)
            for kc in range(KC):
                if kc >= 2:
                    dve.wait_ge(out, (kc - 1) * len(halves))
                nc.vector.tensor_tensor(tmp[:, kc % 2, :], k.xT[:, kc, t0:T], rstd[:], ALU.mult).then_inc(timed, 1)
                dve.wait_ge(timed, kc + 1)
                for c, a, b in halves:
                    if layer is None:
                        nc.vector.tensor_scalar(dst[:, kc, a:b], tmp[:, kc % 2, a:b], scale[:, kc, c:c + 1], None,
                                                ALU.mult).then_inc(out, 1)
                    else:
                        nc.vector.tensor_scalar(dst[:, kc, a:b], tmp[:, kc % 2, a:b], scale[:, kc, c:c + 1],
                                                k.mod[:, layer, shift * KC + kc, c:c + 1], ALU.mult,
                                                ALU.add).then_inc(out, 1)
            dve.wait_ge(out, KC * len(halves))


def stage_gdn_gates(k, g):
    nc, ar = k.nc, k.arena(k.norm_at)
    H2 = 2 * HEADS
    w_ab = ar("w_ab", [P, KC, 2 * H2])
    ab = ar("ab", [P, NT, 2, 2, HEADS])
    t1, t2, t3, t4 = (ar(f"t{i}", [P, NT, H2]) for i in range(4))
    gdec, beta, gcum, ecum = (ar(f"g{i}", [P, NT, H2]) for i in range(4))
    rows = ar("rows", [H2, 3, T])
    ea = ar("ea", [P, H2])
    one = ar("one", [P, 1])
    landed, stored = k.sem("w_ab"), k.sem("rows_stored")
    projected, cumulated, rows_turned = k.sem("ab_projected"), k.sem("cumulated"), k.sem("rows_turned")
    inputs_ready, decay_ready, cum_ready, ecum_seen = (k.sem(n) for n in ("gate_in", "decay_ready", "cum_ready", "ecum"))
    exps, logs, cum_exps = k.sem("gate_exps"), k.sem("gate_logs"), k.sem("cum_exps")
    rows_ready = k.sem("rows_ready")
    link = k.links("gates_link")

    with nc.Block() as block:
        @block.sync
        def _(sp):
            nc.sync.dma_start(w_ab[:], k.ins["gdn_w_in"][0].rearrange("(k p) n -> p k n", p=P)
                              [:, :, 4 * D:GDN_COLS]).then_inc(landed, 16)
            sp.wait_ge(rows_ready, 3)
            for d in range(2):
                nc.sync.dma_start(k.rows_dram[:, d], rows[d * HEADS:(d + 1) * HEADS]).then_inc(stored, 16)
            sp.wait_ge(stored, 32)

        @block.tensor
        def _(pe):
            pe.wait_ge(landed, 16)
            for t in range(NT):
                for kc in range(KC):
                    last = nc.tensor.matmul(k.bank[0][:, t * 2 * H2:(t + 1) * 2 * H2], g["hT"][:, kc, t * P:(t + 1) * P],
                                            w_ab[:, kc, :], start=(kc == 0), stop=(kc == KC - 1))
            last.then_inc(projected, 1)
            pe.wait_ge(decay_ready, 1)
            for t in range(NT):
                for d, m in enumerate(("cum_f", "cum_b")):
                    nc.tensor.matmul(k.bank[1][:, t * H2 + d * HEADS:t * H2 + (d + 1) * HEADS], k.c(m),
                                     gdec[:, t, d * HEADS:(d + 1) * HEADS], start=True, stop=True)
                last = nc.tensor.matmul(k.bank[2][:, t * H2:(t + 1) * H2], k.c("block"), gdec[:, t, :],
                                        start=True, stop=True)
            last.then_inc(cumulated, 1)
            pe.wait_ge(cum_ready, 1)
            pe.wait_ge(cum_exps, 1)
            for n, src in enumerate((gcum, beta, ecum)):
                for t in range(NT):
                    last = nc.tensor.transpose(k.bank[3 + n][0:H2, t * P:(t + 1) * P], src[:, t, :], k.c("ident"))
                last.then_inc(rows_turned, 1)

        @block.scalar
        def _(act):
            act.wait_ge(inputs_ready, 1)
            nc.scalar.activation(ea[:], k.p("alog"), ACT.Exp).then_inc(exps, 1)
            nc.scalar.activation(t2[:], t2[:], ACT.Exp, scale=-1.0).then_inc(exps, 1)
            nc.scalar.activation(t1[:], t1[:], ACT.Exp).then_inc(exps, 1)
            act.wait_ge(exps, 3)
            nc.scalar.activation(t1[:], t1[:], ACT.Ln, bias=one[:]).then_inc(logs, 1)
            act.wait_ge(cum_ready, 1)
            nc.scalar.activation(ecum[:], gcum[:], ACT.Exp).then_inc(cum_exps, 1)
            nc.scalar.activation(t3[:], t3[:], ACT.Exp).then_inc(cum_exps, 1)

        @block.vector
        def _(dve):
            link(dve, nc.vector.memset(one[:], 1.0))
            dve.wait_ge(projected, 1)
            link(dve, nc.vector.tensor_copy(ab[:].rearrange("p t a b h -> p (t a b h)"), k.bank[0][:, 0:NT * 2 * H2]))
            for t in range(NT):
                for d in range(2):
                    cols = slice(d * HEADS, (d + 1) * HEADS)
                    nc.vector.tensor_tensor(t3[:, t, cols], ab[:, t, d, 0, :],
                                            k.p("dt")[:, cols], ALU.add).then_inc(ecum_seen, 1)
                    nc.vector.tensor_copy(t2[:, t, cols], ab[:, t, d, 1, :]).then_inc(ecum_seen, 1)
            dve.wait_ge(ecum_seen, 4 * NT)
            link(dve, nc.vector.tensor_scalar(t4[:], t3[:], -1.0, None, ALU.mult))
            link(dve, nc.vector.tensor_tensor(t1[:], t3[:], t4[:], ALU.min))
            nc.vector.tensor_scalar(t3[:], t3[:], 0.0, None, ALU.max).then_inc(inputs_ready, 1)
            dve.wait_ge(logs, 1)
            dve.wait_ge(inputs_ready, 1)
            link(dve, nc.vector.tensor_tensor(t1[:], t1[:], t3[:], ALU.add))
            link(dve, nc.vector.tensor_tensor(t1[:], t1[:], spread(ea[:], 1, NT), ALU.mult))
            nc.vector.tensor_scalar(gdec[:], t1[:], -1.0, None, ALU.mult).then_inc(decay_ready, 1)
            link(dve, nc.vector.tensor_scalar(t2[:], t2[:], 1.0, None, ALU.add))
            link(dve, nc.vector.reciprocal(beta[:], t2[:]))
            dve.wait_ge(cumulated, 1)
            link(dve, nc.vector.tensor_copy(gcum[:].rearrange("p t h -> p (t h)"), k.bank[1][:, 0:NT * H2]))
            nc.vector.tensor_tensor(t3[:].rearrange("p t h -> p (t h)"), k.bank[2][:, 0:NT * H2],
                                    gcum[:].rearrange("p t h -> p (t h)"), ALU.subtract).then_inc(cum_ready, 1)
            dve.wait_ge(cum_exps, 2)
            link(dve, nc.vector.tensor_tensor(t4[:], beta[:], ecum[:], ALU.mult))
            link(dve, nc.vector.tensor_scalar(t1[:], gcum[:], -1.0, None, ALU.mult))
            for kind, src in enumerate((beta, t4, t3, t1)):
                for d in range(2):
                    for t in range(NT):
                        link(dve, nc.vector.tensor_copy(g["cols"][:, :, kind, d, t], src[:, t, d * HEADS:(d + 1) * HEADS]))
            for n in range(3):
                dve.wait_ge(rows_turned, n + 1)
                nc.vector.tensor_copy(rows[:, n, :], k.bank[3 + n][0:H2, :]).then_inc(rows_ready, 1)
            dve.wait_ge(rows_ready, 3)


PIECES = "qkvz"


def project_piece(k, g, piece, kc):
    return k.nc.tensor.matmul(k.bank[piece % 2][:], g["w"][piece][:, kc, :], g["hT"][:, kc, :],
                              start=(kc == 0), stop=(kc == KC - 1))


def evacuate_piece(k, g, piece):
    if piece == 3:
        return k.nc.scalar.activation(g["zraw"][:], k.bank[1][:], ACT.Copy)
    return k.nc.scalar.activation(g["pad"][piece][:, :, HALO:HALO + N_CTX],
                                  k.bank[piece % 2][:].rearrange("p (s t) -> p s t", s=2), ACT.Copy)


def conv_tap(k, g, piece, tap):
    src = g["pad"][piece][:, :, tap:tap + N_CTX]
    dst = g["conv"][piece][:].rearrange("p (s t) -> p s t", s=2)
    w = g["taps"][:, piece * TAPS + tap:piece * TAPS + tap + 1]
    if tap == 0:
        return k.nc.vector.tensor_scalar(dst, src, w, None, ALU.mult)
    return k.nc.vector.scalar_tensor_tensor(out=dst, in0=src, scalar=w, in1=dst, op0=ALU.mult, op1=ALU.add)


def head_weight(k, piece, head):
    w = k.ins["gdn_w_in"][0].rearrange("(k p) n -> p k n", p=P)
    return w[:, :, bass.ds(head * P + piece * D, P)]


def stage_gdn_first(k, g):
    nc = k.nc
    landed = [k.sem(f"w0_{p}") for p in PIECES]
    projected, moved, zeroed, taps_in, convolved = (k.sem(n) for n in ("proj0", "moved0", "pads_zero", "taps0", "conv0"))
    with nc.Block() as block:
        @block.sync
        def _(sp):
            for p in range(4):
                nc.sync.dma_start(g["w"][p][:], head_weight(k, p, 0)).then_inc(landed[p], 16)

        @block.gpsimd
        def _(pool):
            for p in range(3):
                nc.gpsimd.memset(g["pad"][p][:], 0.0).then_inc(zeroed, 1)
            pool.wait_ge(zeroed, 3)

        @block.tensor
        def _(pe):
            for p in range(4):
                pe.wait_ge(landed[p], 16)
                if p >= 2:
                    pe.wait_ge(moved, p - 1)
                for kc in range(KC):
                    last = project_piece(k, g, p, kc)
                last.then_inc(projected, 1)

        @block.scalar
        def _(act):
            act.wait_ge(zeroed, 3)
            for p in range(4):
                act.wait_ge(projected, p + 1)
                evacuate_piece(k, g, p).then_inc(moved, 1)
            act.wait_ge(moved, 4)

        @block.vector
        def _(dve):
            nc.vector.tensor_copy(g["taps"][:], k.p("conv")[:, 0:3 * TAPS]).then_inc(taps_in, 1)
            dve.wait_ge(taps_in, 1)
            for p in range(3):
                dve.wait_ge(moved, p + 1)
                for tap in range(TAPS):
                    conv_tap(k, g, p, tap).then_inc(convolved, 1)
                    dve.wait_ge(convolved, p * TAPS + tap + 1)


def fetch_rows(k, g, head, sem):
    src = k.rows_dram[bass.ds(head, 1)].rearrange("o d n t -> o (d n t)").broadcast_to([P, 6 * T])
    return k.nc.sync.dma_start(g["rows"][:].rearrange("p d n t -> p (d n t)"), src).then_inc(sem, 16)


def stage_gdn_heads(k, g):
    nc = k.nc
    L = range(1, len(LEVELS))
    last_level = len(LEVELS) - 1
    DIR = (0, 1)
    per_seq = N_CTX // CHUNK
    order = [list(range(NCH)), list(range(per_seq - 1, -1, -1)) + list(range(NCH - 1, per_seq - 1, -1))]
    E, B, KQ, A = g["E"], g["B"], g["KQ"], g["A"]
    X, XT, Z, As = g["E"], g["XT"], g["B"], g["As"]
    U, W = g["A"], g["W"]

    rec = [(c, d) for c in range(NCH) for d in DIR]
    PE = Steps(k.sem("gdn_pe"), ["nq", "nk", "kk", "kq", "pr_q", "trk", "trv", "x0_0", "x0_1"]
               + [s for l in L for s in ([f"Z{l}_0", f"Z{l}_1", f"D{l}_0", f"D{l}_1"]
                                         + ([f"T{l}_0", f"T{l}_1"] if l < last_level else [])
                                         + (["pr_k"] if l == 3 else []))]
               + ["u0", "w0", "u1", "w1", "pr_v"]
               + [s for c, d in rec for s in ([f"ws{c}_{d}", f"o{c}_{d}"] + ([f"up{c}_{d}"] if c < NCH - 1 else [])
                                              + (["pr_z"] if (c, d) == (3, 1) else []))]
               + ["on"])
    SC = Steps(k.sem("gdn_act"), ["silu_q", "silu_k", "silu_v", "silu_z", "sq_q", "sq_k", "ln_q", "rs_q", "ln_k", "rs_k"]
               + [f"E{d}_{t}" for d in DIR for t in range(NT)] + ["ktok", "vtok", "ev_q", "x0_0", "x0_1"]
               + [s for l in L for s in ([f"Z{l}_0", f"Z{l}_1"] + ([f"T{l}_0", f"T{l}_1"] if l < last_level else [])
                                         + (["ev_k"] if l == 3 else []))]
               + ["u0", "w0", "u1", "w1", "ev_v", "ev_z", "osq", "ln_o", "rs_o"])
    V = Steps(k.sem("gdn_dve"), ["cols", "taps", "S0", "S1", "tmp0", "tmp1", "last0", "last1", "qn", "kn"]
              + ["qe0", "qe1", "B0", "B1", "A0", "A1", "aT0", "aT1", "m0", "m1", "XT0", "XT1"]
              + [f"X{l}_{d}" for l in L for d in DIR]
              + [s for c, d in rec for s in ([f"vn{c}_{d}"] + ([f"S{c}_{d}"] if c < NCH - 1 else [])
                                             + ([f"c{c - 1}_{t}" for t in range(TAPS)] if d == 1 and 1 <= c <= 3 else []))]
              + ["on", "og"])
    G = Steps(k.sem("gdn_pool"), [f"As{l}_{d}" for l in L for d in DIR]
              + [f"{n}{d}" for n in ("vb", "kbe", "kd") for d in DIR])
    w_in = [k.sem(f"w_{p}") for p in PIECES]
    rows_in = k.sem("rows_in")

    def last_of(d, c):
        return c * CHUNK + (CHUNK - 1 if d == 0 else 0)

    def place(d, step):
        c = order[d][step]
        return c, c // 2, (c % 2) * CHUNK

    with nc.Block() as block:
        @block.sync
        def _(sp):
            for p in range(4):
                nc.sync.dma_start(g["w"][p][:], head_weight(k, p, 1)).then_inc(w_in[p], 16)
            fetch_rows(k, g, 0, rows_in)

            def fetch_next(h, head):
                sp.wait_ge(V.sem, V.at("aT1", h))
                fetch_rows(k, g, h + 1, rows_in)
                for p in range(4):
                    sp.wait_ge(PE.sem, PE.at(f"pr_{PIECES[p]}", h))
                    nc.sync.dma_start(g["w"][p][:], head_weight(k, p, head)).then_inc(w_in[p], 16)

            with sp.Fori(0, HEADS - 2) as h:
                fetch_next(h, h + 2)
            fetch_next(HEADS - 2, HEADS - 1)

        @block.gpsimd
        def _(pool):
            pool.sem_inc(G.sem, G.n)
            with pool.Fori(0, HEADS) as h:
                for l in L:
                    for d in DIR:
                        if l == 1:
                            pool.wait_ge(V.sem, V.at(f"A{d}", h))
                        m = k.c("level")[:, (d * len(LEVELS) + l) * P:(d * len(LEVELS) + l + 1) * P]
                        nc.gpsimd.tensor_tensor(As[:, l - 1, d], A[:, d], spread(m, 1, NT), ALU.mult)\
                            .then_inc(G.did(f"As{l}_{d}"), 1)
                pool.wait_ge(SC.sem, SC.at("vtok", h))
                for n, src, kind in (("vb", g["vtok"], 0), ("kbe", g["ktok"], 1), ("kd", g["ktok"], 2)):
                    for d in DIR:
                        nc.gpsimd.tensor_tensor(g[n][:, d], src[:], spread(g["hcols"][:, kind, d, :], 2, P), ALU.mult)\
                            .then_inc(G.did(f"{n}{d}"), 1)

        @block.tensor
        def _(pe):
            pe.sem_inc(PE.sem, PE.n)
            with pe.Fori(0, HEADS) as h:
                def fill(p, first, count):
                    for kc in range(first, first + count):
                        if kc == 0:
                            pe.wait_ge(w_in[p], (h + 1) * 16)
                            if p >= 2:
                                pe.wait_ge(SC.sem, SC.at(f"ev_{PIECES[p - 2]}", h))
                        ins = project_piece(k, g, p, kc)
                    if first + count == KC:
                        ins.then_inc(PE.did(f"pr_{PIECES[p]}"), 1)

                pe.wait_ge(SC.sem, SC.at("sq_q", h))
                nc.tensor.matmul(k.bank[3][:], k.c("ones"), g["sq"][:, 0], start=True, stop=True).then_inc(PE.did("nq"), 1)
                pe.wait_ge(SC.sem, SC.at("sq_k", h))
                nc.tensor.matmul(k.bank[4][:], k.c("ones"), g["sq"][:, 1], start=True, stop=True).then_inc(PE.did("nk"), 1)
                fill(0, 0, 7)
                pe.wait_ge(V.sem, V.at("kn", h))
                for t in range(NT):
                    s = slice(t * P, (t + 1) * P)
                    last = nc.tensor.matmul(k.bank[5][:, s], g["k"][:, s], g["k"][:, s], start=True, stop=True)
                last.then_inc(PE.did("kk"), 1)
                for t in range(NT):
                    s = slice(t * P, (t + 1) * P)
                    last = nc.tensor.matmul(k.bank[6][:, s], g["k"][:, s], g["q"][:, s], start=True, stop=True)
                last.then_inc(PE.did("kq"), 1)
                fill(0, 7, 1)
                for t in range(NT):
                    last = nc.tensor.transpose(k.bank[7][:, t * P:(t + 1) * P], g["k"][:, t * P:(t + 1) * P], k.c("ident"))
                last.then_inc(PE.did("trk"), 1)
                pe.wait_ge(SC.sem, SC.at("ln_q", h))
                for t in range(NT):
                    last = nc.tensor.transpose(k.bank[3][:, t * P:(t + 1) * P], g["v"][:, t * P:(t + 1) * P], k.c("ident"))
                last.then_inc(PE.did("trv"), 1)
                pe.wait_ge(SC.sem, SC.at("vtok", h))
                for d in DIR:
                    pe.wait_ge(V.sem, V.at(f"XT{d}", h))
                    for t in range(NT):
                        last = nc.tensor.transpose(k.bank[3 + d][:, t * P:(t + 1) * P], XT[:, d, t], k.c("ident"))
                    last.then_inc(PE.did(f"x0_{d}"), 1)
                for l in L:
                    for d in DIR:
                        pe.wait_ge(G.sem, G.at(f"As{l}_{d}", h))
                        if l == 1:
                            pe.wait_ge(SC.sem, SC.at(f"x0_{d}", h))
                        else:
                            pe.wait_ge(V.sem, V.at(f"X{l - 1}_{d}", h))
                            pe.wait_ge(SC.sem, SC.at(f"T{l - 1}_{d}", h))
                        for t in range(NT):
                            last = nc.tensor.matmul(k.bank[3 + d][:, t * P:(t + 1) * P], As[:, l - 1, d, t], X[:, d, t],
                                                    start=True, stop=True)
                        last.then_inc(PE.did(f"Z{l}_{d}"), 1)
                    fill(1 if l <= 3 else 2, (0, 3, 6, 0, 2)[l - 1], (3, 3, 2, 2, 2)[l - 1]) if l != 3 else None
                    for d in DIR:
                        pe.wait_ge(SC.sem, SC.at(f"Z{l}_{d}", h))
                        for t in range(NT):
                            a, b = (XT[:, d, t], Z[:, d, t]) if l < last_level else (Z[:, d, t], XT[:, d, t])
                            last = nc.tensor.matmul(k.bank[5 + d][:, t * P:(t + 1) * P], a, b, start=True, stop=True)
                        last.then_inc(PE.did(f"D{l}_{d}"), 1)
                    if l < last_level:
                        for d in DIR:
                            pe.wait_ge(V.sem, V.at(f"X{l}_{d}", h))
                            for t in range(NT):
                                last = nc.tensor.transpose(k.bank[3 + d][:, t * P:(t + 1) * P], X[:, d, t], k.c("ident"))
                            last.then_inc(PE.did(f"T{l}_{d}"), 1)
                    if l == 3:
                        fill(1, 6, 2)
                for d in DIR:
                    pe.wait_ge(V.sem, V.at(f"X{last_level}_{d}", h))
                    pe.wait_ge(G.sem, G.at(f"vb{d}", h))
                    for t in range(NT):
                        last = nc.tensor.matmul(k.bank[3 + d][:, t * P:(t + 1) * P], XT[:, d, t], g["vb"][:, d, t],
                                                start=True, stop=True)
                    last.then_inc(PE.did(f"u{d}"), 1)
                    pe.wait_ge(G.sem, G.at(f"kbe{d}", h))
                    for t in range(NT):
                        last = nc.tensor.matmul(k.bank[5 + d][:, t * P:(t + 1) * P], g["kbe"][:, d, t], XT[:, d, t],
                                                start=True, stop=True)
                    last.then_inc(PE.did(f"w{d}"), 1)
                fill(2, 4, 4)
                pe.wait_ge(G.sem, G.at("kd1", h))
                fills = [3, 3, 2, 0]
                zk = 0
                for c, d in rec:
                    ch, tile, r = place(d, c)
                    cols = slice(ch * CHUNK, (ch + 1) * CHUNK)
                    part = slice(r, r + CHUNK)
                    if c == 0:
                        pe.wait_ge(SC.sem, SC.at(f"w{d}", h))
                    else:
                        pe.wait_ge(V.sem, V.at(f"S{c - 1}_{d}", h))
                    S = g["S"][:, d]
                    nc.tensor.matmul(k.bank[3 + d][part, 0:P], W[:, d, cols], S, start=True, stop=True)\
                        .then_inc(PE.did(f"ws{c}_{d}"), 1)
                    if (c, d) == (0, 0):
                        pe.wait_ge(V.sem, V.at("on", h - 1))
                    nc.tensor.matmul(k.bank[2][:, cols], S, g["qe"][:, d, cols], start=((c, d) == (0, 0)), stop=True,
                                     skip_group_check=True)
                    if d == 1 and c < 4 and fills[c]:
                        fill(3, zk, fills[c]) if zk + fills[c] < KC else None
                    pe.wait_ge(V.sem, V.at(f"vn{c}_{d}", h))
                    nc.tensor.matmul(k.bank[2][:, cols], g["vn"][part, d], KQ[part, d, tile, r:r + CHUNK],
                                     start=False, stop=True, skip_group_check=True).then_inc(PE.did(f"o{c}_{d}"), 1)
                    if c < NCH - 1:
                        nc.tensor.matmul(k.bank[5 + d][:, 0:P], g["kd"][part, d, tile], g["vn"][part, d],
                                         start=True, stop=True).then_inc(PE.did(f"up{c}_{d}"), 1)
                    if d == 1 and c < 4:
                        zk += fills[c]
                        if (c, d) == (3, 1):
                            fill(3, 6, 2)
                pe.wait_ge(SC.sem, SC.at("osq", h))
                nc.tensor.matmul(k.bank[7][:], k.c("ones"), g["sq"][:, 0], start=True, stop=True).then_inc(PE.did("on"), 1)

        @block.scalar
        def _(act):
            act.sem_inc(SC.sem, SC.n)
            with act.Fori(0, HEADS) as h:
                act.wait_ge(V.sem, V.at("og", h - 1))
                act.wait_ge(PE.sem, PE.at("on", h - 1))
                for n, (dst, src) in {"q": (g["q"], g["conv"][0]), "k": (g["k"], g["conv"][1]), "v": (g["v"], g["conv"][2]),
                                      "z": (g["z"], g["zraw"])}.items():
                    nc.scalar.activation(dst[:], src[:], ACT.Silu).then_inc(SC.did(f"silu_{n}"), 1)
                act.wait_ge(SC.sem, SC.at("silu_k", h))
                nc.scalar.activation(g["sq"][:, 0], g["q"][:], ACT.Square).then_inc(SC.did("sq_q"), 1)
                nc.scalar.activation(g["sq"][:, 1], g["k"][:], ACT.Square).then_inc(SC.did("sq_k"), 1)
                for n, b in (("q", 0), ("k", 1)):
                    act.wait_ge(PE.sem, PE.at(f"n{n}", h))
                    nc.scalar.activation(g["sq"][:, b], k.bank[3 + b][:], ACT.Ln, bias=g["eps"][:, 0:1])\
                        .then_inc(SC.did(f"ln_{n}"), 1)
                    act.wait_ge(SC.sem, SC.at(f"ln_{n}", h))
                    nc.scalar.activation(g["sq"][:, b], g["sq"][:, b], ACT.Exp, bias=g["eps"][:, 1 + b:2 + b], scale=-0.5)\
                        .then_inc(SC.did(f"rs_{n}"), 1)
                for d in DIR:
                    act.wait_ge(V.sem, V.at(f"tmp{d}", h))
                    for t in range(NT):
                        nc.scalar.activation(E[:, d, t], E[:, d, t], ACT.Exp, bias=g["hcols"][:, 3, d, t:t + 1])\
                            .then_inc(SC.did(f"E{d}_{t}"), 1)
                act.wait_ge(PE.sem, PE.at("trk", h))
                nc.scalar.activation(g["ktok"][:].rearrange("p t d -> p (t d)"), k.bank[7][:], ACT.Copy).then_inc(SC.did("ktok"), 1)
                act.wait_ge(PE.sem, PE.at("trv", h))
                nc.scalar.activation(g["vtok"][:].rearrange("p t d -> p (t d)"), k.bank[3][:], ACT.Copy).then_inc(SC.did("vtok"), 1)
                act.wait_ge(PE.sem, PE.at("pr_q", h))
                evacuate_piece(k, g, 0).then_inc(SC.did("ev_q"), 1)

                def flat(t, d):
                    return t[:, d].rearrange("p t i -> p (t i)")

                act.wait_ge(V.sem, V.at("aT1", h))
                for d in DIR:
                    act.wait_ge(PE.sem, PE.at(f"x0_{d}", h))
                    nc.scalar.activation(flat(X, d), k.bank[3 + d][:], ACT.Copy).then_inc(SC.did(f"x0_{d}"), 1)
                for l in L:
                    for d in DIR:
                        act.wait_ge(PE.sem, PE.at(f"Z{l}_{d}", h))
                        nc.scalar.activation(flat(Z, d), k.bank[3 + d][:], ACT.Copy).then_inc(SC.did(f"Z{l}_{d}"), 1)
                    if l < last_level:
                        for d in DIR:
                            act.wait_ge(PE.sem, PE.at(f"T{l}_{d}", h))
                            nc.scalar.activation(flat(XT, d), k.bank[3 + d][:], ACT.Copy).then_inc(SC.did(f"T{l}_{d}"), 1)
                    if l == 3:
                        act.wait_ge(PE.sem, PE.at("pr_k", h))
                        evacuate_piece(k, g, 1).then_inc(SC.did("ev_k"), 1)
                act.wait_ge(G.sem, G.at(f"As{last_level}_1", h))
                for d in DIR:
                    act.wait_ge(PE.sem, PE.at(f"u{d}", h))
                    nc.scalar.activation(flat(U, d), k.bank[3 + d][:], ACT.Copy).then_inc(SC.did(f"u{d}"), 1)
                    act.wait_ge(PE.sem, PE.at(f"w{d}", h))
                    nc.scalar.activation(W[:, d], k.bank[5 + d][:], ACT.Copy).then_inc(SC.did(f"w{d}"), 1)
                for p in (2, 3):
                    act.wait_ge(PE.sem, PE.at(f"pr_{PIECES[p]}", h))
                    evacuate_piece(k, g, p).then_inc(SC.did(f"ev_{PIECES[p]}"), 1)
                act.wait_ge(PE.sem, PE.at(f"o{NCH - 1}_1", h))
                nc.scalar.activation(g["sq"][:, 0], k.bank[2][:], ACT.Square).then_inc(SC.did("osq"), 1)
                act.wait_ge(PE.sem, PE.at("on", h))
                nc.scalar.activation(g["sq"][:, 1], k.bank[7][:], ACT.Ln, bias=g["eps"][:, 0:1], scale=1.0 / P)\
                    .then_inc(SC.did("ln_o"), 1)
                act.wait_ge(SC.sem, SC.at("ln_o", h))
                nc.scalar.activation(g["sq"][:, 1], g["sq"][:, 1], ACT.Exp, scale=-0.5).then_inc(SC.did("rs_o"), 1)

        @block.vector
        def _(dve):
            dve.sem_inc(V.sem, V.n)
            with dve.Fori(0, HEADS) as h:
                dve.wait_ge(G.sem, G.at("kd1", h - 1))
                dve.wait_ge(SC.sem, SC.at("E1_3", h - 1))
                nc.vector.tensor_copy(g["hcols"][:].rearrange("p a b c -> p (a b c)"),
                                      g["cols"][:].rearrange("p h a b c -> p (h a b c)")[:, bass.ds(h * 8 * NT, 8 * NT)])\
                    .then_inc(V.did("cols"), 1)
                nc.vector.tensor_copy(g["taps"][:], k.p("conv")[:, bass.ds((h + 1) * 3 * TAPS, 3 * TAPS)])\
                    .then_inc(V.did("taps"), 1)
                for d in DIR:
                    nc.vector.memset(g["S"][:, d], 0.0).then_inc(V.did(f"S{d}"), 1)
                dve.wait_ge(rows_in, (h + 1) * 16)
                for d in DIR:
                    nc.vector.tensor_tensor(E[:, d], g["rows"][:, d, 0].rearrange("p (t i) -> p t i", t=NT),
                                            spread(k.c("neg")[:, d * P:(d + 1) * P], 1, NT), ALU.add)\
                        .then_inc(V.did(f"tmp{d}"), 1)
                for d in DIR:
                    a = last_of(d, 0)
                    nc.vector.tensor_copy(g["elast"][:, d], g["rows"][:, d, 2, a:a + (NCH - 1) * CHUNK + 1:CHUNK])\
                        .then_inc(V.did(f"last{d}"), 1)
                for n, b in (("q", 0), ("k", 1)):
                    dve.wait_ge(SC.sem, SC.at(f"rs_{n}", h))
                    nc.vector.tensor_tensor(g[n][:], g[n][:], g["sq"][:, b], ALU.mult).then_inc(V.did(f"{n}n"), 1)
                dve.wait_ge(V.sem, V.at("qn", h))
                for d in DIR:
                    nc.vector.tensor_tensor(g["qe"][:, d], g["q"][:], g["rows"][:, d, 2], ALU.mult).then_inc(V.did(f"qe{d}"), 1)
                for d in DIR:
                    dve.wait_ge(SC.sem, SC.at(f"E{d}_3", h))
                    nc.vector.tensor_tensor(B[:, d].rearrange("p t i -> p (t i)"), E[:, d].rearrange("p t i -> p (t i)"),
                                            g["rows"][:, d, 1], ALU.mult).then_inc(V.did(f"B{d}"), 1)
                for d in DIR:
                    dve.wait_ge(PE.sem, PE.at("kk", h))
                    dve.wait_ge(V.sem, V.at(f"B{d}", h))
                    nc.vector.tensor_tensor(A[:, d].rearrange("p t i -> p (t i)"), k.bank[5][:],
                                            B[:, d].rearrange("p t i -> p (t i)"), ALU.mult).then_inc(V.did(f"A{d}"), 1)
                for d in DIR:
                    dve.wait_ge(PE.sem, PE.at("kq", h))
                    nc.vector.tensor_tensor(KQ[:, d].rearrange("p t i -> p (t i)"), k.bank[6][:],
                                            E[:, d].rearrange("p t i -> p (t i)"), ALU.mult).then_inc(V.did(f"aT{d}"), 1)
                for d in DIR:
                    dve.wait_ge(V.sem, V.at(f"A{d}", h))
                    m = k.c("level")[:, d * len(LEVELS) * P:(d * len(LEVELS) + 1) * P]
                    nc.vector.tensor_tensor(B[:, d], A[:, d], spread(m, 1, NT), ALU.mult).then_inc(V.did(f"m{d}"), 1)
                for d in DIR:
                    dve.wait_ge(V.sem, V.at(f"m{d}", h))
                    nc.vector.tensor_tensor(XT[:, d], spread(k.c("ident"), 1, NT), B[:, d], ALU.subtract)\
                        .then_inc(V.did(f"XT{d}"), 1)
                for l in L:
                    for d in DIR:
                        dst = (X if l < last_level else XT)[:, d].rearrange("p t i -> p (t i)")
                        dve.wait_ge(PE.sem, PE.at(f"D{l}_{d}", h))
                        nc.vector.tensor_tensor(dst, dst, k.bank[5 + d][:], ALU.subtract).then_inc(V.did(f"X{l}_{d}"), 1)
                for c, d in rec:
                    ch, tile, r = place(d, c)
                    part = slice(r, r + CHUNK)
                    if c == 0:
                        dve.wait_ge(SC.sem, SC.at(f"w{d}", h))
                    dve.wait_ge(PE.sem, PE.at(f"ws{c}_{d}", h))
                    nc.vector.tensor_tensor(g["vn"][part, d], U[part, d, tile], k.bank[3 + d][part, 0:P], ALU.subtract)\
                        .then_inc(V.did(f"vn{c}_{d}"), 1)
                    if c < NCH - 1:
                        dve.wait_ge(PE.sem, PE.at(f"up{c}_{d}", h))
                        nc.vector.scalar_tensor_tensor(out=g["S"][:, d], in0=g["S"][:, d], scalar=g["elast"][:, d, ch:ch + 1],
                                                       in1=k.bank[5 + d][:, 0:P], op0=ALU.mult, op1=ALU.add)\
                            .then_inc(V.did(f"S{c}_{d}"), 1)
                    if d == 1 and 1 <= c <= 3:
                        p = c - 1
                        dve.wait_ge(SC.sem, SC.at(f"ev_{PIECES[p]}", h))
                        for tap in range(TAPS):
                            if tap:
                                dve.wait_ge(V.sem, V.at(f"c{p}_{tap - 1}", h))
                            conv_tap(k, g, p, tap).then_inc(V.did(f"c{p}_{tap}"), 1)
                dve.wait_ge(SC.sem, SC.at("rs_o", h))
                nc.vector.tensor_tensor(g["sq"][:, 0], k.bank[2][:], g["sq"][:, 1], ALU.mult).then_inc(V.did("on"), 1)
                dve.wait_ge(V.sem, V.at("on", h))
                nc.vector.scalar_tensor_tensor(out=g["oz"][:].rearrange("p h t -> p (h t)")[:, bass.ds(h * T, T)],
                                               in0=g["sq"][:, 0], scalar=k.p("gdn_gain"), in1=g["z"][:],
                                               op0=ALU.mult, op1=ALU.mult).then_inc(V.did("og"), 1)


def stage_mix_out(k, g, w_out, layer, gate, t0):
    nc, ar = k.nc, k.arena(g["w_at"])
    n = T - t0
    halves = [(0, 0, N_CTX), (1, N_CTX, T)] if t0 == 0 else [(1, 0, n)]
    w = ar("w_out", [P, HEADS, D])
    landed = [k.sem(f"w_out{m}") for m in range(2)]
    product, added = k.sem("out_product"), k.sem("out_added")
    src = w_out.rearrange("(k p) n -> p k n", p=P)
    with nc.Block() as block:
        @block.sync
        def _(sp):
            for m in range(2):
                s = slice(m * D // 2, (m + 1) * D // 2)
                nc.sync.dma_start(w[:, :, s], src[:, :, s]).then_inc(landed[m], 16)

        @block.tensor
        def _(pe):
            for m in range(KC):
                if m % 4 == 0:
                    pe.wait_ge(landed[m // 4], 16)
                for h in range(HEADS):
                    last = nc.tensor.matmul(k.bank[m][:, 0:n], w[:, h, m * P:(m + 1) * P], g["oz"][:, h, 0:n],
                                            start=(h == 0), stop=(h == HEADS - 1))
                last.then_inc(product, 1)

        @block.vector
        def _(dve):
            for m in range(KC):
                dve.wait_ge(product, m + 1)
                for c, a, b in halves:
                    x = k.xT[:, m, t0 + a:t0 + b]
                    nc.vector.scalar_tensor_tensor(out=x, in0=k.bank[m][:, a:b], scalar=k.mod[:, layer, gate * KC + m, c:c + 1],
                                                   in1=x, op0=ALU.mult, op1=ALU.add).then_inc(added, 1)
            dve.wait_ge(added, KC * len(halves))


def stage_route(k, layer, hT, t0, r):
    nt = (T - t0) // P
    nc, ar = k.nc, k.arena(r["tmp_at"])
    R = GROUPS + EXPERTS
    n_pairs_max = (EXPERTS + 2 * nt * P // CAP) // 2
    n_over = MAX_BLOCKS - EXPERTS
    w_r = ar("w_r", [P, KC, R])
    lg = ar("logits", [P, nt, R])
    gmax, gsum, pg, m1, m2, ed, den = (ar(f"c{i}", [P, nt, 1]) for i in range(7))
    g4, goh = ar("g4", [P, nt, GROUPS]), ar("goh", [P, nt, GROUPS])
    em, eq, mem = (ar(f"e{i}", [P, nt, EXPERTS]) for i in range(3))
    oh = ar("oh", [P, 2, nt, EXPERTS])
    rank, quo, blk, slot_e = (ar(f"r{i}", [P, nt, EXPERTS]) for i in range(4))
    cnt, nov, ovend, ovoff, tmp = (ar(f"n{i}", [P, EXPERTS]) for i in range(5))
    zero32 = ar("zero32", [P, EXPERTS])
    cmp_over = ar("cmp_over", [P, n_over, EXPERTS])
    table = ar("table", [P, MAX_BLOCKS])
    slot = ar("slot", [P, 2 * nt])
    cmp_pair = ar("cmp_pair", [P, 2 * nt, MAX_PAIRS - 1])
    pair, inpair = ar("pair", [P, 2 * nt]), ar("inpair", [P, 2 * nt])
    rsel = ar("rsel", [P, 2 * nt, P])
    psel = ar("psel", [P, 2 * nt, MAX_PAIRS])
    rows = ar("rows", [P, nt, D])
    landed, stored = k.sem("w_router"), k.sem("h_stored")
    logits_done, ranked, slots_done, exps = k.sem("logits"), k.sem("ranked"), k.sem("slot_tokens"), k.sem("route_exp")
    onehots, selects, exp_in, finished = k.sem("onehots"), k.sem("selects"), k.sem("exp_in"), k.sem("route_done")
    turned, moved = k.sem("h_turned"), k.sem("h_moved")
    link = k.links("route_link")
    tiles = [(kc, h) for h in range(nt // 2) for kc in range(KC)]

    with k.nc.Block() as block:
        @block.sync
        def _(sp):
            nc.sync.dma_start(w_r[:, :, 0:GROUPS], k.ins["moe_w_group"][layer].rearrange("(k p) n -> p k n", p=P)).then_inc(landed, 16)
            nc.sync.dma_start(w_r[:, :, GROUPS:R], k.ins["moe_w_expert"][layer].rearrange("(k p) n -> p k n", p=P)).then_inc(landed, 16)
            for t in range(nt):
                sp.wait_ge(moved, 2 * (t + 1))
                nc.sync.dma_start(k.h_dram[t * P:(t + 1) * P, :], rows[:, t, :]).then_inc(stored, 16)
            sp.wait_ge(stored, 16 * nt)

        @block.tensor
        def _(pe):
            pe.wait_ge(landed, 32)
            for t in range(nt):
                for kc in range(KC):
                    last = nc.tensor.matmul(k.bank[0][:, t * R:(t + 1) * R], hT[:, kc, t * P:(t + 1) * P], w_r[:, kc, :],
                                            start=(kc == 0), stop=(kc == KC - 1))
            last.then_inc(logits_done, 1)
            for t in range(nt):
                for half in range(2):
                    if t >= 1:
                        pe.wait_ge(moved, 2 * (t - 1) + half + 1)
                    for j in range(4):
                        kc = half * 4 + j
                        last = nc.tensor.transpose(k.bank[4 + half][:, j * P:(j + 1) * P], hT[:, kc, t * P:(t + 1) * P],
                                                   k.c("ident"))
                    last.then_inc(turned, 1)
            pe.wait_ge(onehots, 1)
            for t in range(nt):
                for e in range(t + 1):
                    last = nc.tensor.matmul(k.bank[1][:, t * EXPERTS:(t + 1) * EXPERTS],
                                            k.c("before") if e == t else k.c("ones"), mem[:, e, :],
                                            start=(e == 0), stop=(e == t))
            for e in range(nt):
                last = nc.tensor.matmul(k.bank[2][:, 0:EXPERTS], k.c("ones"), mem[:, e, :],
                                        start=(e == 0), stop=(e == nt - 1))
            last.then_inc(ranked, 1)
            pe.wait_ge(selects, 1)
            for a in range(2 * nt):
                last = nc.tensor.matmul(k.bank[3][:, 0:MAX_PAIRS], rsel[:, a, :], psel[:, a, :],
                                        start=(a == 0), stop=(a == 2 * nt - 1))
            last.then_inc(slots_done, 1)

        @block.scalar
        def _(act):
            for n in range(2 * nt):
                act.wait_ge(turned, n + 1)
                nc.scalar.activation(rows[:, n // 2, (n % 2) * 512:(n % 2 + 1) * 512], k.bank[4 + n % 2][:], ACT.Copy)\
                    .then_inc(moved, 1)
            act.wait_ge(exp_in, 1)
            nc.scalar.activation(g4[:], g4[:], ACT.Exp).then_inc(exps, 1)
            act.wait_ge(exp_in, 2)
            nc.scalar.activation(ed[:], ed[:], ACT.Exp).then_inc(exps, 1)

        @block.vector
        def _(dve):
            v = nc.vector

            def first_max(dst, src, m, desc, width):
                link(dve, v.tensor_reduce(m[:], src, AX.X, ALU.max))
                link(dve, v.tensor_tensor(eq[:, :, 0:width], src, m[:].broadcast_to([P, nt, width]), ALU.is_ge))
                link(dve, v.tensor_tensor(eq[:, :, 0:width], eq[:, :, 0:width], spread(desc, 1, nt), ALU.mult))
                link(dve, v.tensor_reduce(den[:], eq[:, :, 0:width], AX.X, ALU.max))
                link(dve, v.tensor_tensor(dst, eq[:, :, 0:width], den[:].broadcast_to([P, nt, width]), ALU.is_equal))

            dve.wait_ge(logits_done, 1)
            a = PARAM["rbias"][0] + layer * R
            link(dve, v.tensor_tensor(lg[:], k.bank[0][:, 0:nt * R].rearrange("p (t r) -> p t r", t=nt),
                                      spread(k.par[:, a:a + R], 1, nt), ALU.add))
            first_max(goh[:], lg[:, :, 0:GROUPS], gmax, k.c("desc4"), GROUPS)
            v.tensor_tensor(g4[:], lg[:, :, 0:GROUPS], gmax[:].broadcast_to([P, nt, GROUPS]), ALU.subtract).then_inc(exp_in, 1)
            for t in range(nt):
                ohx = spread(goh[:, t, :], 2, PER_GROUP)
                link(dve, v.tensor_tensor(em[:, t].rearrange("p (g e) -> p g e", g=GROUPS),
                                          lg[:, t, GROUPS:R].rearrange("p (g e) -> p g e", g=GROUPS), ohx, ALU.mult))
            link(dve, v.tensor_scalar(goh[:], goh[:], -1.0, BIG, ALU.add, ALU.mult))
            for t in range(nt):
                ohx = spread(goh[:, t, :], 2, PER_GROUP)
                e = em[:, t].rearrange("p (g e) -> p g e", g=GROUPS)
                link(dve, v.tensor_tensor(e, e, ohx, ALU.add))
            first_max(oh[:, 0], em[:], m1, k.c("desc32"), EXPERTS)
            link(dve, v.tensor_scalar(eq[:], oh[:, 0], -2.0 * BIG, None, ALU.mult))
            link(dve, v.tensor_tensor(em[:], em[:], eq[:], ALU.add))
            first_max(oh[:, 1], em[:], m2, k.c("desc32"), EXPERTS)
            v.tensor_tensor(mem[:], oh[:, 0], oh[:, 1], ALU.add).then_inc(onehots, 1)
            v.tensor_tensor(ed[:], m2[:], m1[:], ALU.subtract).then_inc(exp_in, 1)
            dve.wait_ge(exps, 2)
            link(dve, v.tensor_reduce(gsum[:], g4[:], AX.X, ALU.add))
            link(dve, v.reciprocal(pg[:], gsum[:]))
            link(dve, v.tensor_scalar(den[:], ed[:], 1.0, None, ALU.add))
            link(dve, v.reciprocal(gsum[:], den[:]))
            link(dve, v.tensor_tensor(r["gate"][:, 0], pg[:], gsum[:], ALU.mult))
            link(dve, v.tensor_tensor(r["gate"][:, 1], r["gate"][:, 0], ed[:], ALU.mult))
            dve.wait_ge(ranked, 1)
            link(dve, v.tensor_copy(rank[:].rearrange("p t e -> p (t e)"), k.bank[1][:, 0:nt * EXPERTS]))
            link(dve, v.tensor_copy(cnt[:], k.bank[2][:, 0:EXPERTS]))
            link(dve, v.memset(nov[:], 0.0))
            link(dve, v.memset(quo[:], 0.0))
            link(dve, v.memset(zero32[:], 0.0))
            for j in range(1, 2 * nt):
                cap = float(CAP * j)
                link(dve, v.tensor_scalar(tmp[:], cnt[:], cap, None, ALU.is_gt))
                link(dve, v.tensor_tensor(nov[:], nov[:], tmp[:], ALU.add))
                link(dve, v.tensor_scalar(eq[:], rank[:], cap, None, ALU.is_ge))
                link(dve, v.tensor_tensor(quo[:], quo[:], eq[:], ALU.add))
            link(dve, v.tensor_copy(ovend[:], nov[:]))
            for s in (1, 2, 4, 8, 16):
                link(dve, v.tensor_copy(tmp[:], ovend[:]))
                link(dve, v.tensor_tensor(ovend[:, s:], tmp[:, s:], tmp[:, 0:EXPERTS - s], ALU.add))
            link(dve, v.tensor_tensor(ovoff[:], ovend[:], nov[:], ALU.subtract))
            link(dve, v.tensor_tensor(ovoff[:], ovoff[:], k.c("eid31"), ALU.add))
            link(dve, v.tensor_tensor(blk[:], quo[:], spread(ovoff[:], 1, nt), ALU.add))
            link(dve, v.tensor_scalar(eq[:], quo[:], 0.5, None, ALU.is_gt))
            link(dve, v.tensor_tensor(blk[:], blk[:], eq[:], ALU.mult))
            link(dve, v.tensor_tensor(blk[:], blk[:], spread(k.c("eid"), 1, nt), ALU.add))
            link(dve, v.tensor_tensor(blk[:], blk[:], quo[:], ALU.subtract))
            link(dve, v.tensor_scalar(slot_e[:], blk[:], float(CAP), None, ALU.mult))
            link(dve, v.tensor_tensor(slot_e[:], slot_e[:], rank[:], ALU.add))
            for c in range(2):
                link(dve, v.tensor_tensor(eq[:], oh[:, c], slot_e[:], ALU.mult))
                link(dve, v.tensor_reduce(slot[:, c * nt:(c + 1) * nt], eq[:], AX.X, ALU.add))
            link(dve, v.tensor_copy(r["slot"][:], slot[:]))
            link(dve, v.tensor_tensor(cmp_pair[:], spread(slot[:], 2, MAX_PAIRS - 1), spread(k.c("pairs"), 1, 2 * nt), ALU.is_ge))
            link(dve, v.tensor_reduce(pair[:], cmp_pair[:], AX.X, ALU.add))
            link(dve, v.tensor_scalar(inpair[:], pair[:], -float(P), None, ALU.mult))
            link(dve, v.tensor_tensor(inpair[:], inpair[:], slot[:], ALU.add))
            link(dve, v.tensor_tensor(rsel[:], spread(inpair[:], 2, P), spread(k.c("iota"), 1, 2 * nt), ALU.is_equal))
            link(dve, v.tensor_tensor(psel[:], spread(pair[:], 2, MAX_PAIRS), spread(k.c("pairid"), 1, 2 * nt), ALU.is_equal))
            for c in range(2):
                for t in range(nt):
                    a = c * nt + t
                    link(dve, v.tensor_tensor(psel[:, a, :], psel[:, a, :],
                                              k.c("tok")[:, t:t + 1].broadcast_to([P, MAX_PAIRS]), ALU.mult))
            v.memset(tmp[:, 0:1], 0.0).then_inc(selects, 1)
            link(dve, v.tensor_copy(table[:, 0:EXPERTS], k.c("eid")))
            link(dve, v.tensor_tensor(cmp_over[:], spread(ovend[:], 1, n_over), spread(k.c("ovid"), 2, EXPERTS), ALU.is_le))
            link(dve, v.tensor_reduce(table[:, EXPERTS:MAX_BLOCKS], cmp_over[:], AX.X, ALU.add))
            link(dve, v.tensor_scalar(table[:], table[:], float(EXPERTS - 1), None, ALU.min))
            link(dve, v.tensor_copy(r["expert"][:], table[0:1, :]))
            link(dve, v.tensor_scalar(cmp_over[:, 0:n_over // 2, 0], k.c("ovid")[:, 0:n_over:2], ovend[:, EXPERTS - 1:EXPERTS], None,
                                      ALU.is_lt))
            link(dve, v.tensor_reduce(tmp[:, 0:1], cmp_over[:, 0:n_over // 2, 0], AX.X, ALU.add))
            link(dve, v.tensor_scalar(tmp[:, 0:1], tmp[:, 0:1], float(EXPERTS // 2), None, ALU.add))
            link(dve, v.tensor_copy(r["pairs"][:], tmp[0:1, 0:1]))
            dve.wait_ge(slots_done, 1)
            v.tensor_copy(r["token"][:], k.bank[3][:, 0:MAX_PAIRS]).then_inc(finished, 1)
            dve.wait_ge(finished, 1)


def stage_experts(k, layer, r, ring_at):
    nc, ar = k.nc, k.arena(ring_at)
    w1, w3 = ([ar(f"w{n}_{j}", [P, KC, FF]) for j in range(2)] for n in (1, 3))
    w2 = [ar(f"w2_{j}", [P, FC, D]) for j in range(2)]
    ar = k.arena(r["tmp_at"])
    xg, y = ar("xg", [P, D]), ar("y", [P, D])
    xgT = ar("xgT", [P, KC, P])
    gate = ar("act", [P, 2, FC * CAP])
    hid = ar("hid", [P, 2, FC * CAP])
    yT = ar("yT", [P, KC, P])
    W1, W3, W2 = (k.ins[n][layer] for n in ("moe_w1", "moe_w3", "moe_w2"))
    ins = [[k.sem(f"in_w{n}_{j}") for j in range(2)] for n in (1, 3, 2)]
    gathered, closing = k.sem("gathered"), k.sem("closing")
    PE = Steps(k.sem("moe_pe"), ["xt0", "xt1", "a0", "b0", "a1", "b1", "c0", "c1", "yt0", "yt1"])
    SC = Steps(k.sem("moe_act"), ["xt0", "g0", "g1", "yt0"])
    V = Steps(k.sem("moe_dve"), ["xt1", "h0", "h1", "y0", "y1", "yt1"])
    SP = Steps(k.sem("moe_store"), ["y"])

    def loads(eng, expert, j):
        e = bass.ds(expert, 1)
        eng.dma_start(w1[j][:], W1[e].rearrange("o (k p) f -> p (o k) f", p=P)).then_inc(ins[0][j], 16)
        eng.dma_start(w3[j][:], W3[e].rearrange("o (k p) f -> p (o k) f", p=P)).then_inc(ins[1][j], 16)
        eng.dma_start(w2[j][:], W2[e].rearrange("o (k p) f -> p (o k) f", p=P)).then_inc(ins[2][j], 16)

    def pairs_of(eng):
        return eng.value_load(r["pairs"][0:1, 0:1], min_val=EXPERTS // 2, max_val=MAX_PAIRS)

    with nc.Block() as block:
        @block.sync
        def _(sp):
            for j in range(2):
                loads(nc.sync, j, j)
            n = pairs_of(sp)
            with sp.Fori(1, n) as q:
                for j in range(2):
                    e = sp.value_load(r["expert"][0:1, bass.ds(q * 2 + j, 1)], min_val=0, max_val=EXPERTS - 1)
                    sp.wait_ge(PE.sem, PE.at(f"b{j}", q - 1))
                    es = bass.ds(e, 1)
                    nc.sync.dma_start(w1[j][:], W1[es].rearrange("o (k p) f -> p (o k) f", p=P)).then_inc(ins[0][j], 16)
                    nc.sync.dma_start(w3[j][:], W3[es].rearrange("o (k p) f -> p (o k) f", p=P)).then_inc(ins[1][j], 16)
                    sp.wait_ge(PE.sem, PE.at(f"c{j}", q - 1))
                    nc.sync.dma_start(w2[j][:], W2[es].rearrange("o (k p) f -> p (o k) f", p=P)).then_inc(ins[2][j], 16)

        @block.gpsimd
        def _(pool):
            n = pairs_of(pool)
            with pool.Fori(0, n) as q:
                if True:
                    pool.wait_ge(PE.sem, PE.at("xt1", q - 1))
                nc.gpsimd.tensor_copy(r["index"][:], r["token"][:, bass.ds(q, 1)]).then_inc(r["index_sem"], 1)
                pool.wait_ge(r["index_sem"], q + 1)
                nc.gpsimd.tensor_tensor(r["idle"][:], k.cst[:, 0:1], k.cst[:, 1:2], ALU.add)
                nc.gpsimd.indirect_dma_start(out=xg[:], out_offset=None, in_=k.h_dram[:, :],
                                             in_offset=bass.IndirectOffsetOnAxis(ap=r["index"][:, 0:1], axis=0))\
                    .then_inc(gathered, 16)

        @block.tensor
        def _(pe):
            n = pairs_of(pe)
            pe.sem_inc(PE.sem, PE.n)
            with pe.Fori(0, n) as q:
                pe.wait_ge(gathered, (q + 1) * 16)
                for half in range(2):
                    if half == 0:
                        pe.wait_ge(SC.sem, SC.at("yt0", q - 1))
                    else:
                        pe.wait_ge(V.sem, V.at("yt1", q - 1))
                    for j in range(4):
                        kc = half * 4 + j
                        last = nc.tensor.transpose(k.bank[half][:, j * P:(j + 1) * P], xg[:, kc * P:(kc + 1) * P], k.c("ident"))
                    last.then_inc(PE.did(f"xt{half}"), 1)
                pe.wait_ge(SC.sem, SC.at("xt0", q))
                pe.wait_ge(V.sem, V.at("xt1", q))
                for j in range(2):
                    for n_, w in (("a", w1), ("b", w3)):
                        bank = k.bank[2 + 2 * j + (n_ == "b")]
                        pe.wait_ge(ins[n_ == "b"][j], (q + 1) * 16)
                        for f in range(FC):
                            for kc in range(KC):
                                last = nc.tensor.matmul(bank[:, f * CAP:(f + 1) * CAP], w[j][:, kc, f * P:(f + 1) * P],
                                                        xgT[:, kc, j * CAP:(j + 1) * CAP], start=(kc == 0), stop=(kc == KC - 1))
                        last.then_inc(PE.did(f"{n_}{j}"), 1)
                for j in range(2):
                    pe.wait_ge(V.sem, V.at(f"h{j}", q))
                    pe.wait_ge(ins[2][j], (q + 1) * 16)
                    for m in range(KC):
                        for f in range(FC):
                            last = nc.tensor.matmul(k.bank[6 + j][:, m * CAP:(m + 1) * CAP], w2[j][:, f, m * P:(m + 1) * P],
                                                    hid[:, j, f * CAP:(f + 1) * CAP], start=(f == 0), stop=(f == FC - 1))
                    last.then_inc(PE.did(f"c{j}"), 1)
                pe.wait_ge(V.sem, V.at("y1", q))
                for half in range(2):
                    for j in range(4):
                        m = half * 4 + j
                        last = nc.tensor.transpose(k.bank[half][:, j * P:(j + 1) * P], yT[:, m, :], k.c("ident"))
                    last.then_inc(PE.did(f"yt{half}"), 1)

        @block.scalar
        def _(act):
            n = pairs_of(act)
            act.sem_inc(SC.sem, SC.n)
            act.sem_inc(SP.sem, 16)
            with act.Fori(0, n) as q:
                act.wait_ge(PE.sem, PE.at("xt0", q))
                act.wait_ge(PE.sem, PE.at("b1", q - 1))
                nc.scalar.activation(xgT[:, 0:4, :].rearrange("p k s -> p (k s)"), k.bank[0][:], ACT.Copy).then_inc(SC.did("xt0"), 1)
                for j in range(2):
                    act.wait_ge(PE.sem, PE.at(f"a{j}", q))
                    act.wait_ge(V.sem, V.at(f"h{j}", q - 1))
                    nc.scalar.activation(gate[:, j], k.bank[2 + 2 * j][:, 0:FC * CAP], ACT.Silu).then_inc(SC.did(f"g{j}"), 1)
                act.wait_ge(PE.sem, PE.at("yt0", q))
                act.wait_ge(SP.sem, (q + 1) * 16)
                nc.scalar.activation(y[:, 0:512], k.bank[0][:], ACT.Copy).then_inc(SC.did("yt0"), 1)
                act.wait_ge(SC.sem, SC.at("yt0", q))
                act.wait_ge(V.sem, V.at("yt1", q))
                nc.scalar.dma_start(k.y_dram[bass.ds(q * P, P), :], y[:]).then_inc(SP.sem, 16)
            act.wait_ge(SP.sem, (n + 1) * 16)
            nc.scalar.activation(r["done"][:], k.cst[:, 0:1], ACT.Copy).then_inc(closing, 1)

        @block.vector
        def _(dve):
            n = pairs_of(dve)
            dve.sem_inc(V.sem, V.n)
            with dve.Fori(0, n) as q:
                dve.wait_ge(PE.sem, PE.at("xt1", q))
                dve.wait_ge(PE.sem, PE.at("b1", q - 1))
                nc.vector.tensor_copy(xgT[:, 4:8, :].rearrange("p k s -> p (k s)"), k.bank[1][:]).then_inc(V.did("xt1"), 1)
                for j in range(2):
                    dve.wait_ge(SC.sem, SC.at(f"g{j}", q))
                    dve.wait_ge(PE.sem, PE.at(f"b{j}", q))
                    dve.wait_ge(PE.sem, PE.at(f"c{j}", q - 1))
                    nc.vector.tensor_tensor(hid[:, j], gate[:, j], k.bank[3 + 2 * j][:, 0:FC * CAP], ALU.mult)\
                        .then_inc(V.did(f"h{j}"), 1)
                for j in range(2):
                    dve.wait_ge(PE.sem, PE.at(f"c{j}", q))
                    dve.wait_ge(PE.sem, PE.at("yt1", q - 1))
                    nc.vector.tensor_copy(yT[:, :, j * CAP:(j + 1) * CAP], k.bank[6 + j][:].rearrange("p (m s) -> p m s", m=KC))\
                        .then_inc(V.did(f"y{j}"), 1)
                dve.wait_ge(PE.sem, PE.at("yt1", q))
                dve.wait_ge(SP.sem, (q + 1) * 16)
                nc.vector.tensor_copy(y[:, 512:1024], k.bank[1][:]).then_inc(V.did("yt1"), 1)


def stage_combine(k, layer, r, t0):
    nc, ar = k.nc, k.arena(r["ring_at"])
    nt = (T - t0) // P
    rows = ar("rows", [P, 2 * nt, D])
    mix = ar("mix", [P, nt, D])
    fetched = [k.sem(f"fetched{a}") for a in range(2 * nt)]
    mixed, turned, added = k.sem("mixed"), k.sem("y_turned"), k.sem("y_added")
    link = k.links("combine_link")
    with nc.Block() as block:
        @block.gpsimd
        def _(pool):
            for t in range(nt):
                for c in range(2):
                    a = c * nt + t
                    nc.gpsimd.indirect_dma_start(out=rows[:, a], out_offset=None, in_=k.y_dram[:, :],
                                                 in_offset=bass.IndirectOffsetOnAxis(ap=r["slot"][:, a:a + 1], axis=0))\
                        .then_inc(fetched[a], 16)

        @block.tensor
        def _(pe):
            for t in range(nt):
                pe.wait_ge(mixed, t + 1)
                for m in range(KC):
                    last = nc.tensor.transpose(k.bank[m][:, t * P:(t + 1) * P], mix[:, t, m * P:(m + 1) * P], k.c("ident"))
            last.then_inc(turned, 1)

        @block.vector
        def _(dve):
            for t in range(nt):
                dve.wait_ge(fetched[t], 16)
                link(dve, nc.vector.tensor_scalar(mix[:, t], rows[:, t], r["gate"][:, 0, t, :], None, ALU.mult))
                dve.wait_ge(fetched[nt + t], 16)
                nc.vector.scalar_tensor_tensor(out=mix[:, t], in0=rows[:, nt + t], scalar=r["gate"][:, 1, t, :],
                                               in1=mix[:, t], op0=ALU.mult, op1=ALU.add).then_inc(mixed, 1)
            dve.wait_ge(turned, 1)
            n = nt * P
            halves = [(0, 0, N_CTX), (1, N_CTX, T)] if t0 == 0 else [(1, 0, n)]
            for m in range(KC):
                for c, a, b in halves:
                    x = k.xT[:, m, t0 + a:t0 + b]
                    nc.vector.scalar_tensor_tensor(out=x, in0=k.bank[m][:, a:b], scalar=k.mod[:, layer, 5 * KC + m, c:c + 1],
                                                   in1=x, op0=ALU.mult, op1=ALU.add).then_inc(added, 1)
            dve.wait_ge(added, KC * len(halves))


def stage_diff(k, g):
    nc = k.nc
    NQ = N_LAT // P
    ar = g["ar"]
    w = [ar(f"w{n}", [P, KC, P]) for n in "qkv"]
    q, qr, kk, t1 = ar("q", [P, N_LAT]), ar("qr", [P, N_LAT]), ar("k", [P, T]), ar("t1", [P, N_LAT])
    kraw, qraw = ar("kraw", [P, T]), ar("qraw", [P, N_LAT])
    v, vraw = ar("v", [P, NT, P]), ar("vraw", [P, NT, P])
    prob = ar("prob", [P, NQ, 2, T])
    aT = ar("aT", [P, NT, N_LAT])
    sq, rs = ar("sq", [P, N_LAT]), ar("rs", [P, N_LAT])
    mx, sm = ar("mx", [P, NQ, 2]), ar("sm", [P, NQ, 2])
    lam = ar("lam", [P, 4])
    lv = ar("lv", [P, 2, DH])
    eps = ar("eps", [P, 1])
    gain = ar("gain", [P, 1])
    t0 = N_CTX
    scale = DH ** -0.5
    w_in = [k.sem(f"dw_{n}") for n in "qkv"]
    W = k.ins["diff_w_qkv"][0].rearrange("(k p) n -> p k n", p=P)
    lam_exp = k.sem("lam_exp")
    lam_in = k.sem("lam_in")
    link = k.links("lam_link")

    PR = ["pr_q", "pr_k", "pr_v"]
    PE = Steps(k.sem("diff_pe"), ["rot_q", "rot_k"] + [f"s{t}_{s}" for t in range(NQ) for s in range(2)] + PR
               + [f"tr{t}" for t in range(NQ)] + ["pv", "on"])
    SC = Steps(k.sem("diff_act"), ["cp_v"] + [f"e{t}_{s}" for t in range(NQ) for s in range(2)]
               + ["ev_q", "ev_k", "ev_v", "tr0", "osq", "ln_o", "rs_o"])
    V = Steps(k.sem("diff_dve"), ["qc", "kc", "kctx", "qs", "q", "ks", "k"]
              + [f"m{t}_{s}" for t in range(NQ) for s in range(2)] + [f"n{t}_{s}" for t in range(NQ) for s in range(2)]
              + [f"{n}{t}" for t in range(NQ) for n in ("r", "l", "p", "a")] + ["tr1", "on"])
    PP = Steps(k.sem("first_pe"), PR)
    FA = k.sem("first_act")

    def project(pe, steps, rnd, bank_free):
        for n in range(3):
            pe.wait_ge(w_in[n], 16 if rnd is None else (rnd + 2) * 16)
            bank_free(n)
            if n < 2:
                rhs = (lambda kc: g["hT"][:, kc, t0:T]) if n == 0 else (lambda kc: g["hT"][:, kc, :])
                width = N_LAT if n == 0 else T
                for kc in range(KC):
                    last = nc.tensor.matmul(k.bank[n][:, 0:width], w[n][:, kc, :], rhs(kc), start=(kc == 0), stop=(kc == KC - 1))
            else:
                for t in range(NT):
                    for kc in range(KC):
                        last = nc.tensor.matmul(k.bank[0][:, t * P:(t + 1) * P], g["hT"][:, kc, t * P:(t + 1) * P],
                                                w[2][:, kc, :], start=(kc == 0), stop=(kc == KC - 1))
            last.then_inc(steps.did(PR[n]), 1)

    def evacuate(n):
        if n == 0:
            return nc.scalar.activation(qraw[:], k.bank[0][:, 0:N_LAT], ACT.Copy)
        if n == 1:
            return nc.scalar.activation(kraw[:], k.bank[1][:], ACT.Copy)
        return nc.scalar.activation(vraw[:].rearrange("p t d -> p (t d)"), k.bank[0][:], ACT.Copy)

    with nc.Block() as block:
        @block.sync
        def _(sp):
            for n in range(3):
                nc.sync.dma_start(w[n][:], W[:, :, n * D:n * D + P]).then_inc(w_in[n], 16)
            for n in range(3):
                sp.wait_ge(PP.sem, PP.at(PR[n]))
                nc.sync.dma_start(w[n][:], W[:, :, n * D + P:n * D + 2 * P]).then_inc(w_in[n], 16)

            def fetch_next(h, head):
                for n in range(3):
                    sp.wait_ge(PE.sem, PE.at(PR[n], h))
                    nc.sync.dma_start(w[n][:], W[:, :, bass.ds(head * P + n * D, P)]).then_inc(w_in[n], 16)

            with sp.Fori(0, HEADS - 2) as h:
                fetch_next(h, h + 2)
            fetch_next(HEADS - 2, HEADS - 1)

        @block.tensor
        def _(pe):
            pe.sem_inc(PE.sem, PE.n)

            def first_free(n):
                if n == 2:
                    pe.wait_ge(FA, 1)
            project(pe, PP, None, first_free)
            with pe.Fori(0, HEADS) as h:
                if True:
                    pe.wait_ge(FA, 3)
                    pe.wait_ge(SC.sem, SC.at("ev_v", h - 1))
                pe.wait_ge(V.sem, V.at("on", h - 1))
                nc.tensor.matmul(k.bank[2][:, 0:N_LAT], k.c("rot"), qraw[:], start=True, stop=True).then_inc(PE.did("rot_q"), 1)
                nc.tensor.matmul(k.bank[7][:, 0:N_LAT], k.c("rot"), kraw[:, t0:T], start=True, stop=True).then_inc(PE.did("rot_k"), 1)
                pe.wait_ge(V.sem, V.at("k", h))
                for t in range(NQ):
                    for s in range(2):
                        rows = slice(s * DH, (s + 1) * DH)
                        nc.tensor.matmul(k.bank[3 + 2 * t + s][:], qr[rows, t * P:(t + 1) * P], kk[rows, :], start=True, stop=True)\
                            .then_inc(PE.did(f"s{t}_{s}"), 1)

                def bank_free(n):
                    if n == 2:
                        pe.wait_ge(SC.sem, SC.at("ev_q", h))
                project(pe, PE, h, bank_free)
                for t in range(NQ):
                    pe.wait_ge(V.sem, V.at(f"a{t}", h))
                    for c in range(NT):
                        last = nc.tensor.transpose(k.bank[3 + t][:, c * P:(c + 1) * P], prob[:, t, 0, c * P:(c + 1) * P], k.c("ident"))
                    last.then_inc(PE.did(f"tr{t}"), 1)
                pe.wait_ge(SC.sem, SC.at("tr0", h))
                pe.wait_ge(V.sem, V.at("tr1", h))
                for c in range(NT):
                    last = nc.tensor.matmul(k.bank[7][:, 0:N_LAT], v[:, c, :], aT[:, c, :], start=(c == 0), stop=(c == NT - 1))
                last.then_inc(PE.did("pv"), 1)
                pe.wait_ge(SC.sem, SC.at("osq", h))
                nc.tensor.matmul(k.bank[2][:, 0:N_LAT], k.c("ones"), sq[:], start=True, stop=True).then_inc(PE.did("on"), 1)

        @block.scalar
        def _(act):
            act.sem_inc(SC.sem, SC.n)
            act.wait_ge(lam_in, 1)
            nc.scalar.activation(lam[:, 0:2], lam[:, 2:4], ACT.Exp).then_inc(lam_exp, 1)
            for n in range(3):
                act.wait_ge(PP.sem, PP.at(PR[n]))
                evacuate(n).then_inc(FA, 1)
            act.wait_ge(FA, 3)
            with act.Fori(0, HEADS) as h:
                act.wait_ge(PE.sem, PE.at("pv", h - 1))
                act.wait_ge(SC.sem, SC.at("rs_o", h - 1))
                nc.scalar.activation(v[:].rearrange("p t d -> p (t d)"), vraw[:].rearrange("p t d -> p (t d)"), ACT.Copy)\
                    .then_inc(SC.did("cp_v"), 1)
                for t in range(NQ):
                    for s in range(2):
                        act.wait_ge(V.sem, V.at(f"n{t}_{s}", h))
                        nc.scalar.activation(prob[:, t, s], k.bank[3 + 2 * t + s][:], ACT.Exp, bias=mx[:, t, s:s + 1], scale=scale,
                                             accum_out=sm[:, t, s:s + 1]).then_inc(SC.did(f"e{t}_{s}"), 1)
                for n in range(3):
                    act.wait_ge(PE.sem, PE.at(PR[n], h))
                    if n == 0:
                        act.wait_ge(V.sem, V.at("k", h))
                    evacuate(n).then_inc(SC.did(f"ev_{'qkv'[n]}"), 1)
                act.wait_ge(PE.sem, PE.at("tr0", h))
                nc.scalar.activation(aT[:, :, 0:P], k.bank[3][:].rearrange("p (c q) -> p c q", c=NT), ACT.Copy).then_inc(SC.did("tr0"), 1)
                act.wait_ge(PE.sem, PE.at("pv", h))
                nc.scalar.activation(sq[:], k.bank[7][:, 0:N_LAT], ACT.Square).then_inc(SC.did("osq"), 1)
                act.wait_ge(PE.sem, PE.at("on", h))
                nc.scalar.activation(rs[:], k.bank[2][:, 0:N_LAT], ACT.Ln, bias=eps[:], scale=1.0 / P).then_inc(SC.did("ln_o"), 1)
                act.wait_ge(SC.sem, SC.at("ln_o", h))
                nc.scalar.activation(rs[:], rs[:], ACT.Exp, scale=-0.5).then_inc(SC.did("rs_o"), 1)

        @block.vector
        def _(dve):
            vec = nc.vector
            dve.sem_inc(V.sem, V.n)
            link(dve, vec.memset(eps[:], SUBLN_EPS))
            link(dve, vec.tensor_scalar(gain[:], k.p("diff_gain"), 1.0 - LAM_INIT, None, ALU.mult))
            l4 = k.p("lam").rearrange("p (a b d) -> p a b d", a=2, b=2)
            link(dve, vec.tensor_tensor(lv[:], l4[:, :, 0], l4[:, :, 1], ALU.mult))
            vec.tensor_reduce(lam[:, 2:4], lv[:], AX.X, ALU.add).then_inc(lam_in, 1)
            dve.wait_ge(lam_exp, 1)
            link(dve, vec.tensor_tensor(lam[:, 2:3], lam[:, 0:1], lam[:, 1:2], ALU.subtract))
            link(dve, vec.tensor_scalar(lam[:, 3:4], lam[:, 2:3], LAM_INIT, None, ALU.add))
            with dve.Fori(0, HEADS) as h:
                dve.wait_ge(FA, 3)
                dve.wait_ge(PE.sem, PE.at("rot_k", h))
                dve.wait_ge(PE.sem, PE.at("s1_1", h - 1))
                vec.tensor_tensor(q[:], qraw[:], k.c("cos"), ALU.mult).then_inc(V.did("qc"), 1)
                vec.tensor_tensor(kk[:, t0:T], kraw[:, t0:T], k.c("cos"), ALU.mult).then_inc(V.did("kc"), 1)
                vec.tensor_copy(kk[:, 0:t0], kraw[:, 0:t0]).then_inc(V.did("kctx"), 1)
                vec.tensor_tensor(qr[:], k.bank[2][:, 0:N_LAT], k.c("sin"), ALU.mult).then_inc(V.did("qs"), 1)
                dve.wait_ge(V.sem, V.at("qs", h))
                vec.tensor_tensor(qr[:], qr[:], q[:], ALU.add).then_inc(V.did("q"), 1)
                vec.tensor_tensor(t1[:], k.bank[7][:, 0:N_LAT], k.c("sin"), ALU.mult).then_inc(V.did("ks"), 1)
                dve.wait_ge(V.sem, V.at("ks", h))
                vec.tensor_tensor(kk[:, t0:T], kk[:, t0:T], t1[:], ALU.add).then_inc(V.did("k"), 1)
                for t in range(NQ):
                    for s in range(2):
                        dve.wait_ge(PE.sem, PE.at(f"s{t}_{s}", h))
                        vec.tensor_reduce(mx[:, t, s:s + 1], k.bank[3 + 2 * t + s][:], AX.X, ALU.max).then_inc(V.did(f"m{t}_{s}"), 1)
                for t in range(NQ):
                    for s in range(2):
                        dve.wait_ge(V.sem, V.at(f"m{t}_{s}", h))
                        vec.tensor_scalar(mx[:, t, s:s + 1], mx[:, t, s:s + 1], -scale, None, ALU.mult).then_inc(V.did(f"n{t}_{s}"), 1)
                for t in range(NQ):
                    dve.wait_ge(SC.sem, SC.at(f"e{t}_1", h))
                    vec.reciprocal(sm[:, t, :], sm[:, t, :]).then_inc(V.did(f"r{t}"), 1)
                    dve.wait_ge(V.sem, V.at(f"r{t}", h))
                    vec.tensor_scalar(sm[:, t, 1:2], sm[:, t, 1:2], lam[:, 3:4], None, ALU.mult).then_inc(V.did(f"l{t}"), 1)
                    dve.wait_ge(V.sem, V.at(f"l{t}", h))
                    vec.tensor_scalar(prob[:, t, 1], prob[:, t, 1], sm[:, t, 1:2], None, ALU.mult).then_inc(V.did(f"p{t}"), 1)
                    dve.wait_ge(V.sem, V.at(f"p{t}", h))
                    vec.scalar_tensor_tensor(out=prob[:, t, 0], in0=prob[:, t, 0], scalar=sm[:, t, 0:1], in1=prob[:, t, 1],
                                             op0=ALU.mult, op1=ALU.subtract).then_inc(V.did(f"a{t}"), 1)
                dve.wait_ge(PE.sem, PE.at("tr1", h))
                vec.tensor_copy(aT[:, :, P:2 * P], k.bank[4][:].rearrange("p (c q) -> p c q", c=NT)).then_inc(V.did("tr1"), 1)
                dve.wait_ge(SC.sem, SC.at("rs_o", h))
                vec.scalar_tensor_tensor(out=g["oz"][:].rearrange("p h t -> p (h t)")[:, bass.ds(h * T, N_LAT)],
                                         in0=k.bank[7][:, 0:N_LAT], scalar=gain[:], in1=rs[:], op0=ALU.mult, op1=ALU.mult)\
                    .then_inc(V.did("on"), 1)


def stage_store(k, hT):
    nc, ar = k.nc, k.arena(k.norm_at)
    rows = ar("rows", [P, 2, D])
    turned, moved, stored = k.sem("out_turned"), k.sem("out_moved"), k.sem("out_stored")
    with nc.Block() as block:
        @block.tensor
        def _(pe):
            for t in range(2):
                for half in range(2):
                    for j in range(4):
                        kc = half * 4 + j
                        last = nc.tensor.transpose(k.bank[2 * t + half][:, j * P:(j + 1) * P], hT[:, kc, t * P:(t + 1) * P],
                                                   k.c("ident"))
                    last.then_inc(turned, 1)

        @block.vector
        def _(dve):
            for n in range(4):
                dve.wait_ge(turned, n + 1)
                nc.vector.tensor_copy(rows[:, n // 2, (n % 2) * 512:(n % 2 + 1) * 512], k.bank[n][:]).then_inc(moved, 1)

        @block.sync
        def _(sp):
            for t in range(2):
                sp.wait_ge(moved, 2 * (t + 1))
                nc.sync.dma_start(k.out[0, t * P:(t + 1) * P, :], rows[:, t, :]).then_inc(stored, 16)
            sp.wait_ge(stored, 32)


def moe(k, layer, hT, t0, at):
    keep = k.arena(at)
    nt = (T - t0) // P
    r = {"gate": keep("gate", [P, 2, nt, 1]), "slot": keep("slot", [P, 2 * nt], U32), "token": keep("token", [P, MAX_PAIRS], U32),
         "expert": keep("expert", [1, MAX_BLOCKS], U32), "pairs": keep("pairs", [1, 1], U32), "index": keep("index", [P, 1], U32),
         "idle": keep("idle", [P, 1]), "done": keep("done", [P, 1]),
         "index_sem": k.sem("index")}
    r["tmp_at"] = keep.at
    stage_route(k, layer, hT, t0, r)
    r["ring_at"] = k.nc.sbuf_usable_end - 2 * 3 * 16384 - 64
    r["ring_at"] -= r["ring_at"] % 32
    stage_experts(k, layer, r, r["ring_at"])
    stage_combine(k, layer, r, t0)


def hybrid_kernel(nc, ins, out):
    ctx = ExitStack()
    with ctx:
        k = Core(nc, ctx, ins, out)
        k.rows_dram = nc.dram_tensor("gate_rows", [HEADS, 2, 3, T], F32)
        k.h_dram = nc.dram_tensor("h_rows", [T, D], F32)
        k.y_dram = nc.dram_tensor("y_rows", [MAX_BLOCKS * CAP, D], F32)
        k.norm_at = k.free
        stage_load(k)
        stage_mod(k, 0)
        stage_mod(k, 1)

        ar = k.arena()
        g = {"hT": ar("hT", [P, KC, T]), "oz": ar("oz", [P, HEADS, T]), "cols": ar("cols", [P, HEADS, 4, 2, NT])}
        k.norm_at = ar.at
        stage_norm(k, g["hT"], k.p("mix")[:, 0:KC], 0, 0)
        stage_gdn_gates(k, g)
        g["w_at"] = ar.at
        g["w"] = [ar(f"w{p}", [P, KC, P]) for p in PIECES]
        g["pad"] = [ar(f"pad{p}", [P, 2, SEGW]) for p in PIECES[:3]]
        g["conv"] = [ar(f"conv{p}", [P, T]) for p in PIECES[:3]]
        g["zraw"], g["q"], g["k"], g["v"], g["z"] = (ar(n, [P, T]) for n in ("zraw", "q", "k", "v", "z"))
        g["taps"], g["eps"] = ar("taps", [P, 3 * TAPS]), ar("eps", [P, 4])
        g["hcols"] = ar("hcols", [P, 4, 2, NT])
        g["elast"] = ar("elast", [P, 2, NCH])
        g["rows"] = ar("rows", [P, 2, 3, T])
        g["sq"] = ar("sq", [P, 2, T])
        g["qe"], g["W"] = ar("qe", [P, 2, T]), ar("W", [P, 2, T])
        for n in ("E", "B", "KQ", "A", "XT", "vb", "kbe", "kd"):
            g[n] = ar(n, [P, 2, NT, P])
        g["As"] = ar("As", [P, len(LEVELS) - 1, 2, NT, P])
        g["ktok"], g["vtok"] = ar("ktok", [P, NT, P]), ar("vtok", [P, NT, P])
        g["S"], g["vn"] = ar("S", [P, 2, P]), ar("vn", [P, 2, P])
        eps_set = k.sem("eps_set")
        with nc.Block() as block:
            @block.vector
            def _(dve):
                for n, val in enumerate((EPS, math.log(P ** -0.5), 0.0)):
                    nc.vector.memset(g["eps"][:, n:n + 1], val).then_inc(eps_set, 1)
                dve.wait_ge(eps_set, 3)
        stage_gdn_first(k, g)
        stage_gdn_heads(k, g)
        stage_mix_out(k, g, ins["gdn_w_out"][0], 0, 2, 0)

        ar = k.arena()
        hT = ar("hT", [P, KC, T])
        k.norm_at = ar.at
        stage_norm(k, hT, k.p("ffn")[:, 0:KC], 0, 3)
        moe(k, 0, hT, 0, ar.at)

        k.recycle()
        ar = k.arena()
        g = {"hT": ar("hT", [P, KC, T]), "oz": ar("oz", [P, HEADS, T])}
        k.norm_at = ar.at
        stage_norm(k, g["hT"], k.p("mix")[:, KC:2 * KC], 1, 0)
        g["w_at"] = ar.at
        g["ar"] = ar
        stage_diff(k, g)
        stage_mix_out(k, g, ins["diff_w_out"][0], 1, 2, N_CTX)

        ar = k.arena()
        hT = ar("hT", [P, KC, N_LAT])
        k.norm_at = ar.at
        stage_norm(k, hT, k.p("ffn")[:, KC:2 * KC], 1, 3, t0=N_CTX)
        moe(k, 1, hT, N_CTX, ar.at)
        stage_norm(k, hT, k.p("final"), t0=N_CTX)
        stage_store(k, hT)
        k.recycle()


_BIG = ['x', 'ctx', 'w_mod', 'gdn_w_in', 'gdn_w_out', 'diff_w_qkv', 'diff_w_out', 'moe_w_group', 'moe_w_expert',
        'moe_w1', 'moe_w3', 'moe_w2']


def kernel(**inputs):
    import concourse.bacc as bacc
    from concourse.bass_utils import run_bass_kernel_spmd

    arrays = {n: np.ascontiguousarray(inputs[n]) for n in _BIG}
    arrays["constants"] = shape_constants()
    arrays["params"] = packed_params(inputs)
    nc = bacc.Bacc("TRN2", target_bir_lowering=False, num_devices=1)
    feeds, ins = {}, {}
    for name, a in arrays.items():
        feeds[f"in_{name}"] = a
        ins[name] = nc.dram_tensor(f"in_{name}", a.shape, mybir.dt.from_np(a.dtype), kind="ExternalInput").ap()
    out = nc.dram_tensor("out_0", (1, N_LAT, D), F32, kind="ExternalOutput").ap()
    hybrid_kernel(nc, ins, out)
    r = run_bass_kernel_spmd(nc, [feeds], core_ids=[0])
    return r.results[0]["out_0"]
```

```python
import math
from contextlib import ExitStack

import concourse.bass as bass
from concourse import mybir
import numpy as np

P = 128
F32 = mybir.dt.float32
U32 = mybir.dt.uint32
ALU = mybir.AluOpType
ACT = mybir.ActivationFunctionType
AX = mybir.AxisListType

D = 1024
KC = D // P
N_CTX = 256
N_LAT = 256
T = N_CTX + N_LAT
NT = T // P
DEPTH = 2
GRID_W = 64
EPS = 1e-6
SUBLN_EPS = 1e-5
HEADS = 8
CHUNK = 64
NCH = T // CHUNK
TAPS = 5
HALO = TAPS // 2
SEGW = N_CTX + 2 * HALO
GDN_COLS = 4 * D + 4 * HEADS
DH = 64
GROUPS = 4
PER_GROUP = 8
EXPERTS = GROUPS * PER_GROUP
FF = D // 2
FC = FF // P
CAP = P
MAX_ASSIGN = 2 * T
MAX_BLOCKS = EXPERTS + MAX_ASSIGN // CAP
MAX_PAIRS = MAX_BLOCKS // 2
SLOT_COLS = MAX_BLOCKS + 1
TABLE_LN_EXP, TABLE_SILU = 6, 18
LAM_INIT = 0.8 - 0.6 * math.exp(-0.3)
BIG = 1.0e30
LEVELS = (1, 2, 4, 8, 16, 32)


def layout(widths):
    at, out = 0, {}
    for name, width in widths:
        out[name] = (at, at + width)
        at += width
    return out, at


CONST, CONST_W = layout([
    ("ident", P), ("ones", P), ("cum_f", P), ("cum_b", P), ("block", P), ("before", P),
    ("neg", 2 * P), ("level", 2 * len(LEVELS) * P), ("rot", P), ("cos", N_LAT), ("sin", N_LAT),
    ("iota", P), ("desc4", GROUPS), ("desc32", EXPERTS), ("eid", EXPERTS), ("eid31", EXPERTS),
    ("blockid", SLOT_COLS), ("ovid", MAX_BLOCKS - EXPERTS),
    ("tok", NT),
])
PARAM, PARAM_W = layout([
    ("cond", KC * 2), ("bmod", DEPTH * 6 * KC), ("mix", DEPTH * KC), ("ffn", DEPTH * KC),
    ("final", KC), ("conv", HEADS * 3 * TAPS), ("gdn_gain", 1), ("diff_gain", 1),
    ("alog", 2 * HEADS), ("dt", 2 * HEADS), ("lam", 4 * DH), ("rbias", DEPTH * (GROUPS + EXPERTS)),
])


def shape_constants():
    c = np.zeros((P, CONST_W), np.float32)
    row = np.arange(P)[:, None]
    col = np.arange(P)[None, :]
    same = (row // CHUNK) == (col // CHUNK)

    def put(name, v, at=0):
        a = CONST[name][0] + at
        c[:, a:a + v.shape[-1]] = v

    put("ident", (row == col).astype(np.float32))
    put("ones", np.ones((P, P), np.float32))
    put("cum_f", (same & (row <= col)).astype(np.float32))
    put("cum_b", (same & (row >= col)).astype(np.float32))
    put("block", same.astype(np.float32))
    put("before", (row < col).astype(np.float32))
    put("neg", np.where(same & (row <= col), 0.0, -BIG).astype(np.float32))
    put("neg", np.where(same & (row >= col), 0.0, -BIG).astype(np.float32), P)
    for n, s in enumerate(LEVELS):
        pair = (row // (2 * s)) == (col // (2 * s))
        low_r, low_c = (row // s) % 2 == 0, (col // s) % 2 == 0
        put("level", (pair & low_r & ~low_c).astype(np.float32), n * P)
        put("level", (pair & ~low_r & low_c).astype(np.float32), (len(LEVELS) + n) * P)
    quarter = DH // 4
    ch = np.arange(P)
    second = (ch // quarter) % 2 == 1
    rot = np.zeros((P, P), np.float32)
    for o in range(P):
        if second[o]:
            rot[o - quarter, o] = 1.0
        else:
            rot[o + quarter, o] = -1.0
    put("rot", rot)
    freq = (np.float32(10000.0) ** (-np.arange(quarter, dtype=np.float32) / quarter)).astype(np.float32)
    t = np.arange(N_LAT)
    pos = np.stack([(t // GRID_W), (t % GRID_W)]).astype(np.float32)
    axis = (ch // (2 * quarter)) % 2
    ang = pos[axis] * freq[ch % quarter][:, None]
    put("cos", np.cos(ang))
    put("sin", np.sin(ang))
    put("iota", np.broadcast_to(np.arange(P, dtype=np.float32), (P, P)))
    put("desc4", np.broadcast_to(np.arange(GROUPS, 0, -1, dtype=np.float32), (P, GROUPS)))
    put("desc32", np.broadcast_to(np.arange(EXPERTS, 0, -1, dtype=np.float32), (P, EXPERTS)))
    put("eid", np.broadcast_to(np.arange(EXPERTS, dtype=np.float32), (P, EXPERTS)))
    put("eid31", np.broadcast_to(EXPERTS - 1 - np.arange(EXPERTS, dtype=np.float32), (P, EXPERTS)))
    put("blockid", np.broadcast_to(np.arange(SLOT_COLS, dtype=np.float32), (P, SLOT_COLS)))
    put("ovid", np.broadcast_to(np.arange(MAX_BLOCKS - EXPERTS, dtype=np.float32), (P, MAX_BLOCKS - EXPERTS)))
    put("tok", (np.arange(P)[:, None] + P * np.arange(NT)[None, :]).astype(np.float32))
    return c


def packed_params(i):
    v = np.zeros((P, PARAM_W), np.float32)

    def put(name, a, at=0):
        s = PARAM[name][0] + at
        v[:, s:s + a.shape[-1]] = a

    def columns(a):
        return np.asarray(a).reshape(-1, P).T

    for n, a in enumerate((i["c_ctx"], i["c"][0])):
        for k in range(KC):
            put("cond", np.asarray(a)[k * P:(k + 1) * P, None], 2 * k + n)
    for d in range(DEPTH):
        put("bmod", columns(i["b_mod"][d]), d * 6 * KC)
        put("mix", columns(i["norm_mix"][d]), d * KC)
        put("ffn", columns(i["norm_ffn"][d]), d * KC)
        put("rbias", np.broadcast_to(np.asarray(i["moe_b_group"][d])[None], (P, GROUPS)), d * (GROUPS + EXPERTS))
        put("rbias", np.broadcast_to(np.asarray(i["moe_b_expert"][d])[None], (P, EXPERTS)),
            d * (GROUPS + EXPERTS) + GROUPS)
    put("final", columns(i["final_norm"]))
    conv = np.asarray(i["gdn_conv"][0])
    for h in range(HEADS):
        for piece in range(3):
            a = piece * D + h * P
            put("conv", conv[:, a:a + P].T, (h * 3 + piece) * TAPS)
    put("gdn_gain", np.asarray(i["gdn_norm"][0])[:, None])
    put("diff_gain", np.asarray(i["diff_norm"][0])[:, None])
    put("alog", np.broadcast_to(np.asarray(i["gdn_a_log"][0]).reshape(1, -1), (P, 2 * HEADS)))
    put("dt", np.broadcast_to(np.asarray(i["gdn_dt_bias"][0]).reshape(1, -1), (P, 2 * HEADS)))
    put("lam", np.broadcast_to(np.asarray(i["diff_lambda"][0]).reshape(1, -1), (P, 4 * DH)))
    return v


def load_tables(k, table_set):
    nc = k.nc
    nc.scalar.add_instruction(mybir.InstLoadActFuncSet(act_func_set_id=table_set, name=nc.get_next_instruction_name(),
                                                       engine=mybir.EngineType.Activation))


class Steps:

    def __init__(self, sem, names, last_round=None, left_out=()):
        self.sem, self.names, self.next = sem, list(names), 0
        self.last_round, self.last_names = last_round, [n for n in self.names if n not in left_out]

    def did(self, name):
        done = self.next - len(self.names)
        expected = self.names[self.next] if done < 0 else (self.last_names if self.last_round is not None else self.names)[
            done % len(self.last_names if self.last_round is not None else self.names)]
        assert expected == name, (name, expected)
        self.next += 1
        return self.sem

    def at(self, name, rnd=None):
        if isinstance(rnd, int) and rnd == self.last_round:
            return (rnd + 1) * len(self.names) + self.last_names.index(name) + 1
        n = self.names.index(name) + 1
        return n if rnd is None else (rnd + 1) * len(self.names) + n

    @property
    def n(self):
        return len(self.names)


class Arena:

    def __init__(self, nc, at, tag):
        self.nc, self.at, self.tag = nc, at, tag

    def __call__(self, name, shape, dtype=F32):
        size = 4
        for s in shape[1:]:
            size *= s
        t = self.nc.alloc_sbuf_tensor_at(f"{self.tag}_{name}", shape, dtype, offset=self.at)
        self.at += (size + 31) // 32 * 32
        assert self.at <= self.nc.sbuf_usable_end, (self.tag, name, self.at, self.nc.sbuf_usable_end)
        return t


def spread(ap, axis, n):
    v = ap.unsqueeze(axis)
    shape = list(v.shape)
    shape[axis] = n
    return v.broadcast_to(shape)


class Core:

    def __init__(self, nc, ctx, ins, out):
        self.nc, self.ctx, self.ins, self.out, self.sems = nc, ctx, ins, out, 0
        self.bank = [ctx.enter_context(nc.psum_tensor(f"bank{b}", [P, 512], F32)) for b in range(8)]
        keep = Arena(nc, (nc.sbuf_usable_end - nc.sbuf_bytes_remaining + 31) // 32 * 32, "keep")
        self.cst = keep("constants", [P, CONST_W])
        self.par = keep("params", [P, PARAM_W])
        self.xT = keep("xT", [P, KC, T])
        self.cond = keep("cond", [P, KC, 4 * MOD_RING - 2])
        self.mod = keep("mod", [P, DEPTH, 6 * KC, 2])
        self.small = keep("small", [P, 8])
        self.free = keep.at
        self.stage, self.live = 0, []

    def arena(self, at=None):
        self.stage += 1
        return Arena(self.nc, self.free if at is None else at, f"s{self.stage}")

    def sem(self, name):
        self.sems += 1
        self.live.append(self.nc.alloc_semaphore(f"{name}_{self.sems}"))
        return self.live[-1]

    def recycle(self):
        self.nc.clear_and_free_semaphores(self.live)
        self.live = []
        self.nc.all_engine_barrier()

    def c(self, name):
        a, b = CONST[name]
        return self.cst[:, a:b]

    def p(self, name):
        a, b = PARAM[name]
        return self.par[:, a:b]

    def links(self, name):
        sem, count = self.sem(name), [0]

        def link(eng, ins, wait=True):
            count[0] += 1
            ins.then_inc(sem, 1)
            if wait:
                eng.wait_ge(sem, count[0])
        return link


def stage_load(k):
    nc, ar = k.nc, k.arena()
    x_in = ar("x_in", [P, NT, D])
    loaded, x_loaded = k.sem("loaded"), k.sem("x_loaded")
    turned, moved, done = k.sem("turned"), k.sem("moved"), k.sem("silu")
    cond_zero = k.sem("cond_zero")
    mod_ring(k)
    with nc.Block() as block:
        @block.sync
        def _(sp):
            nc.sync.dma_start(k.cst[:], k.ins["constants"]).then_inc(loaded, 16)
            nc.sync.dma_start(k.par[:], k.ins["params"]).then_inc(loaded, 16)
            nc.sync.dma_start(x_in[:, 0:2, :], k.ins["ctx"][0].rearrange("(t p) d -> p t d", p=P)).then_inc(x_loaded, 16)
            nc.sync.dma_start(x_in[:, 2:4, :], k.ins["x"][0].rearrange("(t p) d -> p t d", p=P)).then_inc(x_loaded, 16)
            for r in range(MOD_RING):
                load_mod_strip(k, 0, 0, r)

        @block.tensor
        def _(pe):
            pe.wait_ge(loaded, 32)
            pe.wait_ge(x_loaded, 32)
            for kc in range(KC):
                for t in range(NT):
                    last = nc.tensor.transpose(k.bank[kc][:, t * P:(t + 1) * P], x_in[:, t, kc * P:(kc + 1) * P],
                                               k.c("ident"))
                last.then_inc(turned, 1)

        @block.vector
        def _(dve):
            nc.vector.memset(k.cond[:], 0.0).then_inc(cond_zero, 1)
            for kc in range(KC):
                dve.wait_ge(turned, kc + 1)
                nc.vector.tensor_copy(k.xT[:, kc, :], k.bank[kc][:]).then_inc(moved, 1)
            dve.wait_ge(moved, KC)

        @block.scalar
        def _(act):
            act.wait_ge(loaded, 32)
            act.wait_ge(cond_zero, 1)
            nc.scalar.activation(k.cond[:, :, 2 * MOD_RING - 2:2 * MOD_RING], k.p("cond").rearrange("p (a b) -> p a b", b=2),
                                 ACT.Silu).then_inc(done, 1)
            act.wait_ge(done, 1)


MOD_RING, MOD_STRIP = 4, 512
MOD_ROUNDS = 6 * D // MOD_STRIP // MOD_RING


def mod_ring(k):
    ar = k.arena(k.free + 24 * 1024)
    k.mod_w = [ar(f"w{r}", [P, KC, MOD_STRIP]) for r in range(MOD_RING)]
    k.mod_landed = [k.sem(f"mod_w{r}") for r in range(MOD_RING)]
    k.mod_free = ar.at


def load_mod_strip(k, layer, g, r):
    w = k.ins["w_mod"][layer].rearrange("(k p) n -> p k n", p=P)
    k.nc.sync.dma_start(k.mod_w[r][:], w[:, :, bass.ds((g * MOD_RING + r) * MOD_STRIP, MOD_STRIP)])\
        .then_inc(k.mod_landed[r], 16)


def stage_mod(k):
    nc, ar = k.nc, k.arena(k.mod_free)
    M = 2 * MOD_RING
    per = MOD_STRIP // P
    rows = ar("rows", [M, DEPTH * MOD_ROUNDS * MOD_STRIP])
    pe_s = Steps(k.sem("mod_strip"), [f"strip{r}" for r in range(MOD_RING)])
    moved, turned, added = k.sem("mod_moved"), k.sem("mod_turned"), k.sem("mod_added")
    with nc.Block() as block:
        @block.sync
        def _(sp):
            for layer in range(DEPTH):
                first = 1 if layer == 0 else 0
                with sp.Fori(0, MOD_ROUNDS - first) as g:
                    for r in range(MOD_RING):
                        sp.wait_ge(pe_s.sem, pe_s.at(f"strip{r}", g + first + layer * MOD_ROUNDS - 1))
                        load_mod_strip(k, layer, g + first, r)

        @block.tensor
        def _(pe):
            pe.sem_inc(pe_s.sem, pe_s.n)
            pe.sem_inc(moved, 1)
            for layer in range(DEPTH):
                with pe.Fori(0, MOD_ROUNDS) as g:
                    pe.wait_ge(moved, g + layer * MOD_ROUNDS + 1)
                    for r in range(MOD_RING):
                        pe.wait_ge(k.mod_landed[r], (g + layer * MOD_ROUNDS + 1) * 16)
                        for kc in range(KC):
                            last = nc.tensor.matmul(k.bank[1][0:M, :], k.cond[:, kc, M - 2 - 2 * r:2 * M - 2 - 2 * r],
                                                    k.mod_w[r][:, kc, :], start=(r == 0 and kc == 0),
                                                    stop=(r == MOD_RING - 1 and kc == KC - 1))
                        last.then_inc(pe_s.did(f"strip{r}"), 1)
            pe.wait_ge(moved, DEPTH * MOD_ROUNDS + 1)
            for n in range(DEPTH * MOD_ROUNDS * per):
                last = nc.tensor.transpose(k.bank[0][:, n * M:(n + 1) * M], rows[:, n * P:(n + 1) * P],
                                           k.c("ident")[0:M, 0:M])
            last.then_inc(turned, 1)

        @block.scalar
        def _(act):
            for layer in range(DEPTH):
                with act.Fori(0, MOD_ROUNDS) as g:
                    act.wait_ge(pe_s.sem, pe_s.at(f"strip{MOD_RING - 1}", g + layer * MOD_ROUNDS))
                    nc.scalar.activation(rows[:, bass.ds((g + layer * MOD_ROUNDS) * MOD_STRIP, MOD_STRIP)],
                                         k.bank[1][0:M, :], ACT.Copy).then_inc(moved, 1)

        @block.vector
        def _(dve):
            dve.wait_ge(turned, 1)
            for n in range(DEPTH * MOD_ROUNDS):
                layer, g = n // MOD_ROUNDS, n % MOD_ROUNDS
                a, m = PARAM["bmod"][0] + layer * 6 * KC, MOD_RING * per
                nc.vector.tensor_tensor(
                    k.mod[:, layer, g * m:(g + 1) * m, :].rearrange("p (r q) c -> p r q c", q=per),
                    k.bank[0][:, n * per * M:(n + 1) * per * M].rearrange("p (q r c) -> p r q c", q=per, c=2),
                    spread(k.par[:, a + g * m:a + (g + 1) * m].rearrange("p (r q) -> p r q", q=per), 3, 2),
                    ALU.add).then_inc(added, 1)
            dve.wait_ge(added, DEPTH * MOD_ROUNDS)


def stage_norm(k, dst, gain, layer=None, shift=None, t0=0, eps=EPS, prefetch=None):
    nc, ar = k.nc, k.arena(k.norm_at)
    n = T - t0
    sq = ar("sq", [P, 2, n])
    rstd = ar("rstd", [P, n])
    tmp = ar("tmp", [P, 2, n])
    scale = ar("scale", [P, KC, 2])
    squared, summed, rooted = k.sem("squared"), k.sem("summed"), k.sem("rooted")
    scaled, timed, out = k.sem("scaled"), k.sem("timed"), k.sem("normed")
    epsc = ar("epsc", [P, 1])
    halves = [(0, 0, N_CTX), (1, N_CTX, T)] if t0 == 0 else [(1, 0, n)]
    with nc.Block() as block:
        @block.sync
        def _(sp):
            if prefetch:
                prefetch()

        @block.tensor
        def _(pe):
            for kc in range(KC):
                pe.wait_ge(squared, kc + 1)
                nc.tensor.matmul(k.bank[0][:, 0:n], k.c("ones"), sq[:, kc % 2, :],
                                 start=(kc == 0), stop=(kc == KC - 1)).then_inc(summed, 1)

        @block.scalar
        def _(act):
            load_tables(k, TABLE_LN_EXP)
            for kc in range(KC):
                if kc >= 2:
                    act.wait_ge(summed, kc - 1)
                nc.scalar.activation(sq[:, kc % 2, :], k.xT[:, kc, t0:T], ACT.Square).then_inc(squared, 1)
            act.wait_ge(summed, KC)
            act.wait_ge(scaled, 2 if layer is None else 3)
            nc.scalar.activation(rstd[:], k.bank[0][:, 0:n], ACT.Ln, bias=epsc[:], scale=1.0 / D).then_inc(rooted, 1)
            act.wait_ge(rooted, 1)
            nc.scalar.activation(rstd[:], rstd[:], ACT.Exp, scale=-0.5).then_inc(rooted, 1)
            for kc in range(KC):
                act.wait_ge(timed, kc + 1)
                for c, a, b in halves:
                    bias = 0.0 if layer is None else k.mod[:, layer, shift * KC + kc, c:c + 1]
                    nc.scalar.activation(dst[:, kc, a:b], tmp[:, kc % 2, a:b], ACT.Identity, bias=bias,
                                         scale=scale[:, kc, c:c + 1]).then_inc(out, 1)
            act.wait_ge(out, KC * len(halves))

        @block.vector
        def _(dve):
            nc.vector.memset(epsc[:], eps).then_inc(scaled, 1)
            if layer is None:
                nc.vector.tensor_copy(scale[:], spread(gain, 2, 2)).then_inc(scaled, 1)
                dve.wait_ge(scaled, 2)
            else:
                nc.vector.tensor_scalar(scale[:], k.mod[:, layer, (shift + 1) * KC:(shift + 2) * KC, :], 1.0, None,
                                        ALU.add).then_inc(scaled, 1)
                dve.wait_ge(scaled, 2)
                nc.vector.tensor_tensor(scale[:], scale[:], spread(gain, 2, 2), ALU.mult).then_inc(scaled, 1)
                dve.wait_ge(scaled, 3)
            dve.wait_ge(rooted, 2)
            for kc in range(KC):
                if kc >= 2:
                    dve.wait_ge(out, (kc - 1) * len(halves))
                nc.vector.tensor_tensor(tmp[:, kc % 2, :], k.xT[:, kc, t0:T], rstd[:], ALU.mult).then_inc(timed, 1)


def stage_gdn_gates(k, g):
    nc, ar = k.nc, k.arena(k.norm_at)
    H2 = 2 * HEADS
    ab = ar("ab", [P, NT, 2, 2, HEADS])
    t1, t2, t3, t4 = (ar(f"t{i}", [P, NT, H2]) for i in range(4))
    gdec, beta, gcum, ecum = (ar(f"g{i}", [P, NT, H2]) for i in range(4))
    rows = ar("rows", [H2, 3, T])
    ea = ar("ea", [P, H2])
    one = ar("one", [P, 1])
    stored = k.sem("rows_stored")
    projected, cumulated, rows_turned = k.sem("ab_projected"), k.sem("cumulated"), k.sem("rows_turned")
    inputs_ready, decay_ready, cum_ready, split = (k.sem(n) for n in ("gate_in", "decay_ready", "cum_ready", "ab_split"))
    exps, logs, cum_exps = k.sem("gate_exps"), k.sem("gate_logs"), k.sem("cum_exps")
    rows_ready = k.sem("rows_ready")
    link = k.links("gates_link")
    zeros = ar("zeros", [P, D])
    zeroed, filled = k.sem("zeroed"), k.sem("filled")

    with nc.Block() as block:
        @block.gpsimd
        def _(pool):
            nc.gpsimd.memset(zeros[:], 0.0).then_inc(zeroed, 1)
            pool.wait_ge(zeroed, 1)
            for b in range(EXPERTS, MAX_BLOCKS):
                nc.gpsimd.dma_start(k.y_dram[b * P:(b + 1) * P, :], zeros[:]).then_inc(filled, 16)
            pool.wait_ge(filled, 16 * (MAX_BLOCKS - EXPERTS))

        @block.sync
        def _(sp):
            sp.wait_ge(rows_ready, 3)
            for d in range(2):
                nc.sync.dma_start(k.rows_dram[:, d], rows[d * HEADS:(d + 1) * HEADS]).then_inc(stored, 16)
            sp.wait_ge(stored, 32)

        @block.tensor
        def _(pe):
            pe.wait_ge(g["w_ab_in"], 16)
            for t in range(NT):
                for kc in range(KC):
                    last = nc.tensor.matmul(k.bank[0][:, t * 2 * H2:(t + 1) * 2 * H2], g["hT"][:, kc, t * P:(t + 1) * P],
                                            g["w_ab"][:, kc, :], start=(kc == 0), stop=(kc == KC - 1))
            last.then_inc(projected, 1)
            for p in range(2):
                pe.wait_ge(g["w0_in"][p], 16)
                for kc in range(KC):
                    last = project_piece(k, g, p, kc, k.bank[6 + p])
                last.then_inc(g["first_qk"], 1)
            pe.wait_ge(decay_ready, 1)
            for t in range(NT):
                for d, m in enumerate(("cum_f", "cum_b")):
                    nc.tensor.matmul(k.bank[1][:, t * H2 + d * HEADS:t * H2 + (d + 1) * HEADS], k.c(m),
                                     gdec[:, t, d * HEADS:(d + 1) * HEADS], start=True, stop=True)
                last = nc.tensor.matmul(k.bank[2][:, t * H2:(t + 1) * H2], k.c("block"), gdec[:, t, :],
                                        start=True, stop=True)
            last.then_inc(cumulated, 1)
            pe.wait_ge(cum_ready, 1)
            pe.wait_ge(cum_exps, 1)
            for n, src in enumerate((gcum, beta, ecum)):
                for t in range(NT):
                    last = nc.tensor.transpose(k.bank[3 + n][0:H2, t * P:(t + 1) * P], src[:, t, :], k.c("ident"))
                last.then_inc(rows_turned, 1)

        @block.scalar
        def _(act):
            load_tables(k, TABLE_LN_EXP)
            act.wait_ge(inputs_ready, 1)
            nc.scalar.activation(ea[:], k.p("alog"), ACT.Exp).then_inc(exps, 1)
            nc.scalar.activation(t2[:], t2[:], ACT.Exp, scale=-1.0).then_inc(exps, 1)
            nc.scalar.activation(t1[:], t1[:], ACT.Exp).then_inc(exps, 1)
            act.wait_ge(exps, 3)
            nc.scalar.activation(t1[:], t1[:], ACT.Ln, bias=one[:]).then_inc(logs, 1)
            act.wait_ge(cum_ready, 1)
            nc.scalar.activation(ecum[:], gcum[:], ACT.Exp).then_inc(cum_exps, 1)
            nc.scalar.activation(t3[:], t3[:], ACT.Exp).then_inc(cum_exps, 1)

        @block.vector
        def _(dve):
            link(dve, nc.vector.memset(one[:], 1.0))
            dve.wait_ge(projected, 1)
            link(dve, nc.vector.tensor_copy(ab[:].rearrange("p t a b h -> p (t a b h)"), k.bank[0][:, 0:NT * 2 * H2]))
            by_dir = "p t (d h) -> p t d h"
            nc.vector.tensor_tensor(t3[:].rearrange(by_dir, d=2), ab[:, :, :, 0, :],
                                    spread(k.p("dt").rearrange("p (d h) -> p d h", d=2), 1, NT), ALU.add).then_inc(split, 1)
            nc.vector.tensor_copy(t2[:].rearrange(by_dir, d=2), ab[:, :, :, 1, :]).then_inc(split, 1)
            dve.wait_ge(split, 2)
            link(dve, nc.vector.tensor_scalar(t4[:], t3[:], -1.0, None, ALU.mult))
            link(dve, nc.vector.tensor_tensor(t1[:], t3[:], t4[:], ALU.min))
            nc.vector.tensor_scalar(t3[:], t3[:], 0.0, None, ALU.max).then_inc(inputs_ready, 1)
            dve.wait_ge(logs, 1)
            dve.wait_ge(inputs_ready, 1)
            link(dve, nc.vector.tensor_tensor(t1[:], t1[:], t3[:], ALU.add))
            link(dve, nc.vector.tensor_tensor(t1[:], t1[:], spread(ea[:], 1, NT), ALU.mult))
            nc.vector.tensor_scalar(gdec[:], t1[:], -1.0, None, ALU.mult).then_inc(decay_ready, 1)
            link(dve, nc.vector.tensor_scalar(t2[:], t2[:], 1.0, None, ALU.add))
            link(dve, nc.vector.reciprocal(beta[:], t2[:]))
            dve.wait_ge(cumulated, 1)
            link(dve, nc.vector.tensor_copy(gcum[:].rearrange("p t h -> p (t h)"), k.bank[1][:, 0:NT * H2]))
            nc.vector.tensor_tensor(t3[:].rearrange("p t h -> p (t h)"), k.bank[2][:, 0:NT * H2],
                                    gcum[:].rearrange("p t h -> p (t h)"), ALU.subtract).then_inc(cum_ready, 1)
            dve.wait_ge(cum_exps, 2)
            link(dve, nc.vector.tensor_tensor(t4[:], beta[:], ecum[:], ALU.mult))
            link(dve, nc.vector.tensor_scalar(t1[:], gcum[:], -1.0, None, ALU.mult))
            for kind, src in enumerate((beta, t4, t3, t1)):
                for d in range(2):
                    link(dve, nc.vector.tensor_copy(g["cols"][:, :, kind, d, :],
                                                    src[:, :, d * HEADS:(d + 1) * HEADS].rearrange("p t h -> p h t")),
                         wait=(kind == 3 and d == 1))
            for n in range(3):
                dve.wait_ge(rows_turned, n + 1)
                nc.vector.tensor_copy(rows[:, n, :], k.bank[3 + n][0:H2, :]).then_inc(rows_ready, 1)
            dve.wait_ge(rows_ready, 3)


PIECES = "qkvz"


def load_first_head(k, g):
    nc = k.nc
    nc.sync.dma_start(g["w_ab"][:], k.ins["gdn_w_in"][0].rearrange("(k p) n -> p k n", p=P)[:, :, 4 * D:GDN_COLS])\
        .then_inc(g["w_ab_in"], 16)
    for p in range(4):
        nc.sync.dma_start(g["w"][p][:], head_weight(k, p, 0)).then_inc(g["w0_in"][p], 16)


def project_piece(k, g, piece, kc, bank=None):
    return k.nc.tensor.matmul((bank or k.bank[piece % 2])[:], g["w"][piece][:, kc, :], g["hT"][:, kc, :],
                              start=(kc == 0), stop=(kc == KC - 1))


def evacuate_piece(k, g, piece, bank=None):
    if piece == 3:
        return k.nc.scalar.activation(g["zraw"][:], k.bank[1][:], ACT.Copy)
    return k.nc.scalar.activation(g["pad"][piece][:, :, HALO:HALO + N_CTX],
                                  (bank or k.bank[piece % 2])[:].rearrange("p (s t) -> p s t", s=2), ACT.Copy)


def conv_tap(k, g, piece, tap):
    src = g["pad"][piece][:, :, tap:tap + N_CTX]
    dst = g["conv"][piece][:].rearrange("p (s t) -> p s t", s=2)
    w = g["taps"][:, piece * TAPS + tap:piece * TAPS + tap + 1]
    if tap == 0:
        return k.nc.vector.tensor_scalar(dst, src, w, None, ALU.mult)
    return k.nc.vector.scalar_tensor_tensor(out=dst, in0=src, scalar=w, in1=dst, op0=ALU.mult, op1=ALU.add)


def head_weight(k, piece, head):
    w = k.ins["gdn_w_in"][0].rearrange("(k p) n -> p k n", p=P)
    return w[:, :, bass.ds(head * P + piece * D, P)]


def stage_gdn_first(k, g):
    nc = k.nc
    projected, moved, zeroed, taps_in, convolved = (k.sem(n) for n in ("proj0", "moved0", "pads_zero", "taps0", "conv0"))
    with nc.Block() as block:
        @block.gpsimd
        def _(pool):
            for p in range(3):
                nc.gpsimd.memset(g["pad"][p][:], 0.0).then_inc(zeroed, 1)
            pool.wait_ge(zeroed, 3)

        @block.tensor
        def _(pe):
            for p in (2, 3):
                pe.wait_ge(g["w0_in"][p], 16)
                for kc in range(KC):
                    last = project_piece(k, g, p, kc)
                last.then_inc(projected, 1)

        @block.scalar
        def _(act):
            act.wait_ge(zeroed, 3)
            act.wait_ge(g["first_qk"], 2)
            for p in range(4):
                if p >= 2:
                    act.wait_ge(projected, p - 1)
                evacuate_piece(k, g, p, k.bank[6 + p] if p < 2 else None).then_inc(moved, 1)
            act.wait_ge(moved, 4)

        @block.vector
        def _(dve):
            nc.vector.tensor_copy(g["taps"][:], k.p("conv")[:, 0:3 * TAPS]).then_inc(taps_in, 1)
            dve.wait_ge(taps_in, 1)
            for p in range(3):
                dve.wait_ge(moved, p + 1)
                for tap in range(TAPS):
                    conv_tap(k, g, p, tap).then_inc(convolved, 1)
                    dve.wait_ge(convolved, p * TAPS + tap + 1)


def fetch_rows(k, g, head, sem):
    src = k.rows_dram[bass.ds(head, 1)].rearrange("o d n t -> o (d n t)").broadcast_to([P, 6 * T])
    return k.nc.sync.dma_start(g["rows"][:].rearrange("p d n t -> p (d n t)"), src).then_inc(sem, 16)


def stage_gdn_heads(k, g):
    nc = k.nc
    L = range(1, len(LEVELS))
    last_level = len(LEVELS) - 1
    DIR = (0, 1)
    per_seq = N_CTX // CHUNK
    order = [list(range(NCH)), list(range(per_seq - 1, -1, -1)) + list(range(NCH - 1, per_seq - 1, -1))]
    E, B, KQ, A = g["E"], g["B"], g["KQ"], g["A"]
    X, XT, Z, As = g["E"], g["XT"], g["B"], g["As"]
    U, W = g["A"], g["W"]

    level_taps = [(p, t) for p in (0, 1) for t in range(TAPS)]
    step_taps = {c: [] for c in range(NCH)} | {4: [0], 5: [1], 6: [2], 7: [3, 4]}
    PE = Steps(k.sem("gdn_pe"), ["nq", "nk", "kk", "kq", "pr_q", "trk", "trv", "pr_k", "x0_0", "x0_1"]
               + [s for l in L for s in ([f"Z{l}_0", f"Z{l}_1", f"D{l}_0", f"D{l}_1"]
                                         + ([f"T{l}_0", f"T{l}_1"] if l < last_level else []))]
               + ["u0", "w0", "u1", "w1"]
               + [s for c in range(NCH) for s in ([f"ws{c}_0", f"ws{c}_1"] + (["pr_v"] if c == 3 else [])
                                                  + [f"{n}{c}_{d}" for d in DIR for n in ("up", "o") if c < NCH - 1 or n == "o"])]
               + ["pr_z", "on"], HEADS - 1, [f"pr_{p}" for p in PIECES])
    SC = Steps(k.sem("gdn_act"), ["silu_q", "silu_k", "silu_v", "silu_z", "sq_q", "sq_k", "ln_q", "rs_q", "ln_k", "rs_k"]
               + [f"E{d}_{t}" for d in DIR for t in range(NT)] + ["ktok", "vtok", "ev_q", "ev_k", "x0_0", "x0_1"]
               + [s for l in L for s in ([f"Z{l}_0", f"Z{l}_1"] + ([f"T{l}_0", f"T{l}_1"] if l < last_level else []))]
               + ["u0", "w0", "u1", "w1", "ev_v", "osq", "ev_z", "ln_o", "rs_o"],
               HEADS - 1, [f"ev_{p}" for p in PIECES])
    V = Steps(k.sem("gdn_dve"), ["cols", "taps", "S0", "S1", "tmp0", "tmp1", "last0", "last1", "qn", "kn"]
              + ["B0", "B1", "A0", "A1", "m0", "m1", "XT0", "XT1", "aT0", "aT1"]
              + [s for l in L for s in ([f"X{l}_0", f"X{l}_1"] + (["qe0", "qe1"] if l == 1 else [])
                                        + [f"c{p}_{t}" for p, t in level_taps[2 * (l - 1):2 * l]])]
              + [s for c in range(NCH) for s in ([f"vn{c}_0", f"vn{c}_1"] + ([f"S{c}_0", f"S{c}_1"] if c < NCH - 1 else [])
                                                 + [f"c2_{t}" for t in step_taps[c]])]
              + ["on", "og"], HEADS - 1, ["taps"] + [f"c{p}_{t}" for p in range(3) for t in range(TAPS)])
    G = Steps(k.sem("gdn_pool"), [f"As{l}_{d}" for l in L for d in DIR]
              + [f"{n}{d}" for n in ("vb", "kbe", "kd") for d in DIR], HEADS - 1)
    w_in = [k.sem(f"w_{p}") for p in PIECES]
    rows_in = k.sem("rows_in")

    def last_of(d, c):
        return c * CHUNK + (CHUNK - 1 if d == 0 else 0)

    def place(d, step):
        c = order[d][step]
        return c, c // 2, (c % 2) * CHUNK

    with nc.Block() as block:
        @block.sync
        def _(sp):
            for p in range(4):
                nc.sync.dma_start(g["w"][p][:], head_weight(k, p, 1)).then_inc(w_in[p], 16)
            fetch_rows(k, g, 0, rows_in)

            def fetch_next(h, head):
                sp.wait_ge(V.sem, V.at("qe1", h))
                fetch_rows(k, g, h + 1, rows_in)
                for p in range(4):
                    sp.wait_ge(PE.sem, PE.at(f"pr_{PIECES[p]}", h))
                    nc.sync.dma_start(g["w"][p][:], head_weight(k, p, head)).then_inc(w_in[p], 16)

            with sp.Fori(0, HEADS - 2) as h:
                fetch_next(h, h + 2)
            sp.wait_ge(V.sem, V.at("qe1", HEADS - 2))
            fetch_rows(k, g, HEADS - 1, rows_in)

        @block.gpsimd
        def _(pool):
            pool.sem_inc(G.sem, G.n)
            def head(h, last_head):
                for l in L:
                    for d in DIR:
                        if l == 1:
                            pool.wait_ge(V.sem, V.at(f"A{d}", h))
                        m = k.c("level")[:, (d * len(LEVELS) + l) * P:(d * len(LEVELS) + l + 1) * P]
                        nc.gpsimd.tensor_tensor(As[:, l - 1, d], A[:, d], spread(m, 1, NT), ALU.mult)\
                            .then_inc(G.did(f"As{l}_{d}"), 1)
                pool.wait_ge(SC.sem, SC.at("vtok", h))
                for n, src, kind in (("vb", g["vtok"], 0), ("kbe", g["ktok"], 1), ("kd", g["ktok"], 2)):
                    for d in DIR:
                        nc.gpsimd.tensor_tensor(g[n][:, d], src[:], spread(g["hcols"][:, kind, d, :], 2, P), ALU.mult)\
                            .then_inc(G.did(f"{n}{d}"), 1)

            with pool.Fori(0, HEADS - 1) as h:
                head(h, False)
            head(HEADS - 1, True)

        @block.tensor
        def _(pe):
            pe.sem_inc(PE.sem, PE.n)
            def head(h, last_head):
                def fill(p, first, count):
                    if last_head:
                        return
                    for kc in range(first, first + count):
                        if kc == 0:
                            pe.wait_ge(w_in[p], (h + 1) * 16)
                            if p >= 2:
                                pe.wait_ge(SC.sem, SC.at(f"ev_{PIECES[p - 2]}", h))
                        ins = project_piece(k, g, p, kc)
                    if first + count == KC:
                        ins.then_inc(PE.did(f"pr_{PIECES[p]}"), 1)

                pe.wait_ge(SC.sem, SC.at("sq_q", h))
                nc.tensor.matmul(k.bank[3][:], k.c("ones"), g["sq"][:, 0], start=True, stop=True).then_inc(PE.did("nq"), 1)
                pe.wait_ge(SC.sem, SC.at("sq_k", h))
                nc.tensor.matmul(k.bank[4][:], k.c("ones"), g["sq"][:, 1], start=True, stop=True).then_inc(PE.did("nk"), 1)
                fill(0, 0, 4)
                pe.wait_ge(V.sem, V.at("kn", h))
                for t in range(NT):
                    s = slice(t * P, (t + 1) * P)
                    last = nc.tensor.matmul(k.bank[5][:, s], g["k"][:, s], g["k"][:, s], start=True, stop=True)
                last.then_inc(PE.did("kk"), 1)
                for t in range(NT):
                    s = slice(t * P, (t + 1) * P)
                    last = nc.tensor.matmul(k.bank[6][:, s], g["k"][:, s], g["q"][:, s], start=True, stop=True)
                last.then_inc(PE.did("kq"), 1)
                fill(0, 4, 4)
                for t in range(NT):
                    last = nc.tensor.transpose(k.bank[7][:, t * P:(t + 1) * P], g["k"][:, t * P:(t + 1) * P], k.c("ident"))
                last.then_inc(PE.did("trk"), 1)
                pe.wait_ge(SC.sem, SC.at("ln_q", h))
                for t in range(NT):
                    last = nc.tensor.transpose(k.bank[3][:, t * P:(t + 1) * P], g["v"][:, t * P:(t + 1) * P], k.c("ident"))
                last.then_inc(PE.did("trv"), 1)
                fill(1, 0, KC)
                pe.wait_ge(SC.sem, SC.at("vtok", h))
                for d in DIR:
                    pe.wait_ge(V.sem, V.at(f"XT{d}", h))
                    for t in range(NT):
                        last = nc.tensor.transpose(k.bank[3 + d][:, t * P:(t + 1) * P], XT[:, d, t], k.c("ident"))
                    last.then_inc(PE.did(f"x0_{d}"), 1)
                for l in L:
                    for d in DIR:
                        pe.wait_ge(G.sem, G.at(f"As{l}_{d}", h))
                        if l == 1:
                            pe.wait_ge(SC.sem, SC.at(f"x0_{d}", h))
                        else:
                            pe.wait_ge(V.sem, V.at(f"X{l - 1}_{d}", h))
                            pe.wait_ge(SC.sem, SC.at(f"T{l - 1}_{d}", h))
                        for t in range(NT):
                            last = nc.tensor.matmul(k.bank[3 + d][:, t * P:(t + 1) * P], As[:, l - 1, d, t], X[:, d, t],
                                                    start=True, stop=True)
                        last.then_inc(PE.did(f"Z{l}_{d}"), 1)
                    for d in DIR:
                        pe.wait_ge(SC.sem, SC.at(f"Z{l}_{d}", h))
                        for t in range(NT):
                            a, b = (XT[:, d, t], Z[:, d, t]) if l < last_level else (Z[:, d, t], XT[:, d, t])
                            last = nc.tensor.matmul(k.bank[5 + d][:, t * P:(t + 1) * P], a, b, start=True, stop=True)
                        last.then_inc(PE.did(f"D{l}_{d}"), 1)
                    if l < last_level:
                        for d in DIR:
                            pe.wait_ge(V.sem, V.at(f"X{l}_{d}", h))
                            for t in range(NT):
                                last = nc.tensor.transpose(k.bank[3 + d][:, t * P:(t + 1) * P], X[:, d, t], k.c("ident"))
                            last.then_inc(PE.did(f"T{l}_{d}"), 1)
                for d in DIR:
                    pe.wait_ge(V.sem, V.at(f"X{last_level}_{d}", h))
                    pe.wait_ge(G.sem, G.at(f"vb{d}", h))
                    for t in range(NT):
                        last = nc.tensor.matmul(k.bank[3 + d][:, t * P:(t + 1) * P], XT[:, d, t], g["vb"][:, d, t],
                                                start=True, stop=True)
                    last.then_inc(PE.did(f"u{d}"), 1)
                    pe.wait_ge(G.sem, G.at(f"kbe{d}", h))
                    for t in range(NT):
                        last = nc.tensor.matmul(k.bank[5 + d][:, t * P:(t + 1) * P], g["kbe"][:, d, t], XT[:, d, t],
                                                start=True, stop=True)
                    last.then_inc(PE.did(f"w{d}"), 1)
                pe.wait_ge(G.sem, G.at("kd1", h))
                v_fill, z_fill = {0: (0, 2), 1: (2, 2), 2: (4, 2), 3: (6, 2)}, {4: (0, 2), 5: (2, 2), 6: (4, 1), 7: (5, 1)}
                for c in range(NCH):
                    def part_of(d):
                        ch, tile, r = place(d, c)
                        return slice(ch * CHUNK, (ch + 1) * CHUNK), slice(r, r + CHUNK), tile, r

                    for d in DIR:
                        cols, part, tile, r = part_of(d)
                        if c == 0:
                            pe.wait_ge(SC.sem, SC.at(f"w{d}", h))
                        else:
                            pe.wait_ge(V.sem, V.at(f"S{c - 1}_{d}", h))
                        nc.tensor.matmul(k.bank[3 + d][part, 0:P], W[:, d, cols], g["S"][:, d], start=True, stop=True)\
                            .then_inc(PE.did(f"ws{c}_{d}"), 1)
                    if c == 0:
                        pe.wait_ge(V.sem, V.at("on", h - 1))
                    for d in DIR:
                        cols, part, tile, r = part_of(d)
                        nc.tensor.matmul(k.bank[2][:, cols], g["S"][:, d], g["qe"][:, d, cols], start=((c, d) == (0, 0)),
                                         stop=True, skip_group_check=True)
                    if c in v_fill:
                        fill(2, *v_fill[c])
                    if c in z_fill:
                        fill(3, *z_fill[c])
                    for d in DIR:
                        cols, part, tile, r = part_of(d)
                        pe.wait_ge(V.sem, V.at(f"vn{c}_{d}", h))
                        if c < NCH - 1:
                            nc.tensor.matmul(k.bank[5 + d][:, 0:P], g["kd"][part, d, tile], g["vn"][part, d],
                                             start=True, stop=True).then_inc(PE.did(f"up{c}_{d}"), 1)
                        if d == 1:
                            pe.wait_ge(PE.sem, PE.at(f"o{c}_0", h))
                        nc.tensor.matmul(k.bank[2][:, cols], g["vn"][part, d], KQ[part, d, tile, r:r + CHUNK],
                                         start=False, stop=True, skip_group_check=True).then_inc(PE.did(f"o{c}_{d}"), 1)
                fill(3, 6, 2)
                pe.wait_ge(SC.sem, SC.at("osq", h))
                nc.tensor.matmul(k.bank[7][:], k.c("ones"), g["sq"][:, 0], start=True, stop=True).then_inc(PE.did("on"), 1)

            with pe.Fori(0, HEADS - 1) as h:
                head(h, False)
            head(HEADS - 1, True)

        @block.scalar
        def _(act):
            act.sem_inc(SC.sem, SC.n)
            def head(h, last_head):
                load_tables(k, TABLE_SILU)
                act.wait_ge(V.sem, V.at("c2_4", h - 1))
                for n, (dst, src) in {"q": (g["q"], g["conv"][0]), "k": (g["k"], g["conv"][1]), "v": (g["v"], g["conv"][2]),
                                      "z": (g["z"], g["zraw"])}.items():
                    if n == "z":
                        act.wait_ge(SC.sem, SC.at("ev_z", h - 1))
                        act.wait_ge(V.sem, V.at("og", h - 1))
                    nc.scalar.activation(dst[:], src[:], ACT.Silu).then_inc(SC.did(f"silu_{n}"), 1)
                load_tables(k, TABLE_LN_EXP)
                act.wait_ge(SC.sem, SC.at("silu_k", h))
                nc.scalar.activation(g["sq"][:, 0], g["q"][:], ACT.Square).then_inc(SC.did("sq_q"), 1)
                nc.scalar.activation(g["sq"][:, 1], g["k"][:], ACT.Square).then_inc(SC.did("sq_k"), 1)
                for n, b in (("q", 0), ("k", 1)):
                    act.wait_ge(PE.sem, PE.at(f"n{n}", h))
                    nc.scalar.activation(g["sq"][:, b], k.bank[3 + b][:], ACT.Ln, bias=g["eps"][:, 0:1])\
                        .then_inc(SC.did(f"ln_{n}"), 1)
                    act.wait_ge(SC.sem, SC.at(f"ln_{n}", h))
                    nc.scalar.activation(g["sq"][:, b], g["sq"][:, b], ACT.Exp, bias=g["eps"][:, 1 + b:2 + b], scale=-0.5)\
                        .then_inc(SC.did(f"rs_{n}"), 1)
                for d in DIR:
                    act.wait_ge(V.sem, V.at(f"tmp{d}", h))
                    for t in range(NT):
                        nc.scalar.activation(E[:, d, t], E[:, d, t], ACT.Exp, bias=g["hcols"][:, 3, d, t:t + 1])\
                            .then_inc(SC.did(f"E{d}_{t}"), 1)
                act.wait_ge(PE.sem, PE.at("trk", h))
                nc.scalar.activation(g["ktok"][:].rearrange("p t d -> p (t d)"), k.bank[7][:], ACT.Copy).then_inc(SC.did("ktok"), 1)
                act.wait_ge(PE.sem, PE.at("trv", h))
                nc.scalar.activation(g["vtok"][:].rearrange("p t d -> p (t d)"), k.bank[3][:], ACT.Copy).then_inc(SC.did("vtok"), 1)
                if not last_head:
                    act.wait_ge(PE.sem, PE.at("pr_q", h))
                    evacuate_piece(k, g, 0).then_inc(SC.did("ev_q"), 1)
                    act.wait_ge(PE.sem, PE.at("pr_k", h))
                    evacuate_piece(k, g, 1).then_inc(SC.did("ev_k"), 1)

                def flat(t, d):
                    return t[:, d].rearrange("p t i -> p (t i)")

                act.wait_ge(V.sem, V.at("aT1", h))
                for d in DIR:
                    act.wait_ge(PE.sem, PE.at(f"x0_{d}", h))
                    nc.scalar.activation(flat(X, d), k.bank[3 + d][:], ACT.Copy).then_inc(SC.did(f"x0_{d}"), 1)
                for l in L:
                    for d in DIR:
                        act.wait_ge(PE.sem, PE.at(f"Z{l}_{d}", h))
                        nc.scalar.activation(flat(Z, d), k.bank[3 + d][:], ACT.Copy).then_inc(SC.did(f"Z{l}_{d}"), 1)
                    if l < last_level:
                        for d in DIR:
                            act.wait_ge(PE.sem, PE.at(f"T{l}_{d}", h))
                            nc.scalar.activation(flat(XT, d), k.bank[3 + d][:], ACT.Copy).then_inc(SC.did(f"T{l}_{d}"), 1)
                act.wait_ge(G.sem, G.at(f"As{last_level}_1", h))
                for d in DIR:
                    act.wait_ge(PE.sem, PE.at(f"u{d}", h))
                    nc.scalar.activation(flat(U, d), k.bank[3 + d][:], ACT.Copy).then_inc(SC.did(f"u{d}"), 1)
                    act.wait_ge(PE.sem, PE.at(f"w{d}", h))
                    nc.scalar.activation(W[:, d], k.bank[5 + d][:], ACT.Copy).then_inc(SC.did(f"w{d}"), 1)
                if not last_head:
                    act.wait_ge(PE.sem, PE.at("pr_v", h))
                    evacuate_piece(k, g, 2).then_inc(SC.did("ev_v"), 1)
                act.wait_ge(PE.sem, PE.at(f"o{NCH - 1}_1", h))
                nc.scalar.activation(g["sq"][:, 0], k.bank[2][:], ACT.Square).then_inc(SC.did("osq"), 1)
                if not last_head:
                    act.wait_ge(PE.sem, PE.at("pr_z", h))
                    evacuate_piece(k, g, 3).then_inc(SC.did("ev_z"), 1)
                act.wait_ge(PE.sem, PE.at("on", h))
                nc.scalar.activation(g["sq"][:, 1], k.bank[7][:], ACT.Ln, bias=g["eps"][:, 0:1], scale=1.0 / P)\
                    .then_inc(SC.did("ln_o"), 1)
                act.wait_ge(SC.sem, SC.at("ln_o", h))
                nc.scalar.activation(g["sq"][:, 1], g["sq"][:, 1], ACT.Exp, scale=-0.5).then_inc(SC.did("rs_o"), 1)

            with act.Fori(0, HEADS - 1) as h:
                head(h, False)
            head(HEADS - 1, True)

        @block.vector
        def _(dve):
            dve.sem_inc(V.sem, V.n)
            def head(h, last_head):
                def next_tap(p, tap):
                    if last_head:
                        return
                    if tap == 0:
                        dve.wait_ge(SC.sem, SC.at(f"ev_{PIECES[p]}", h))
                    else:
                        dve.wait_ge(V.sem, V.at(f"c{p}_{tap - 1}", h))
                    conv_tap(k, g, p, tap).then_inc(V.did(f"c{p}_{tap}"), 1)

                dve.wait_ge(G.sem, G.at("kd1", h - 1))
                dve.wait_ge(SC.sem, SC.at("E1_3", h - 1))
                nc.vector.tensor_copy(g["hcols"][:].rearrange("p a b c -> p (a b c)"),
                                      g["cols"][:].rearrange("p h a b c -> p (h a b c)")[:, bass.ds(h * 8 * NT, 8 * NT)])\
                    .then_inc(V.did("cols"), 1)
                if not last_head:
                    nc.vector.tensor_copy(g["taps"][:], k.p("conv")[:, bass.ds((h + 1) * 3 * TAPS, 3 * TAPS)])\
                        .then_inc(V.did("taps"), 1)
                for d in DIR:
                    nc.vector.memset(g["S"][:, d], 0.0).then_inc(V.did(f"S{d}"), 1)
                dve.wait_ge(rows_in, (h + 1) * 16)
                for d in DIR:
                    nc.vector.tensor_tensor(E[:, d], g["rows"][:, d, 0].rearrange("p (t i) -> p t i", t=NT),
                                            spread(k.c("neg")[:, d * P:(d + 1) * P], 1, NT), ALU.add)\
                        .then_inc(V.did(f"tmp{d}"), 1)
                for d in DIR:
                    a = last_of(d, 0)
                    nc.vector.tensor_copy(g["elast"][:, d], g["rows"][:, d, 2, a:a + (NCH - 1) * CHUNK + 1:CHUNK])\
                        .then_inc(V.did(f"last{d}"), 1)
                for n, b in (("q", 0), ("k", 1)):
                    dve.wait_ge(SC.sem, SC.at(f"rs_{n}", h))
                    nc.vector.tensor_tensor(g[n][:], g[n][:], g["sq"][:, b], ALU.mult).then_inc(V.did(f"{n}n"), 1)
                for d in DIR:
                    dve.wait_ge(SC.sem, SC.at(f"E{d}_3", h))
                    nc.vector.tensor_tensor(B[:, d].rearrange("p t i -> p (t i)"), E[:, d].rearrange("p t i -> p (t i)"),
                                            g["rows"][:, d, 1], ALU.mult).then_inc(V.did(f"B{d}"), 1)
                for d in DIR:
                    dve.wait_ge(PE.sem, PE.at("kk", h))
                    dve.wait_ge(V.sem, V.at(f"B{d}", h))
                    nc.vector.tensor_tensor(A[:, d].rearrange("p t i -> p (t i)"), k.bank[5][:],
                                            B[:, d].rearrange("p t i -> p (t i)"), ALU.mult).then_inc(V.did(f"A{d}"), 1)
                for d in DIR:
                    dve.wait_ge(V.sem, V.at(f"A{d}", h))
                    m = k.c("level")[:, d * len(LEVELS) * P:(d * len(LEVELS) + 1) * P]
                    nc.vector.tensor_tensor(B[:, d], A[:, d], spread(m, 1, NT), ALU.mult).then_inc(V.did(f"m{d}"), 1)
                for d in DIR:
                    dve.wait_ge(V.sem, V.at(f"m{d}", h))
                    nc.vector.tensor_tensor(XT[:, d], spread(k.c("ident"), 1, NT), B[:, d], ALU.subtract)\
                        .then_inc(V.did(f"XT{d}"), 1)
                for d in DIR:
                    dve.wait_ge(PE.sem, PE.at("kq", h))
                    nc.vector.tensor_tensor(KQ[:, d].rearrange("p t i -> p (t i)"), k.bank[6][:],
                                            E[:, d].rearrange("p t i -> p (t i)"), ALU.mult).then_inc(V.did(f"aT{d}"), 1)
                for l in L:
                    for d in DIR:
                        dst = (X if l < last_level else XT)[:, d].rearrange("p t i -> p (t i)")
                        dve.wait_ge(PE.sem, PE.at(f"D{l}_{d}", h))
                        nc.vector.tensor_tensor(dst, dst, k.bank[5 + d][:], ALU.subtract).then_inc(V.did(f"X{l}_{d}"), 1)
                    if l == 1:
                        for d in DIR:
                            nc.vector.tensor_tensor(g["qe"][:, d], g["q"][:], g["rows"][:, d, 2], ALU.mult)\
                                .then_inc(V.did(f"qe{d}"), 1)
                    for p, tap in level_taps[2 * (l - 1):2 * l]:
                        next_tap(p, tap)
                for c in range(NCH):
                    for d in DIR:
                        ch, tile, r = place(d, c)
                        part = slice(r, r + CHUNK)
                        if c == 0:
                            dve.wait_ge(SC.sem, SC.at(f"w{d}", h))
                        dve.wait_ge(PE.sem, PE.at(f"ws{c}_{d}", h))
                        nc.vector.tensor_tensor(g["vn"][part, d], U[part, d, tile], k.bank[3 + d][part, 0:P], ALU.subtract)\
                            .then_inc(V.did(f"vn{c}_{d}"), 1)
                    for d in DIR:
                        if c < NCH - 1:
                            ch, tile, r = place(d, c)
                            dve.wait_ge(PE.sem, PE.at(f"up{c}_{d}", h))
                            nc.vector.scalar_tensor_tensor(out=g["S"][:, d], in0=g["S"][:, d],
                                                           scalar=g["elast"][:, d, ch:ch + 1], in1=k.bank[5 + d][:, 0:P],
                                                           op0=ALU.mult, op1=ALU.add).then_inc(V.did(f"S{c}_{d}"), 1)
                    for tap in step_taps[c]:
                        next_tap(2, tap)
                dve.wait_ge(SC.sem, SC.at("rs_o", h))
                nc.vector.tensor_tensor(g["sq"][:, 0], k.bank[2][:], g["sq"][:, 1], ALU.mult).then_inc(V.did("on"), 1)
                dve.wait_ge(V.sem, V.at("on", h))
                nc.vector.scalar_tensor_tensor(out=g["oz"][:].rearrange("p h t -> p (h t)")[:, bass.ds(h * T, T)],
                                               in0=g["sq"][:, 0], scalar=k.p("gdn_gain"), in1=g["z"][:],
                                               op0=ALU.mult, op1=ALU.mult).then_inc(V.did("og"), 1)

            with dve.Fori(0, HEADS - 1) as h:
                head(h, False)
            head(HEADS - 1, True)


def stage_mix_out(k, g, w_out, layer, gate, t0):
    nc, ar = k.nc, k.arena(g["w_at"])
    n = T - t0
    halves = [(0, 0, N_CTX), (1, N_CTX, T)] if t0 == 0 else [(1, 0, n)]
    w = ar("w_out", [P, HEADS, D])
    landed = [k.sem(f"w_out{m}") for m in range(KC)]
    product, added = k.sem("out_product"), k.sem("out_added")
    src = w_out.rearrange("(k p) n -> p k n", p=P)
    with nc.Block() as block:
        @block.sync
        def _(sp):
            for m in range(KC):
                s = slice(m * P, (m + 1) * P)
                nc.sync.dma_start(w[:, :, s], src[:, :, s]).then_inc(landed[m], 16)

        @block.tensor
        def _(pe):
            for m in range(KC):
                pe.wait_ge(landed[m], 16)
                for h in range(HEADS):
                    last = nc.tensor.matmul(k.bank[m][:, 0:n], w[:, h, m * P:(m + 1) * P], g["oz"][:, h, 0:n],
                                            start=(h == 0), stop=(h == HEADS - 1))
                last.then_inc(product, 1)

        @block.vector
        def _(dve):
            for m in range(KC):
                dve.wait_ge(product, m + 1)
                for c, a, b in halves:
                    x = k.xT[:, m, t0 + a:t0 + b]
                    nc.vector.scalar_tensor_tensor(out=x, in0=k.bank[m][:, a:b], scalar=k.mod[:, layer, gate * KC + m, c:c + 1],
                                                   in1=x, op0=ALU.mult, op1=ALU.add).then_inc(added, 1)
            dve.wait_ge(added, KC * len(halves))


def stage_route(k, layer, hT, t0, r):
    nt = (T - t0) // P
    nc, ar = k.nc, k.arena(r["tmp_at"])
    R = GROUPS + EXPERTS
    n_over = MAX_BLOCKS - EXPERTS
    w_r, landed = r["w_r"], r["w_r_in"]
    lg = ar("logits", [P, nt, R])
    gmax, gsum, pg, m1, m2, ed, den = (ar(f"c{i}", [P, nt, 1]) for i in range(7))
    g4, goh = ar("g4", [P, nt, GROUPS]), ar("goh", [P, nt, GROUPS])
    em, eq, mem = (ar(f"e{i}", [P, nt, EXPERTS]) for i in range(3))
    oh = ar("oh", [P, 2, nt, EXPERTS])
    rank, quo, blk, slot_e = (ar(f"r{i}", [P, nt, EXPERTS]) for i in range(4))
    cnt, nov, ovend, ovoff, tmp = (ar(f"n{i}", [P, EXPERTS]) for i in range(5))
    cmp_over = ar("cmp_over", [P, n_over, EXPERTS])
    table = ar("table", [P, MAX_BLOCKS])
    slot = ar("slot", [P, 2 * nt])
    block_of, place = ar("block_of", [P, 2 * nt]), ar("place", [P, 2 * nt])
    rsel = ar("rsel", [P, 2 * nt, P])
    psel = ar("psel", [P, 2 * nt, SLOT_COLS])
    rows = ar("rows", [P, nt, D])
    stored = k.sem("h_stored")
    logits_done, ranked, slots_done, exps = k.sem("logits"), k.sem("ranked"), k.sem("slot_tokens"), k.sem("route_exp")
    onehots, selects, exp_in, finished = k.sem("onehots"), k.sem("selects"), k.sem("exp_in"), k.sem("route_done")
    turned, moved = k.sem("h_turned"), k.sem("h_moved")
    link = k.links("route_link")
    tiles = [(kc, h) for h in range(nt // 2) for kc in range(KC)]

    with k.nc.Block() as block:
        @block.sync
        def _(sp):
            for t in range(nt):
                sp.wait_ge(moved, 2 * (t + 1))
                nc.sync.dma_start(k.h_dram[t * P:(t + 1) * P, :], rows[:, t, :]).then_inc(stored, 16)
            sp.wait_ge(stored, 16 * nt)

        @block.tensor
        def _(pe):
            pe.wait_ge(landed, 32)
            for t in range(nt):
                for kc in range(KC):
                    last = nc.tensor.matmul(k.bank[0][:, t * R:(t + 1) * R], hT[:, kc, t * P:(t + 1) * P], w_r[:, kc, :],
                                            start=(kc == 0), stop=(kc == KC - 1))
            last.then_inc(logits_done, 1)
            for t in range(nt):
                for half in range(2):
                    if t >= 1:
                        pe.wait_ge(moved, 2 * (t - 1) + half + 1)
                    for j in range(4):
                        kc = half * 4 + j
                        last = nc.tensor.transpose(k.bank[4 + half][:, j * P:(j + 1) * P], hT[:, kc, t * P:(t + 1) * P],
                                                   k.c("ident"))
                    last.then_inc(turned, 1)
            pe.wait_ge(onehots, 1)
            for t in range(nt):
                for e in range(t + 1):
                    last = nc.tensor.matmul(k.bank[1][:, t * EXPERTS:(t + 1) * EXPERTS],
                                            k.c("before") if e == t else k.c("ones"), mem[:, e, :],
                                            start=(e == 0), stop=(e == t))
            for e in range(nt):
                last = nc.tensor.matmul(k.bank[2][:, 0:EXPERTS], k.c("ones"), mem[:, e, :],
                                        start=(e == 0), stop=(e == nt - 1))
            last.then_inc(ranked, 1)
            pe.wait_ge(selects, 1)
            for a in range(2 * nt):
                last = nc.tensor.matmul(k.bank[3][:, 0:SLOT_COLS], rsel[:, a, :], psel[:, a, :],
                                        start=(a == 0), stop=(a == 2 * nt - 1))
            last.then_inc(slots_done, 1)

        @block.scalar
        def _(act):
            load_tables(k, TABLE_LN_EXP)
            for n in range(2 * nt):
                act.wait_ge(turned, n + 1)
                nc.scalar.activation(rows[:, n // 2, (n % 2) * 512:(n % 2 + 1) * 512], k.bank[4 + n % 2][:], ACT.Copy)\
                    .then_inc(moved, 1)
            act.wait_ge(exp_in, 1)
            nc.scalar.activation(g4[:], g4[:], ACT.Exp).then_inc(exps, 1)
            act.wait_ge(exp_in, 2)
            nc.scalar.activation(ed[:], ed[:], ACT.Exp).then_inc(exps, 1)

        @block.vector
        def _(dve):
            v = nc.vector

            def first_max(dst, src, m, desc, width):
                link(dve, v.tensor_reduce(m[:], src, AX.X, ALU.max))
                link(dve, v.tensor_tensor(eq[:, :, 0:width], src, m[:].broadcast_to([P, nt, width]), ALU.is_ge))
                link(dve, v.tensor_tensor(eq[:, :, 0:width], eq[:, :, 0:width], spread(desc, 1, nt), ALU.mult))
                link(dve, v.tensor_reduce(den[:], eq[:, :, 0:width], AX.X, ALU.max))
                link(dve, v.tensor_tensor(dst, eq[:, :, 0:width], den[:].broadcast_to([P, nt, width]), ALU.is_equal))

            dve.wait_ge(logits_done, 1)
            a = PARAM["rbias"][0] + layer * R
            link(dve, v.tensor_tensor(lg[:], k.bank[0][:, 0:nt * R].rearrange("p (t r) -> p t r", t=nt),
                                      spread(k.par[:, a:a + R], 1, nt), ALU.add))
            first_max(goh[:], lg[:, :, 0:GROUPS], gmax, k.c("desc4"), GROUPS)
            v.tensor_tensor(g4[:], lg[:, :, 0:GROUPS], gmax[:].broadcast_to([P, nt, GROUPS]), ALU.subtract).then_inc(exp_in, 1)
            for t in range(nt):
                ohx = spread(goh[:, t, :], 2, PER_GROUP)
                link(dve, v.tensor_tensor(em[:, t].rearrange("p (g e) -> p g e", g=GROUPS),
                                          lg[:, t, GROUPS:R].rearrange("p (g e) -> p g e", g=GROUPS), ohx, ALU.mult),
                     wait=(t == nt - 1))
            link(dve, v.tensor_scalar(goh[:], goh[:], -1.0, BIG, ALU.add, ALU.mult))
            for t in range(nt):
                ohx = spread(goh[:, t, :], 2, PER_GROUP)
                e = em[:, t].rearrange("p (g e) -> p g e", g=GROUPS)
                link(dve, v.tensor_tensor(e, e, ohx, ALU.add), wait=(t == nt - 1))
            first_max(oh[:, 0], em[:], m1, k.c("desc32"), EXPERTS)
            link(dve, v.tensor_scalar(eq[:], oh[:, 0], -2.0 * BIG, None, ALU.mult))
            link(dve, v.tensor_tensor(em[:], em[:], eq[:], ALU.add))
            first_max(oh[:, 1], em[:], m2, k.c("desc32"), EXPERTS)
            v.tensor_tensor(mem[:], oh[:, 0], oh[:, 1], ALU.add).then_inc(onehots, 1)
            v.tensor_tensor(ed[:], m2[:], m1[:], ALU.subtract).then_inc(exp_in, 1)
            dve.wait_ge(exps, 2)
            link(dve, v.tensor_reduce(gsum[:], g4[:], AX.X, ALU.add))
            link(dve, v.reciprocal(pg[:], gsum[:]))
            link(dve, v.tensor_scalar(den[:], ed[:], 1.0, None, ALU.add))
            link(dve, v.reciprocal(gsum[:], den[:]))
            link(dve, v.tensor_tensor(r["gate"][:, 0], pg[:], gsum[:], ALU.mult))
            link(dve, v.tensor_tensor(r["gate"][:, 1], r["gate"][:, 0], ed[:], ALU.mult))
            dve.wait_ge(ranked, 1)
            link(dve, v.tensor_copy(rank[:].rearrange("p t e -> p (t e)"), k.bank[1][:, 0:nt * EXPERTS]), wait=False)
            link(dve, v.tensor_copy(cnt[:], k.bank[2][:, 0:EXPERTS]), wait=False)
            link(dve, v.memset(nov[:], 0.0), wait=False)
            link(dve, v.memset(quo[:], 0.0))
            for j in range(1, nt * P // CAP):
                cap = float(CAP * j)
                link(dve, v.tensor_scalar(tmp[:], cnt[:], cap, None, ALU.is_gt), wait=False)
                link(dve, v.tensor_scalar(eq[:], rank[:], cap, None, ALU.is_ge))
                link(dve, v.tensor_tensor(nov[:], nov[:], tmp[:], ALU.add), wait=False)
                link(dve, v.tensor_tensor(quo[:], quo[:], eq[:], ALU.add))
            link(dve, v.tensor_copy(ovend[:], nov[:]))
            for s in (1, 2, 4, 8, 16):
                link(dve, v.tensor_copy(tmp[:], ovend[:]))
                link(dve, v.tensor_tensor(ovend[:, s:], tmp[:, s:], tmp[:, 0:EXPERTS - s], ALU.add))
            link(dve, v.tensor_tensor(ovoff[:], ovend[:], nov[:], ALU.subtract))
            link(dve, v.tensor_tensor(ovoff[:], ovoff[:], k.c("eid31"), ALU.add))
            link(dve, v.tensor_tensor(blk[:], quo[:], spread(ovoff[:], 1, nt), ALU.add))
            link(dve, v.tensor_scalar(eq[:], quo[:], 0.5, None, ALU.is_gt))
            link(dve, v.tensor_tensor(blk[:], blk[:], eq[:], ALU.mult))
            link(dve, v.tensor_tensor(blk[:], blk[:], spread(k.c("eid"), 1, nt), ALU.add))
            link(dve, v.tensor_tensor(blk[:], blk[:], quo[:], ALU.subtract))
            link(dve, v.tensor_scalar(slot_e[:], blk[:], float(CAP), None, ALU.mult))
            link(dve, v.tensor_tensor(slot_e[:], slot_e[:], rank[:], ALU.add))
            for c in range(2):
                link(dve, v.tensor_tensor(eq[:], oh[:, c], slot_e[:], ALU.mult))
                link(dve, v.tensor_reduce(slot[:, c * nt:(c + 1) * nt], eq[:], AX.X, ALU.add))
                link(dve, v.tensor_tensor(eq[:], oh[:, c], blk[:], ALU.mult))
                link(dve, v.tensor_reduce(block_of[:, c * nt:(c + 1) * nt], eq[:], AX.X, ALU.add))
            link(dve, v.tensor_copy(r["slot"][:], slot[:]))
            link(dve, v.tensor_scalar(place[:], block_of[:], -float(CAP), None, ALU.mult))
            link(dve, v.tensor_tensor(place[:], place[:], slot[:], ALU.add))
            link(dve, v.tensor_tensor(rsel[:], spread(place[:], 2, P), spread(k.c("iota"), 1, 2 * nt), ALU.is_equal),
                 wait=False)
            link(dve, v.tensor_tensor(psel[:], spread(block_of[:], 2, SLOT_COLS), spread(k.c("blockid"), 1, 2 * nt),
                                      ALU.is_equal))
            for c in range(2):
                for t in range(nt):
                    a = c * nt + t
                    link(dve, v.tensor_tensor(psel[:, a, :], psel[:, a, :],
                                              k.c("tok")[:, t:t + 1].broadcast_to([P, SLOT_COLS]), ALU.mult),
                         wait=(a == 2 * nt - 1))
            v.memset(tmp[:, 0:1], 0.0).then_inc(selects, 1)
            link(dve, v.tensor_copy(table[:, 0:EXPERTS], k.c("eid")))
            link(dve, v.tensor_tensor(cmp_over[:], spread(ovend[:], 1, n_over), spread(k.c("ovid"), 2, EXPERTS), ALU.is_le))
            link(dve, v.tensor_reduce(table[:, EXPERTS:MAX_BLOCKS], cmp_over[:], AX.X, ALU.add))
            link(dve, v.tensor_scalar(table[:], table[:], float(EXPERTS - 1), None, ALU.min))
            link(dve, v.tensor_copy(r["expert"][:], table[0:1, :]))
            link(dve, v.tensor_scalar(cmp_over[:, 0:n_over // 2, 0], k.c("ovid")[:, 0:n_over:2], ovend[:, EXPERTS - 1:EXPERTS], None,
                                      ALU.is_lt))
            link(dve, v.tensor_reduce(tmp[:, 0:1], cmp_over[:, 0:n_over // 2, 0], AX.X, ALU.add))
            link(dve, v.tensor_scalar(tmp[:, 0:1], tmp[:, 0:1], float(EXPERTS // 2), None, ALU.add))
            link(dve, v.tensor_copy(r["pairs"][:], tmp[0:1, 0:1]))
            dve.wait_ge(slots_done, 1)
            v.tensor_copy(r["token"][:], k.bank[3][:, 0:SLOT_COLS]).then_inc(finished, 1)
            dve.wait_ge(finished, 1)


def expert_buffers(k, ring_at):
    ar = k.arena(ring_at)
    b = {"w1": [ar(f"w1_{j}", [P, KC, FF]) for j in range(2)], "w3": [ar(f"w3_{j}", [P, KC, FF]) for j in range(2)],
         "w2": [ar(f"w2_{j}", [P, FC, D]) for j in range(2)]}
    for n in ("w1", "w3", "w2"):
        b["in_" + n] = [k.sem(f"in_{n}_{j}") for j in range(2)]
    return b


def load_expert(k, layer, b, which, expert, j):
    src = k.ins["moe_" + which][layer][bass.ds(expert, 1)].rearrange("o (k p) f -> p (o k) f", p=P)
    k.nc.sync.dma_start(b[which][j][:], src).then_inc(b["in_" + which][j], 16)


def load_first_pair(k, layer, b):
    for j in range(2):
        for which in ("w1", "w3", "w2"):
            load_expert(k, layer, b, which, j, j)


def stage_experts(k, layer, r, b):
    nc = k.nc
    ar = k.arena(r["tmp_at"])
    xg = [ar(f"xg{j}", [P, D]) for j in range(2)]
    xgT = [ar(f"xgT{j}", [P, KC, CAP]) for j in range(2)]
    y = [ar(f"y{j}", [P, D]) for j in range(2)]
    gate, hid = ar("gate", [P, 2, FC * CAP]), ar("hid", [P, 2, FC * CAP])
    gathered = [k.sem(f"gathered{j}") for j in range(2)]
    stored = [k.sem(f"stored{j}") for j in range(2)]
    closing, index_in = k.sem("closing"), k.sem("index")
    first_turned, first_moved = k.sem("first_turned"), k.sem("first_moved")
    PE = Steps(k.sem("moe_pe"), ["a0", "xt1", "b0", "a1", "b1", "c0", "xt0", "c1"])
    SC = Steps(k.sem("moe_act"), ["g0", "xt1", "g1", "y0", "xt0", "y1"])
    V = Steps(k.sem("moe_dve"), ["xt1", "h0", "h1", "y0", "xt0", "y1"])
    A_BANK, B_BANK, Y_BANK = (2, 3), (4, 5), (6, 7)

    def pairs_of(eng):
        return eng.value_load(r["pairs"][0:1, 0:1], min_val=EXPERTS // 2, max_val=MAX_PAIRS)

    def turn(j, half):
        for i in range(4):
            kc = half * 4 + i
            last = nc.tensor.transpose(k.bank[half][:, i * P:(i + 1) * P], xg[j][:, kc * P:(kc + 1) * P], k.c("ident"))
        return last

    def move_turned(copy, j, half):
        return copy(xgT[j][:, half * 4:half * 4 + 4, :].rearrange("p k s -> p (k s)"), k.bank[half][:])

    def act_copy(dst, src):
        return nc.scalar.activation(dst, src, ACT.Copy)

    with nc.Block() as block:
        @block.sync
        def _(sp):
            n = pairs_of(sp)
            with sp.Fori(1, n) as q:
                e = [sp.value_load(r["expert"][0:1, bass.ds(q * 2 + j, 1)], min_val=0, max_val=EXPERTS - 1) for j in range(2)]
                for j in range(2):
                    sp.wait_ge(PE.sem, PE.at(f"a{j}", q - 1))
                    load_expert(k, layer, b, "w1", e[j], j)
                    sp.wait_ge(PE.sem, PE.at(f"b{j}", q - 1))
                    load_expert(k, layer, b, "w3", e[j], j)
                for j in range(2):
                    sp.wait_ge(PE.sem, PE.at(f"c{j}", q - 1))
                    load_expert(k, layer, b, "w2", e[j], j)

        @block.gpsimd
        def _(pool):
            def gather(j, col, count):
                nc.gpsimd.tensor_copy(r["index"][:, j:j + 1], r["token"][:, bass.ds(col, 1)]).then_inc(index_in, 1)
                pool.wait_ge(index_in, count)
                nc.gpsimd.tensor_tensor(r["idle"][:], k.cst[:, 0:1], k.cst[:, 1:2], ALU.add)
                nc.gpsimd.indirect_dma_start(out=xg[j][:], out_offset=None, in_=k.h_dram[:, :],
                                             in_offset=bass.IndirectOffsetOnAxis(ap=r["index"][:, j:j + 1], axis=0))\
                    .then_inc(gathered[j], 16)

            n = pairs_of(pool)
            gather(0, 0, 1)
            with pool.Fori(0, n) as q:
                pool.wait_ge(PE.sem, PE.at("xt1", q - 1))
                gather(1, q * 2 + 1, q * 2 + 2)
                pool.wait_ge(first_turned, 2)
                pool.wait_ge(PE.sem, PE.at("xt0", q - 1))
                gather(0, q * 2 + 2, q * 2 + 3)

        @block.tensor
        def _(pe):
            n = pairs_of(pe)
            pe.sem_inc(PE.sem, PE.n)
            pe.wait_ge(gathered[0], 16)
            for half in range(2):
                turn(0, half).then_inc(first_turned, 1)
            pe.wait_ge(first_moved, 2)
            with pe.Fori(0, n) as q:
                def product(j, name, which, bank):
                    pe.wait_ge(b["in_" + which][j], (q + 1) * 16)
                    for f in range(FC):
                        for kc in range(KC):
                            last = nc.tensor.matmul(k.bank[bank][:, f * CAP:(f + 1) * CAP], b[which][j][:, kc, f * P:(f + 1) * P],
                                                    xgT[j][:, kc, :], start=(kc == 0), stop=(kc == KC - 1))
                    last.then_inc(PE.did(f"{name}{j}"), 1)

                def down(j):
                    pe.wait_ge(V.sem, V.at(f"h{j}", q))
                    pe.wait_ge(SC.sem, SC.at("y1", q - 1) if j == 0 else SC.at("y0", q))
                    pe.wait_ge(V.sem, V.at("y1", q - 1) if j == 0 else V.at("y0", q))
                    pe.wait_ge(b["in_w2"][j], (q + 1) * 16)
                    for half in range(2):
                        for f in range(FC):
                            last = nc.tensor.matmul(k.bank[Y_BANK[half]][:], hid[:, j, f * CAP:(f + 1) * CAP],
                                                    b["w2"][j][:, f, half * 512:(half + 1) * 512],
                                                    start=(f == 0), stop=(f == FC - 1))
                    last.then_inc(PE.did(f"c{j}"), 1)

                pe.wait_ge(SC.sem, SC.at("xt0", q - 1))
                pe.wait_ge(V.sem, V.at("xt0", q - 1))
                product(0, "a", "w1", A_BANK[0])
                pe.wait_ge(gathered[1], (q + 1) * 16)
                turn(1, 0)
                turn(1, 1).then_inc(PE.did("xt1"), 1)
                product(0, "b", "w3", B_BANK[0])
                pe.wait_ge(SC.sem, SC.at("xt1", q))
                pe.wait_ge(V.sem, V.at("xt1", q))
                product(1, "a", "w1", A_BANK[1])
                product(1, "b", "w3", B_BANK[1])
                down(0)
                pe.wait_ge(gathered[0], (q + 2) * 16)
                turn(0, 0)
                turn(0, 1).then_inc(PE.did("xt0"), 1)
                down(1)

        @block.scalar
        def _(act):
            load_tables(k, TABLE_SILU)
            n = pairs_of(act)
            act.sem_inc(SC.sem, SC.n)
            for j in range(2):
                act.sem_inc(stored[j], 16)
            act.wait_ge(first_turned, 1)
            move_turned(act_copy, 0, 0).then_inc(first_moved, 1)
            with act.Fori(0, n) as q:
                def silu(j):
                    act.wait_ge(PE.sem, PE.at(f"a{j}", q))
                    nc.scalar.activation(gate[:, j], k.bank[A_BANK[j]][:], ACT.Silu).then_inc(SC.did(f"g{j}"), 1)

                def store(j):
                    act.wait_ge(PE.sem, PE.at(f"c{j}", q))
                    act.wait_ge(stored[j], (q + 1) * 16)
                    act_copy(y[j][:, 0:512], k.bank[Y_BANK[0]][:]).then_inc(SC.did(f"y{j}"), 1)
                    act.wait_ge(SC.sem, SC.at(f"y{j}", q))
                    act.wait_ge(V.sem, V.at(f"y{j}", q))
                    nc.scalar.dma_start(k.y_dram[bass.ds(q * 2 * CAP + j * CAP, CAP), :], y[j][:]).then_inc(stored[j], 16)

                silu(0)
                act.wait_ge(PE.sem, PE.at("xt1", q))
                move_turned(act_copy, 1, 0).then_inc(SC.did("xt1"), 1)
                silu(1)
                store(0)
                act.wait_ge(PE.sem, PE.at("xt0", q))
                move_turned(act_copy, 0, 0).then_inc(SC.did("xt0"), 1)
                store(1)
            for j in range(2):
                act.wait_ge(stored[j], (n + 1) * 16)
                act_copy(r["done"][:, j:j + 1], k.cst[:, 0:1]).then_inc(closing, 1)

        @block.vector
        def _(dve):
            n = pairs_of(dve)
            dve.sem_inc(V.sem, V.n)
            dve.wait_ge(first_turned, 2)
            move_turned(nc.vector.tensor_copy, 0, 1).then_inc(first_moved, 1)
            with dve.Fori(0, n) as q:
                def hidden(j):
                    dve.wait_ge(SC.sem, SC.at(f"g{j}", q))
                    dve.wait_ge(PE.sem, PE.at(f"b{j}", q))
                    nc.vector.tensor_tensor(hid[:, j], gate[:, j], k.bank[B_BANK[j]][:], ALU.mult).then_inc(V.did(f"h{j}"), 1)

                def result(j):
                    dve.wait_ge(PE.sem, PE.at(f"c{j}", q))
                    dve.wait_ge(stored[j], (q + 1) * 16)
                    nc.vector.tensor_copy(y[j][:, 512:1024], k.bank[Y_BANK[1]][:]).then_inc(V.did(f"y{j}"), 1)

                dve.wait_ge(PE.sem, PE.at("xt1", q))
                move_turned(nc.vector.tensor_copy, 1, 1).then_inc(V.did("xt1"), 1)
                hidden(0)
                hidden(1)
                result(0)
                dve.wait_ge(PE.sem, PE.at("xt0", q))
                move_turned(nc.vector.tensor_copy, 0, 1).then_inc(V.did("xt0"), 1)
                result(1)


def stage_combine(k, layer, r, t0):
    nc, ar = k.nc, k.arena(r["ring_at"])
    nt = (T - t0) // P
    rows = ar("rows", [P, 2 * nt, D])
    mix = ar("mix", [P, nt, D])
    fetched = [k.sem(f"fetched{a}") for a in range(2 * nt)]
    mixed, turned, added = k.sem("mixed"), k.sem("y_turned"), k.sem("y_added")
    link = k.links("combine_link")
    with nc.Block() as block:
        @block.gpsimd
        def _(pool):
            for t in range(nt):
                for c in range(2):
                    a = c * nt + t
                    nc.gpsimd.indirect_dma_start(out=rows[:, a], out_offset=None, in_=k.y_dram[:, :],
                                                 in_offset=bass.IndirectOffsetOnAxis(ap=r["slot"][:, a:a + 1], axis=0))\
                        .then_inc(fetched[a], 16)

        @block.tensor
        def _(pe):
            for t in range(nt):
                pe.wait_ge(mixed, t + 1)
                for m in range(KC):
                    last = nc.tensor.transpose(k.bank[m][:, t * P:(t + 1) * P], mix[:, t, m * P:(m + 1) * P], k.c("ident"))
            last.then_inc(turned, 1)

        @block.vector
        def _(dve):
            for t in range(nt):
                dve.wait_ge(fetched[t], 16)
                link(dve, nc.vector.tensor_scalar(mix[:, t], rows[:, t], r["gate"][:, 0, t, :], None, ALU.mult))
                dve.wait_ge(fetched[nt + t], 16)
                nc.vector.scalar_tensor_tensor(out=mix[:, t], in0=rows[:, nt + t], scalar=r["gate"][:, 1, t, :],
                                               in1=mix[:, t], op0=ALU.mult, op1=ALU.add).then_inc(mixed, 1)
            dve.wait_ge(turned, 1)
            n = nt * P
            halves = [(0, 0, N_CTX), (1, N_CTX, T)] if t0 == 0 else [(1, 0, n)]
            for m in range(KC):
                for c, a, b in halves:
                    x = k.xT[:, m, t0 + a:t0 + b]
                    nc.vector.scalar_tensor_tensor(out=x, in0=k.bank[m][:, a:b], scalar=k.mod[:, layer, 5 * KC + m, c:c + 1],
                                                   in1=x, op0=ALU.mult, op1=ALU.add).then_inc(added, 1)
            dve.wait_ge(added, KC * len(halves))


def stage_diff(k, g):
    nc = k.nc
    NQ = N_LAT // P
    ar = g["ar"]
    w, w_in = g["w"], g["w_in"]
    q, qr, kk, t1 = ar("q", [P, N_LAT]), ar("qr", [P, N_LAT]), ar("k", [P, T]), ar("t1", [P, N_LAT])
    kraw, qraw = ar("kraw", [P, T]), ar("qraw", [P, N_LAT])
    v = ar("v", [P, NT, P])
    prob = ar("prob", [P, NQ, 2, T])
    aT = ar("aT", [P, NT, N_LAT])
    sq, rs = ar("sq", [P, N_LAT]), ar("rs", [P, N_LAT])
    mx, sm = ar("mx", [P, NQ, 2]), ar("sm", [P, NQ, 2])
    lam = ar("lam", [P, 4])
    lv = ar("lv", [P, 2, DH])
    eps = ar("eps", [P, 1])
    gain = ar("gain", [P, 1])
    t0 = N_CTX
    scale = DH ** -0.5
    W = k.ins["diff_w_qkv"][0].rearrange("(k p) n -> p k n", p=P)
    lam_exp = k.sem("lam_exp")
    lam_in = k.sem("lam_in")
    link = k.links("lam_link")

    PR, ROT = ["pr_q", "pr_k", "pr_v"], ["rot_q", "rot_k"]
    ROPE = ["qc", "kc", "kctx", "qs", "q", "ks", "k"]
    PE = Steps(k.sem("diff_pe"), [f"s{t}_{s}" for t in range(NQ) for s in range(2)] + PR[:2]
               + [f"tr{t}" for t in range(NQ)] + ROT + ["pv", "on", "pr_v"], HEADS - 1, PR + ROT)
    SC = Steps(k.sem("diff_act"), [f"e{t}_{s}" for t in range(NQ) for s in range(2)]
               + ["ev_q", "ev_k", "tr0", "osq", "ln_o", "rs_o", "ev_v"], HEADS - 1, ["ev_q", "ev_k", "ev_v"])
    V = Steps(k.sem("diff_dve"), [f"m{t}_{s}" for t in range(NQ) for s in range(2)]
              + [f"n{t}_{s}" for t in range(NQ) for s in range(2)]
              + [f"{n}{t}" for t in range(NQ) for n in ("r", "l", "p", "a")] + ["tr1"] + ROPE + ["on"], HEADS - 1, ROPE)
    PP = Steps(k.sem("first_pe"), PR[:2] + ROT + PR[2:])
    FA = Steps(k.sem("first_act"), ["ev_q", "ev_k", "ev_v"])
    FV = Steps(k.sem("first_rope"), ROPE)

    def project_qk(pe, steps, n):
        width, first = (N_LAT, t0) if n == 0 else (T, 0)
        for kc in range(KC):
            last = nc.tensor.matmul(k.bank[n][:, 0:width], w[n][:, kc, :], g["hT"][:, kc, first:T],
                                    start=(kc == 0), stop=(kc == KC - 1))
        last.then_inc(steps.did(PR[n]), 1)

    def project_v(t):
        for kc in range(KC):
            last = nc.tensor.matmul(k.bank[0][:, t * P:(t + 1) * P], g["hT"][:, kc, t * P:(t + 1) * P],
                                    w[2][:, kc, :], start=(kc == 0), stop=(kc == KC - 1))
        return last

    def rotate(steps):
        nc.tensor.matmul(k.bank[5][:, 0:N_LAT], k.c("rot"), qraw[:], start=True, stop=True).then_inc(steps.did("rot_q"), 1)
        nc.tensor.matmul(k.bank[6][:, 0:N_LAT], k.c("rot"), kraw[:, t0:T], start=True, stop=True)\
            .then_inc(steps.did("rot_k"), 1)

    def evacuate(n):
        if n == 0:
            return nc.scalar.activation(qraw[:], k.bank[0][:, 0:N_LAT], ACT.Copy)
        if n == 1:
            return nc.scalar.activation(kraw[:], k.bank[1][:], ACT.Copy)
        return nc.scalar.activation(v[:].rearrange("p t d -> p (t d)"), k.bank[0][:], ACT.Copy)

    def rope(dve, S, rnd):
        vec = nc.vector
        vec.tensor_tensor(q[:], qraw[:], k.c("cos"), ALU.mult).then_inc(S.did("qc"), 1)
        vec.tensor_tensor(kk[:, t0:T], kraw[:, t0:T], k.c("cos"), ALU.mult).then_inc(S.did("kc"), 1)
        vec.tensor_copy(kk[:, 0:t0], kraw[:, 0:t0]).then_inc(S.did("kctx"), 1)
        vec.tensor_tensor(qr[:], k.bank[5][:, 0:N_LAT], k.c("sin"), ALU.mult).then_inc(S.did("qs"), 1)
        dve.wait_ge(S.sem, S.at("qs", rnd))
        vec.tensor_tensor(qr[:], qr[:], q[:], ALU.add).then_inc(S.did("q"), 1)
        vec.tensor_tensor(t1[:], k.bank[6][:, 0:N_LAT], k.c("sin"), ALU.mult).then_inc(S.did("ks"), 1)
        dve.wait_ge(S.sem, S.at("ks", rnd))
        vec.tensor_tensor(kk[:, t0:T], kk[:, t0:T], t1[:], ALU.add).then_inc(S.did("k"), 1)

    with nc.Block() as block:
        @block.sync
        def _(sp):
            for n in range(3):
                sp.wait_ge(PP.sem, PP.at(PR[n]))
                nc.sync.dma_start(w[n][:], W[:, :, n * D + P:n * D + 2 * P]).then_inc(w_in[n], 16)

            def fetch_next(h, head):
                for n in range(3):
                    sp.wait_ge(PE.sem, PE.at(PR[n], h))
                    nc.sync.dma_start(w[n][:], W[:, :, bass.ds(head * P + n * D, P)]).then_inc(w_in[n], 16)

            with sp.Fori(0, HEADS - 2) as h:
                fetch_next(h, h + 2)

        @block.tensor
        def _(pe):
            pe.sem_inc(PE.sem, PE.n)
            for n in range(2):
                pe.wait_ge(w_in[n], 16)
                project_qk(pe, PP, n)
            pe.wait_ge(FA.sem, FA.at("ev_k"))
            rotate(PP)
            pe.wait_ge(w_in[2], 16)
            for t in range(NT):
                last = project_v(t)
            last.then_inc(PP.did("pr_v"), 1)
            pe.wait_ge(FV.sem, FV.at("k"))
            pe.wait_ge(FA.sem, FA.at("ev_v"))
            def head(h, last_head):
                pe.wait_ge(V.sem, V.at("k", h - 1))
                for t in range(NQ):
                    for s in range(2):
                        rows = slice(s * DH, (s + 1) * DH)
                        nc.tensor.matmul(k.bank[3 + 2 * t + s][:], qr[rows, t * P:(t + 1) * P], kk[rows, :], start=True, stop=True)\
                            .then_inc(PE.did(f"s{t}_{s}"), 1)
                pe.wait_ge(SC.sem, SC.at("ev_v", h - 1))
                if not last_head:
                    for n in range(2):
                        pe.wait_ge(w_in[n], (h + 2) * 16)
                        project_qk(pe, PE, n)
                for t in range(NQ):
                    pe.wait_ge(V.sem, V.at(f"a{t}", h))
                    for c in range(NT):
                        last = nc.tensor.transpose(k.bank[3 + t][:, c * P:(c + 1) * P], prob[:, t, 0, c * P:(c + 1) * P], k.c("ident"))
                    last.then_inc(PE.did(f"tr{t}"), 1)
                if not last_head:
                    pe.wait_ge(SC.sem, SC.at("ev_k", h))
                    rotate(PE)
                    pe.wait_ge(w_in[2], (h + 2) * 16)
                    project_v(0)
                pe.wait_ge(V.sem, V.at("on", h - 1))
                pe.wait_ge(SC.sem, SC.at("tr0", h))
                pe.wait_ge(V.sem, V.at("tr1", h))
                for c in range(NT):
                    last = nc.tensor.matmul(k.bank[7][:, 0:N_LAT], v[:, c, :], aT[:, c, :], start=(c == 0), stop=(c == NT - 1))
                last.then_inc(PE.did("pv"), 1)
                if not last_head:
                    project_v(1)
                pe.wait_ge(SC.sem, SC.at("osq", h))
                nc.tensor.matmul(k.bank[2][:, 0:N_LAT], k.c("ones"), sq[:], start=True, stop=True).then_inc(PE.did("on"), 1)
                if not last_head:
                    project_v(2)
                    project_v(3).then_inc(PE.did("pr_v"), 1)

            with pe.Fori(0, HEADS - 1) as h:
                head(h, False)
            head(HEADS - 1, True)

        @block.scalar
        def _(act):
            act.sem_inc(SC.sem, SC.n)
            load_tables(k, TABLE_LN_EXP)
            act.wait_ge(lam_in, 1)
            nc.scalar.activation(lam[:, 0:2], lam[:, 2:4], ACT.Exp).then_inc(lam_exp, 1)
            for n in range(3):
                act.wait_ge(PP.sem, PP.at(PR[n]))
                evacuate(n).then_inc(FA.did(f"ev_{'qkv'[n]}"), 1)
            def head(h, last_head):
                for t in range(NQ):
                    for s in range(2):
                        act.wait_ge(V.sem, V.at(f"n{t}_{s}", h))
                        nc.scalar.activation(prob[:, t, s], k.bank[3 + 2 * t + s][:], ACT.Exp, bias=mx[:, t, s:s + 1], scale=scale,
                                             accum_out=sm[:, t, s:s + 1]).then_inc(SC.did(f"e{t}_{s}"), 1)
                if not last_head:
                    for n in range(2):
                        act.wait_ge(PE.sem, PE.at(PR[n], h))
                        evacuate(n).then_inc(SC.did(f"ev_{'qkv'[n]}"), 1)
                act.wait_ge(PE.sem, PE.at("tr0", h))
                nc.scalar.activation(aT[:, :, 0:P], k.bank[3][:].rearrange("p (c q) -> p c q", c=NT), ACT.Copy).then_inc(SC.did("tr0"), 1)
                act.wait_ge(PE.sem, PE.at("pv", h))
                nc.scalar.activation(sq[:], k.bank[7][:, 0:N_LAT], ACT.Square).then_inc(SC.did("osq"), 1)
                act.wait_ge(PE.sem, PE.at("on", h))
                nc.scalar.activation(rs[:], k.bank[2][:, 0:N_LAT], ACT.Ln, bias=eps[:], scale=1.0 / P).then_inc(SC.did("ln_o"), 1)
                act.wait_ge(SC.sem, SC.at("ln_o", h))
                nc.scalar.activation(rs[:], rs[:], ACT.Exp, scale=-0.5).then_inc(SC.did("rs_o"), 1)
                if not last_head:
                    act.wait_ge(PE.sem, PE.at("pr_v", h))
                    evacuate(2).then_inc(SC.did("ev_v"), 1)

            with act.Fori(0, HEADS - 1) as h:
                head(h, False)
            head(HEADS - 1, True)

        @block.vector
        def _(dve):
            vec = nc.vector
            dve.sem_inc(V.sem, V.n)
            link(dve, vec.memset(eps[:], SUBLN_EPS))
            link(dve, vec.tensor_scalar(gain[:], k.p("diff_gain"), 1.0 - LAM_INIT, None, ALU.mult))
            l4 = k.p("lam").rearrange("p (a b d) -> p a b d", a=2, b=2)
            link(dve, vec.tensor_tensor(lv[:], l4[:, :, 0], l4[:, :, 1], ALU.mult))
            vec.tensor_reduce(lam[:, 2:4], lv[:], AX.X, ALU.add).then_inc(lam_in, 1)
            dve.wait_ge(lam_exp, 1)
            link(dve, vec.tensor_tensor(lam[:, 2:3], lam[:, 0:1], lam[:, 1:2], ALU.subtract))
            link(dve, vec.tensor_scalar(lam[:, 3:4], lam[:, 2:3], LAM_INIT, None, ALU.add))
            dve.wait_ge(PP.sem, PP.at("rot_k"))
            rope(dve, FV, None)
            def head(h, last_head):
                for t in range(NQ):
                    for s in range(2):
                        dve.wait_ge(PE.sem, PE.at(f"s{t}_{s}", h))
                        vec.tensor_reduce(mx[:, t, s:s + 1], k.bank[3 + 2 * t + s][:], AX.X, ALU.max).then_inc(V.did(f"m{t}_{s}"), 1)
                for t in range(NQ):
                    for s in range(2):
                        dve.wait_ge(V.sem, V.at(f"m{t}_{s}", h))
                        vec.tensor_scalar(mx[:, t, s:s + 1], mx[:, t, s:s + 1], -scale, None, ALU.mult).then_inc(V.did(f"n{t}_{s}"), 1)
                for t in range(NQ):
                    dve.wait_ge(SC.sem, SC.at(f"e{t}_1", h))
                    vec.reciprocal(sm[:, t, :], sm[:, t, :]).then_inc(V.did(f"r{t}"), 1)
                    dve.wait_ge(V.sem, V.at(f"r{t}", h))
                    vec.tensor_scalar(sm[:, t, 1:2], sm[:, t, 1:2], lam[:, 3:4], None, ALU.mult).then_inc(V.did(f"l{t}"), 1)
                    dve.wait_ge(V.sem, V.at(f"l{t}", h))
                    vec.tensor_scalar(prob[:, t, 1], prob[:, t, 1], sm[:, t, 1:2], None, ALU.mult).then_inc(V.did(f"p{t}"), 1)
                    dve.wait_ge(V.sem, V.at(f"p{t}", h))
                    vec.scalar_tensor_tensor(out=prob[:, t, 0], in0=prob[:, t, 0], scalar=sm[:, t, 0:1], in1=prob[:, t, 1],
                                             op0=ALU.mult, op1=ALU.subtract).then_inc(V.did(f"a{t}"), 1)
                dve.wait_ge(PE.sem, PE.at("tr1", h))
                vec.tensor_copy(aT[:, :, P:2 * P], k.bank[4][:].rearrange("p (c q) -> p c q", c=NT)).then_inc(V.did("tr1"), 1)
                if not last_head:
                    dve.wait_ge(PE.sem, PE.at("rot_k", h))
                    rope(dve, V, h)
                dve.wait_ge(SC.sem, SC.at("rs_o", h))
                vec.scalar_tensor_tensor(out=g["oz"][:].rearrange("p h t -> p (h t)")[:, bass.ds(h * T, N_LAT)],
                                         in0=k.bank[7][:, 0:N_LAT], scalar=gain[:], in1=rs[:], op0=ALU.mult, op1=ALU.mult)\
                    .then_inc(V.did("on"), 1)

            with dve.Fori(0, HEADS - 1) as h:
                head(h, False)
            head(HEADS - 1, True)


def stage_store(k, hT):
    nc, ar = k.nc, k.arena(k.norm_at)
    rows = ar("rows", [P, 2, D])
    turned, moved, stored = k.sem("out_turned"), k.sem("out_moved"), k.sem("out_stored")
    with nc.Block() as block:
        @block.tensor
        def _(pe):
            for t in range(2):
                for half in range(2):
                    for j in range(4):
                        kc = half * 4 + j
                        last = nc.tensor.transpose(k.bank[2 * t + half][:, j * P:(j + 1) * P], hT[:, kc, t * P:(t + 1) * P],
                                                   k.c("ident"))
                    last.then_inc(turned, 1)

        @block.vector
        def _(dve):
            for n in range(4):
                dve.wait_ge(turned, n + 1)
                nc.vector.tensor_copy(rows[:, n // 2, (n % 2) * 512:(n % 2 + 1) * 512], k.bank[n][:]).then_inc(moved, 1)

        @block.sync
        def _(sp):
            for t in range(2):
                sp.wait_ge(moved, 2 * (t + 1))
                nc.sync.dma_start(k.out[0, t * P:(t + 1) * P, :], rows[:, t, :]).then_inc(stored, 16)
            sp.wait_ge(stored, 32)


def moe(k, layer, hT, t0, at):
    keep = k.arena(at)
    nt = (T - t0) // P
    ring_at = (k.nc.sbuf_usable_end - 2 * 3 * 4 * D * FF // P) // 32 * 32
    b = expert_buffers(k, ring_at)
    r = {"gate": keep("gate", [P, 2, nt, 1]), "slot": keep("slot", [P, 2 * nt], U32), "token": keep("token", [P, SLOT_COLS], U32),
         "expert": keep("expert", [1, MAX_BLOCKS], U32), "pairs": keep("pairs", [1, 1], U32), "index": keep("index", [P, 2], U32),
         "w_r": keep("w_r", [P, KC, GROUPS + EXPERTS]), "w_r_in": k.sem("w_router"), "idle": keep("idle", [P, 1]), "done": keep("done", [P, 2]), "tmp_at": keep.at, "ring_at": ring_at}
    k.norm_at = keep.at

    def prefetch():
        for name, cols in (("moe_w_group", slice(0, GROUPS)), ("moe_w_expert", slice(GROUPS, GROUPS + EXPERTS))):
            k.nc.sync.dma_start(r["w_r"][:, :, cols], k.ins[name][layer].rearrange("(k p) n -> p k n", p=P))\
                .then_inc(r["w_r_in"], 16)
        load_first_pair(k, layer, b)

    stage_norm(k, hT, k.p("ffn")[:, layer * KC:(layer + 1) * KC], layer, 3, t0=t0, prefetch=prefetch)
    stage_route(k, layer, hT, t0, r)
    stage_experts(k, layer, r, b)
    stage_combine(k, layer, r, t0)


def hybrid_kernel(nc, ins, out):
    ctx = ExitStack()
    with ctx:
        k = Core(nc, ctx, ins, out)
        k.rows_dram = nc.dram_tensor("gate_rows", [HEADS, 2, 3, T], F32)
        k.h_dram = nc.dram_tensor("h_rows", [T, D], F32)
        k.y_dram = nc.dram_tensor("y_rows", [MAX_BLOCKS * CAP, D], F32)
        k.norm_at = k.free
        stage_load(k)
        stage_mod(k)

        ar = k.arena()
        g = {"hT": ar("hT", [P, KC, T]), "oz": ar("oz", [P, HEADS, T]), "cols": ar("cols", [P, HEADS, 4, 2, NT])}
        g["w_at"] = ar.at
        g["w"] = [ar(f"w{p}", [P, KC, P]) for p in PIECES]
        g["w_ab"], g["w_ab_in"] = ar("w_ab", [P, KC, 4 * HEADS]), k.sem("w_ab")
        g["w0_in"], g["first_qk"] = [k.sem(f"w0_{p}") for p in PIECES], k.sem("first_qk")
        k.norm_at = ar.at
        stage_norm(k, g["hT"], k.p("mix")[:, 0:KC], 0, 0, prefetch=lambda: load_first_head(k, g))
        stage_gdn_gates(k, g)
        g["pad"] = [ar(f"pad{p}", [P, 2, SEGW]) for p in PIECES[:3]]
        g["conv"] = [ar(f"conv{p}", [P, T]) for p in PIECES[:3]]
        g["zraw"], g["q"], g["k"], g["v"], g["z"] = (ar(n, [P, T]) for n in ("zraw", "q", "k", "v", "z"))
        g["taps"], g["eps"] = ar("taps", [P, 3 * TAPS]), ar("eps", [P, 4])
        g["hcols"] = ar("hcols", [P, 4, 2, NT])
        g["elast"] = ar("elast", [P, 2, NCH])
        g["rows"] = ar("rows", [P, 2, 3, T])
        g["sq"] = ar("sq", [P, 2, T])
        g["qe"], g["W"] = ar("qe", [P, 2, T]), ar("W", [P, 2, T])
        for n in ("E", "B", "KQ", "A", "XT", "vb", "kbe", "kd"):
            g[n] = ar(n, [P, 2, NT, P])
        g["As"] = ar("As", [P, len(LEVELS) - 1, 2, NT, P])
        g["ktok"], g["vtok"] = ar("ktok", [P, NT, P]), ar("vtok", [P, NT, P])
        g["S"], g["vn"] = ar("S", [P, 2, P]), ar("vn", [P, 2, P])
        eps_set = k.sem("eps_set")
        with nc.Block() as block:
            @block.vector
            def _(dve):
                for n, val in enumerate((EPS, math.log(P ** -0.5), 0.0)):
                    nc.vector.memset(g["eps"][:, n:n + 1], val).then_inc(eps_set, 1)
                dve.wait_ge(eps_set, 3)
        stage_gdn_first(k, g)
        stage_gdn_heads(k, g)
        stage_mix_out(k, g, ins["gdn_w_out"][0], 0, 2, 0)

        ar = k.arena()
        hT = ar("hT", [P, KC, T])
        moe(k, 0, hT, 0, ar.at)

        k.recycle()
        ar = k.arena()
        g = {"hT": ar("hT", [P, KC, T]), "oz": ar("oz", [P, HEADS, T])}
        g["w_at"] = ar.at
        g["w"], g["w_in"] = [ar(f"w{n}", [P, KC, P]) for n in "qkv"], [k.sem(f"dw_{n}") for n in "qkv"]
        k.norm_at = ar.at

        def first_weights():
            src = ins["diff_w_qkv"][0].rearrange("(k p) n -> p k n", p=P)
            for n in range(3):
                nc.sync.dma_start(g["w"][n][:], src[:, :, n * D:n * D + P]).then_inc(g["w_in"][n], 16)

        stage_norm(k, g["hT"], k.p("mix")[:, KC:2 * KC], 1, 0, prefetch=first_weights)
        g["ar"] = ar
        stage_diff(k, g)
        stage_mix_out(k, g, ins["diff_w_out"][0], 1, 2, N_CTX)

        ar = k.arena()
        hT = ar("hT", [P, KC, N_LAT])
        moe(k, 1, hT, N_CTX, ar.at)
        stage_norm(k, hT, k.p("final"), t0=N_CTX)
        stage_store(k, hT)
        k.recycle()


_BIG = ['x', 'ctx', 'w_mod', 'gdn_w_in', 'gdn_w_out', 'diff_w_qkv', 'diff_w_out', 'moe_w_group', 'moe_w_expert',
        'moe_w1', 'moe_w3', 'moe_w2']


def kernel(**inputs):
    import concourse.bacc as bacc
    from concourse.bass_utils import run_bass_kernel_spmd

    arrays = {n: np.ascontiguousarray(inputs[n]) for n in _BIG}
    arrays["constants"] = shape_constants()
    arrays["params"] = packed_params(inputs)
    nc = bacc.Bacc("TRN2", target_bir_lowering=False, num_devices=1)
    feeds, ins = {}, {}
    for name, a in arrays.items():
        feeds[f"in_{name}"] = a
        ins[name] = nc.dram_tensor(f"in_{name}", a.shape, mybir.dt.from_np(a.dtype), kind="ExternalInput").ap()
    out = nc.dram_tensor("out_0", (1, N_LAT, D), F32, kind="ExternalOutput").ap()
    hybrid_kernel(nc, ins, out)
    r = run_bass_kernel_spmd(nc, [feeds], core_ids=[0])
    return r.results[0]["out_0"]
```
